# Optimizing a Trainium2 kernel written in Bass

```python
import math
import jax, jax.numpy as jnp
from jax import lax
import numpy as np

D_MODEL = 1024
BATCH = 1
SEQ = 512
DEPTH = 1

HEAD_DIM = 128
MIX_WIDTH = D_MODEL
GDN_WIDTH = MIX_WIDTH // 2
RET_WIDTH = MIX_WIDTH - GDN_WIDTH
GDN_HEADS = GDN_WIDTH // HEAD_DIM
RET_HEADS = RET_WIDTH // HEAD_DIM
SHORT_CONV = 4
FFN_CONV = 3
D_FF = ((8 * D_MODEL // 3 + 255) // 256) * 256
CHUNK = 64
RET_ROPE_BASE = 10000.0
EPS = 1e-6
IN_SPLITS = (GDN_WIDTH, GDN_WIDTH, GDN_WIDTH, GDN_WIDTH, GDN_HEADS, GDN_HEADS,
             RET_WIDTH, RET_WIDTH, RET_WIDTH, RET_WIDTH)
IN_COLS = 4 * GDN_WIDTH + 2 * GDN_HEADS + 4 * RET_WIDTH


def _rms_norm(x, w):
    xf = x.astype(jnp.float32)
    y = xf * lax.rsqrt(jnp.mean(xf * xf, axis=-1, keepdims=True) + EPS)
    return (y * w.astype(jnp.float32)).astype(x.dtype)

def _rms_f32(xf):
    return xf * lax.rsqrt(jnp.mean(xf * xf, axis=-1, keepdims=True) + EPS)

def _l2norm(xf):
    return xf * lax.rsqrt(jnp.sum(xf * xf, axis=-1, keepdims=True) + EPS)

def _causal_dwconv(x, w):
    k, c = w.shape
    return lax.conv_general_dilated(
        x, w[:, None, :].astype(x.dtype), window_strides=(1,), padding=[(k - 1, 0)],
        dimension_numbers=("NWC", "WIO", "NWC"), feature_group_count=c)

def _to_chunks(t):
    b, s, h, d = t.shape
    return t.reshape(b, s // CHUNK, CHUNK, h, d).transpose(1, 0, 3, 2, 4)

def _from_chunks(t):
    nc, b, h, c, d = t.shape
    return t.transpose(1, 0, 3, 2, 4).reshape(b, nc * c, h, d)

def _scalar_chunks(t):
    b, s, h = t.shape
    return t.reshape(b, s // CHUNK, CHUNK, h).transpose(1, 0, 3, 2)

def _gated_deltanet(q, k, v, gate, a, b, conv_w, a_log, dt_bias, norm_w):
    bsz, s, _ = q.shape
    h, d = GDN_HEADS, HEAD_DIM
    qkv = jax.nn.silu(_causal_dwconv(jnp.concatenate([q, k, v], axis=-1), conv_w))
    qkv = qkv.astype(jnp.float32)
    q, k, v = jnp.split(qkv, 3, axis=-1)
    q = _l2norm(q.reshape(bsz, s, h, d)) * (d ** -0.5)
    k = _l2norm(k.reshape(bsz, s, h, d))
    v = v.reshape(bsz, s, h, d)
    beta = jax.nn.sigmoid(b.astype(jnp.float32))
    g = -jnp.exp(a_log.astype(jnp.float32)) * jax.nn.softplus(
        a.astype(jnp.float32) + dt_bias.astype(jnp.float32))

    qc, kc, vc = _to_chunks(q), _to_chunks(k), _to_chunks(v)
    gcum = jnp.cumsum(_scalar_chunks(g), axis=-1)
    betac = _scalar_chunks(beta)
    causal = jnp.tril(jnp.ones((CHUNK, CHUNK), dtype=bool))
    strict = jnp.tril(jnp.ones((CHUNK, CHUNK), dtype=bool), -1)
    diff = gcum[..., :, None] - gcum[..., None, :]
    decay = jnp.exp(jnp.where(causal, diff, -jnp.inf))
    kb = kc * betac[..., None]
    vb = vc * betac[..., None]
    m = jnp.where(strict, jnp.einsum('nbhik,nbhjk->nbhij', kb, kc) * decay, 0.0)
    eye = jnp.eye(CHUNK, dtype=jnp.float32)
    t_mat = lax.linalg.triangular_solve(eye + m, jnp.broadcast_to(eye, m.shape),
                                        left_side=True, lower=True, unit_diagonal=True)
    u_base = jnp.einsum('nbhij,nbhjv->nbhiv', t_mat, vb)
    w_mat = jnp.einsum('nbhij,nbhjk->nbhik', t_mat, kb * jnp.exp(gcum)[..., None])
    qk = jnp.einsum('nbhik,nbhjk->nbhij', qc, kc) * decay
    q_dec = qc * jnp.exp(gcum)[..., None]
    k_dec = kc * jnp.exp(gcum[..., -1:] - gcum)[..., None]
    chunk_decay = jnp.exp(gcum[..., -1])

    def step(state, inp):
        u_b, w_c, qk_c, qd_c, kd_c, cd_c = inp
        u = u_b - jnp.einsum('bhck,bhkv->bhcv', w_c, state)
        o = jnp.einsum('bhck,bhkv->bhcv', qd_c, state) + jnp.einsum('bhij,bhjv->bhiv', qk_c, u)
        state = state * cd_c[..., None, None] + jnp.einsum('bhck,bhcv->bhkv', kd_c, u)
        return state, o

    s0 = jnp.zeros((bsz, h, d, d), dtype=jnp.float32)
    _, o = lax.scan(step, s0, (u_base, w_mat, qk, q_dec, k_dec, chunk_decay))
    o = _from_chunks(o)
    gt = gate.astype(jnp.float32).reshape(bsz, s, h, d)
    o = _rms_f32(o) * norm_w.astype(jnp.float32) * jax.nn.silu(gt)
    return o.reshape(bsz, s, h * d).astype(gate.dtype)

def _rotate_every_two(x):
    x1 = x[..., ::2]
    x2 = x[..., 1::2]
    return jnp.stack((-x2, x1), axis=-1).reshape(x.shape)

def _xpos_rotary(x, pos):
    d = x.shape[-1]
    angle = 1.0 / (RET_ROPE_BASE ** jnp.linspace(0.0, 1.0, d // 2, dtype=jnp.float32))
    angle = jnp.repeat(angle, 2)
    phase = pos[:, None] * angle[None, :]
    return x * jnp.cos(phase)[:, None, :] + _rotate_every_two(x) * jnp.sin(phase)[:, None, :]

def _retention(q, k, v, gate):
    bsz, s, _ = q.shape
    h, d = RET_HEADS, HEAD_DIM
    pos = jnp.arange(s, dtype=jnp.float32)
    q = _xpos_rotary(q.astype(jnp.float32).reshape(bsz, s, h, d), pos)
    k = _xpos_rotary(k.astype(jnp.float32).reshape(bsz, s, h, d), pos) * (d ** -0.5)
    v = v.astype(jnp.float32).reshape(bsz, s, h, d)
    log_gamma = jnp.log(1.0 - jnp.exp2(-5.0 - jnp.arange(h, dtype=jnp.float32)))
    idx = jnp.arange(CHUNK, dtype=jnp.float32)
    causal = jnp.tril(jnp.ones((CHUNK, CHUNK), dtype=bool))
    rel = idx[:, None] - idx[None, :]
    d_mat = jnp.exp(jnp.where(causal[None], rel[None] * log_gamma[:, None, None], -jnp.inf))
    xi = jnp.exp((idx[None, :] + 1.0) * log_gamma[:, None])[..., None]
    zeta = jnp.exp((CHUNK - 1.0 - idx[None, :]) * log_gamma[:, None])[..., None]
    chunk_gamma = jnp.exp(CHUNK * log_gamma)

    qc, kc, vc = _to_chunks(q), _to_chunks(k), _to_chunks(v)
    inner = jnp.einsum('nbhij,nbhjv->nbhiv',
                       jnp.einsum('nbhik,nbhjk->nbhij', qc, kc) * d_mat, vc)
    q_xi = qc * xi
    kv = jnp.einsum('nbhck,nbhcv->nbhkv', kc * zeta, vc)

    def step(r, inp):
        inner_c, qx_c, kv_c = inp
        o = inner_c + jnp.einsum('bhck,bhkv->bhcv', qx_c, r)
        r = r * chunk_gamma[:, None, None] + kv_c
        return r, o

    r0 = jnp.zeros((bsz, h, d, d), dtype=jnp.float32)
    _, o = lax.scan(step, r0, (inner, q_xi, kv))
    o = _rms_f32(_from_chunks(o))
    o = jax.nn.silu(gate.astype(jnp.float32).reshape(bsz, s, h, d)) * o
    return o.reshape(bsz, s, h * d).astype(gate.dtype)

def _conv_glu_mlp(x, w_up, conv_w, w_down):
    hdn = jnp.einsum('bsd,df->bsf', x, w_up)
    hdn = _causal_dwconv(hdn, conv_w)
    g, u = jnp.split(hdn, 2, axis=-1)
    return jnp.einsum('bsf,fd->bsd', jax.nn.silu(g) * u, w_down)

def first_inputs(seed: int = 0) -> dict:
    key = jax.random.key(seed)
    ks = jax.random.split(key, 14)
    f32 = jnp.float32
    x = jax.random.normal(ks[0], (BATCH, SEQ, D_MODEL), f32)
    attn_norm_w = 1.0 + 0.02 * jax.random.normal(ks[1], (DEPTH, D_MODEL), f32)
    w_in = jax.random.normal(ks[2], (DEPTH, D_MODEL, IN_COLS), f32) * D_MODEL ** -0.5
    gdn_conv_w = jax.random.normal(ks[3], (DEPTH, SHORT_CONV, 3 * GDN_WIDTH), f32) * SHORT_CONV ** -0.5
    gdn_a_log = jnp.log(jax.random.uniform(ks[4], (DEPTH, GDN_HEADS), f32, minval=1.0, maxval=16.0))
    dt = jnp.exp(jax.random.uniform(ks[5], (DEPTH, GDN_HEADS), f32,
                                    minval=math.log(1e-3), maxval=math.log(1e-1)))
    gdn_dt_bias = dt + jnp.log(-jnp.expm1(-dt))
    gdn_norm_w = 1.0 + 0.02 * jax.random.normal(ks[6], (DEPTH, HEAD_DIM), f32)
    w_out = jax.random.normal(ks[7], (DEPTH, MIX_WIDTH, D_MODEL), f32) * MIX_WIDTH ** -0.5
    mlp_norm_w = 1.0 + 0.02 * jax.random.normal(ks[8], (DEPTH, D_MODEL), f32)
    w_up = jax.random.normal(ks[9], (DEPTH, D_MODEL, 2 * D_FF), f32) * D_MODEL ** -0.5
    mlp_conv_w = jax.random.normal(ks[10], (DEPTH, FFN_CONV, 2 * D_FF), f32) * FFN_CONV ** -0.5
    w_down = jax.random.normal(ks[11], (DEPTH, D_FF, D_MODEL), f32) * D_FF ** -0.5
    final_norm_w = 1.0 + 0.02 * jax.random.normal(ks[12], (D_MODEL,), f32)
    return {"x": x, "attn_norm_w": attn_norm_w, "w_in": w_in, "gdn_conv_w": gdn_conv_w,
            "gdn_a_log": gdn_a_log, "gdn_dt_bias": gdn_dt_bias, "gdn_norm_w": gdn_norm_w,
            "w_out": w_out, "mlp_norm_w": mlp_norm_w, "w_up": w_up, "mlp_conv_w": mlp_conv_w,
            "w_down": w_down, "final_norm_w": final_norm_w}

def first_block(x, attn_norm_w, w_in, gdn_conv_w, gdn_a_log, gdn_dt_bias, gdn_norm_w,
              w_out, mlp_norm_w, w_up, mlp_conv_w, w_down, final_norm_w):
    split_idx = []
    acc = 0
    for sz in IN_SPLITS[:-1]:
        acc += sz
        split_idx.append(acc)
    h = x
    for l in range(DEPTH):
        n = _rms_norm(h, attn_norm_w[l])
        proj = jnp.einsum('bsd,dc->bsc', n, w_in[l])
        (gq, gk, gv, gg, ga, gb, rq, rk, rv, rg) = jnp.split(proj, split_idx, axis=-1)
        o_gdn = _gated_deltanet(gq, gk, gv, gg, ga, gb, gdn_conv_w[l], gdn_a_log[l],
                                gdn_dt_bias[l], gdn_norm_w[l])
        o_ret = _retention(rq, rk, rv, rg)
        mix = jnp.concatenate([o_gdn, o_ret], axis=-1)
        h = h + jnp.einsum('bsm,md->bsd', mix, w_out[l])
        n2 = _rms_norm(h, mlp_norm_w[l])
        h = h + _conv_glu_mlp(n2, w_up[l], mlp_conv_w[l], w_down[l])
    return _rms_norm(h, final_norm_w)


DEPTH_2 = 2

HEAD_DIM_2 = 64
Q_HEADS = 8
KV_HEADS = 2
GROUP = Q_HEADS // KV_HEADS
ATTN_WIDTH = Q_HEADS * HEAD_DIM_2
KV_WIDTH = KV_HEADS * HEAD_DIM_2
WINDOW = 128
BLOCK = 128
POOL_WIDTH = D_MODEL - ATTN_WIDTH
POOL_WINDOWS = (2, 4, 8, 16)
POOL_GROUPS = len(POOL_WINDOWS)
POOL_GC = POOL_WIDTH // POOL_GROUPS
EVEN_IN = ATTN_WIDTH + 2 * KV_WIDTH + ATTN_WIDTH + POOL_WIDTH + POOL_WIDTH
EVEN_MIX = ATTN_WIDTH + POOL_WIDTH
CONV_WIDTH = D_MODEL
CONV_K = 31
ODD_IN = 3 * CONV_WIDTH
NEG = -1e30
N_EVEN = (DEPTH_2 + 1) // 2
N_ODD = DEPTH_2 // 2


def rms_norm(x, g):
    xf = x.astype(jnp.float32)
    y = xf * lax.rsqrt(jnp.mean(xf * xf, axis=-1, keepdims=True) + EPS)
    return (y * g.astype(jnp.float32)).astype(x.dtype)

def alibi_slopes(n):
    return jnp.exp2(-8.0 * jnp.arange(1, n + 1, dtype=jnp.float32) / n)

def sliding_window_attention(q, k, v, sinks):
    B, S, _ = q.shape
    nb = S // BLOCK
    q = q.reshape(B, nb, BLOCK, KV_HEADS, GROUP, HEAD_DIM_2)
    k = k.reshape(B, nb, BLOCK, KV_HEADS, HEAD_DIM_2)
    v = v.reshape(B, nb, BLOCK, KV_HEADS, HEAD_DIM_2)
    kpad = jnp.zeros_like(k[:, :1])
    vpad = jnp.zeros_like(v[:, :1])
    kk = jnp.concatenate([jnp.concatenate([kpad, k[:, :-1]], axis=1), k], axis=2)
    vv = jnp.concatenate([jnp.concatenate([vpad, v[:, :-1]], axis=1), v], axis=2)
    scores = jnp.einsum('bnqkgd,bnskd->bnkgqs', q, kk).astype(jnp.float32) * (HEAD_DIM_2 ** -0.5)
    qi = jnp.arange(BLOCK)[:, None] + BLOCK
    sj = jnp.arange(2 * BLOCK)[None, :]
    dist = qi - sj
    key_pos = jnp.arange(nb)[:, None, None] * BLOCK + sj[None] - BLOCK
    valid = (dist >= 0)[None] & (dist < WINDOW)[None] & (key_pos >= 0)
    slopes = alibi_slopes(Q_HEADS).reshape(KV_HEADS, GROUP)
    bias = -slopes[:, :, None, None] * dist.astype(jnp.float32)
    scores = jnp.where(valid[None, :, None, None], scores + bias, NEG)
    sink = sinks.astype(jnp.float32).reshape(KV_HEADS, GROUP)[None, None, :, :, None, None]
    mx = jnp.maximum(jnp.max(scores, axis=-1, keepdims=True), sink)
    p = jnp.exp(scores - mx)
    p = p / (jnp.sum(p, axis=-1, keepdims=True) + jnp.exp(sink - mx))
    out = jnp.einsum('bnkgqs,bnskd->bnqkgd', p.astype(vv.dtype), vv)
    return out.reshape(B, S, ATTN_WIDTH)

def multiscale_pool(u, pool_w, pool_scale):
    B, S, _ = u.shape
    uf = u.astype(jnp.float32).reshape(B, S, POOL_GROUPS, POOL_GC)
    cs = jnp.concatenate([jnp.zeros_like(uf[:, :1]), jnp.cumsum(uf, axis=1)], axis=1)
    t = jnp.arange(S)[:, None]
    win = jnp.array(POOL_WINDOWS, dtype=jnp.int32)[None, :]
    lo = jnp.maximum(t + 1 - win, 0)
    cnt = (t + 1 - lo).astype(jnp.float32)
    lower = cs[:, lo, jnp.arange(POOL_GROUPS)[None, :]]
    pooled = (cs[:, 1:] - lower) / cnt[None, :, :, None] - uf
    y = jnp.einsum('bsgc,gcd->bsgd', pooled, pool_w.astype(jnp.float32))
    y = y * pool_scale.astype(jnp.float32).reshape(POOL_GROUPS, POOL_GC)
    return y.reshape(B, S, POOL_WIDTH).astype(u.dtype)

def even_mixer(h, w_in, sinks, pool_w, pool_scale, w_out):
    proj = h @ w_in
    splits = np.cumsum([ATTN_WIDTH, KV_WIDTH, KV_WIDTH, ATTN_WIDTH, POOL_WIDTH]).tolist()
    q, k, v, ga, u, gb = jnp.split(proj, splits, axis=-1)
    ya = sliding_window_attention(q, k, v, sinks).astype(h.dtype) * jax.nn.silu(ga)
    yb = multiscale_pool(u, pool_w, pool_scale) * jax.nn.silu(gb)
    return jnp.concatenate([ya, yb], axis=-1) @ w_out

def odd_mixer(h, w_in, dw_w, dw_b, ln_g, ln_b, w_out):
    proj = h @ w_in
    a, b, gate = jnp.split(proj, [CONV_WIDTH, 2 * CONV_WIDTH], axis=-1)
    glu = a * jax.nn.sigmoid(b)
    conv = lax.conv_general_dilated(
        glu, dw_w.astype(glu.dtype), window_strides=(1,), padding=[(CONV_K - 1, 0)],
        dimension_numbers=('NWC', 'WIO', 'NWC'), feature_group_count=CONV_WIDTH)
    cf = conv.astype(jnp.float32) + dw_b.astype(jnp.float32)
    mu = jnp.mean(cf, axis=-1, keepdims=True)
    var = jnp.mean(jnp.square(cf - mu), axis=-1, keepdims=True)
    cn = (cf - mu) * lax.rsqrt(var + EPS) * ln_g.astype(jnp.float32) + ln_b.astype(jnp.float32)
    y = jax.nn.silu(cn).astype(h.dtype) * jax.nn.silu(gate)
    return y @ w_out

def second_inputs(seed: int = 0) -> dict:
    key = jax.random.key(seed)
    ks = jax.random.split(key, 16)
    f32 = jnp.float32
    nrm = lambda k, shape, s: jax.random.normal(k, shape, f32) * s
    return {
        'x': nrm(ks[0], (BATCH, SEQ, D_MODEL), 1.0),
        'pre_norm': 1.0 + nrm(ks[1], (DEPTH_2, D_MODEL), 0.05),
        'post_norm': 1.0 + nrm(ks[2], (DEPTH_2, D_MODEL), 0.05),
        'a_w_in': nrm(ks[3], (N_EVEN, D_MODEL, EVEN_IN), D_MODEL ** -0.5),
        'a_sinks': nrm(ks[4], (N_EVEN, Q_HEADS), 0.5),
        'b_pool_w': nrm(ks[5], (N_EVEN, POOL_GROUPS, POOL_GC, POOL_GC), POOL_GC ** -0.5),
        'b_pool_scale': 1.0 + nrm(ks[6], (N_EVEN, POOL_WIDTH), 0.1),
        'ab_w_out': nrm(ks[7], (N_EVEN, EVEN_MIX, D_MODEL), EVEN_MIX ** -0.5),
        'c_w_in': nrm(ks[8], (N_ODD, D_MODEL, ODD_IN), D_MODEL ** -0.5),
        'c_dw_w': nrm(ks[9], (N_ODD, CONV_K, 1, CONV_WIDTH), CONV_K ** -0.5),
        'c_dw_b': nrm(ks[10], (N_ODD, CONV_WIDTH), 0.02),
        'c_ln_g': 1.0 + nrm(ks[11], (N_ODD, CONV_WIDTH), 0.05),
        'c_ln_b': nrm(ks[12], (N_ODD, CONV_WIDTH), 0.02),
        'c_w_out': nrm(ks[13], (N_ODD, CONV_WIDTH, D_MODEL), CONV_WIDTH ** -0.5),
    }

def second_block(x, pre_norm, post_norm, a_w_in, a_sinks, b_pool_w, b_pool_scale, ab_w_out,
              c_w_in, c_dw_w, c_dw_b, c_ln_g, c_ln_b, c_w_out):
    for layer in range(DEPTH_2):
        h = rms_norm(x, pre_norm[layer])
        if layer % 2 == 0:
            i = layer // 2
            y = even_mixer(h, a_w_in[i], a_sinks[i], b_pool_w[i], b_pool_scale[i], ab_w_out[i])
        else:
            i = layer // 2
            y = odd_mixer(h, c_w_in[i], c_dw_w[i], c_dw_b[i], c_ln_g[i], c_ln_b[i], c_w_out[i])
        x = x + rms_norm(y, post_norm[layer])
    return x


def setup_inputs(seed=0):
    out = dict(first_inputs(seed))
    for name, value in second_inputs(seed + 1).items():
        if name != "x":
            out[name + "_2"] = value
    return out


def reference(
    x, attn_norm_w, w_in, gdn_conv_w, gdn_a_log, gdn_dt_bias, gdn_norm_w, w_out, mlp_norm_w,
    w_up, mlp_conv_w, w_down, final_norm_w, pre_norm_2, post_norm_2, a_w_in_2, a_sinks_2,
    b_pool_w_2, b_pool_scale_2, ab_w_out_2, c_w_in_2, c_dw_w_2, c_dw_b_2, c_ln_g_2, c_ln_b_2,
    c_w_out_2,
):
    x = first_block(
        x, attn_norm_w, w_in, gdn_conv_w, gdn_a_log, gdn_dt_bias, gdn_norm_w, w_out, mlp_norm_w,
        w_up, mlp_conv_w, w_down, final_norm_w,
    )
    return second_block(
        x, pre_norm_2, post_norm_2, a_w_in_2, a_sinks_2, b_pool_w_2, b_pool_scale_2, ab_w_out_2,
        c_w_in_2, c_dw_w_2, c_dw_b_2, c_ln_g_2, c_ln_b_2, c_w_out_2,
    )


_drawn_inputs = setup_inputs


def setup_inputs(seed=0):
    import zlib

    import numpy as np

    out = dict(_drawn_inputs(seed))
    spreads = {}
    factors = {'gdn_norm_w': 4.504, 'mlp_norm_w': 2.939, 'a_sinks_2': 3.802, 'c_ln_b_2': 4.766}
    for name, (base, spread) in spreads.items():
        noise = np.random.default_rng([zlib.crc32(name.encode()), seed]).standard_normal(out[name].shape)
        drawn = base * np.exp(spread * noise) if base else spread * noise
        out[name] = __import__('jax').numpy.asarray(drawn.astype(out[name].dtype))
    for name, factor in factors.items():
        out[name] = (out[name] * factor).astype(out[name].dtype)
    return out
```

```python
import math
from contextlib import ExitStack

import numpy as np

import concourse.bass as bass
from concourse import mybir

P = 128
S = 512
D = 1024
KT = D // P
NB = S // P
H = 4
GW = H * P
IN_COLS = 8 * GW + 2 * H
DFF = 2816
FT = DFF // P
EPS = 1e-6
EVEN_IN = 2304
QH = 8
HD2 = 64
CK = 31
NEG = -1e30

F32 = mybir.dt.float32
F32R = mybir.dt.float32r
ACT = mybir.ActivationFunctionType
ALU = mybir.AluOpType
AX = mybir.AxisListType
MUL, ADD, SUB = ALU.mult, ALU.add, ALU.subtract

VECS = [("attn_norm_w", 8), ("mlp_norm_w", 8), ("final_norm_w", 8), ("pre0", 8), ("pre1", 8),
        ("post0", 8), ("post1", 8), ("pool_scale", 4), ("dw_b", 8), ("ln_g", 8), ("ln_b", 8),
        ("gdn_norm_w", 1)]
VEC_AT, _n = {}, 0
for _name, _rows in VECS:
    VEC_AT[_name] = _n
    _n += _rows
NVEC = _n

U1, U2, U3, U4, U5, U6, U7, U8 = 0, 32, 40, 84, 108, 126, 134, 158
UNITS = 166
M1, M2, M3, M4, M5, M6, M7, M8 = 0, 32, 40, 84, 92, 110, 118, 142
PAIRS = UNITS // 2
FILL = {1: 0, 2: 1, 3: 2, 5: 3, 6: 4, 7: 5, 8: 6}
RET_GAP = [19, 20, 23, 24]


def loads_before(p):
    n = 0
    for q in range(p % 2, p + 1, 2):
        n += 3 if U6 <= 2 * q < U7 else 2
    return n


def build(nc, a, const, out):
    ctx = ExitStack()
    with ctx:
        base = (nc.sbuf_base + 31) // 32 * 32

        def at(name, shape, dt, off):
            return nc.alloc_sbuf_tensor_at(name, shape, dt, offset=base + off)

        def sem(name):
            return ctx.enter_context(nc.semaphore(name))

        RAW = at("raw", [P, 2, KT, 256], F32, 0)
        WH = at("w_hi", [P, 4, 4, P], F32R, 16384)
        WL = at("w_lo", [P, 4, 4, P], F32R, 24576)
        XA = at("x_a", [P, KT, 2, S], F32R, 32768)
        AR = 65536
        G = 204800
        IDENT = at("ident", [P, P], F32, G)
        ONES = at("ones", [P, P], F32, G + 512)
        RSTD = at("rstd", [P, S], F32, G + 1024)
        ACC = at("acc", [P, S], F32, G + 3072)
        VEC = at("vec", [P, NVEC], F32, G + 5120)
        GCW = at("gdn_conv", [P, 4, 12], F32, G + 5120 + 352)
        MCW = at("mlp_conv", [P, 3, 44], F32, G + 5664)
        DCW = at("dw_conv", [P, CK, KT], F32, G + 6208)
        RCOL = at("rstd_col", [P, NB], F32, G + 7200)
        CB = at("const_bias", [P, 4], F32, G + 7232)

        KQ = at("kq", [P, H, 2, S], F32, AR)
        ROWS = at("rows", [P, 6, P], F32, AR)
        V = at("v", [P, H, S], F32, AR + 16384)
        RV = at("ret_v", [P, H, NB, P], F32, AR + 24576)
        XTOK = at("x_tok", [P, NB, D], F32, AR + 32768)
        GT = at("gates", [P, 8, S], F32, AR + 32768)
        M = at("m", [P, NB * H, P], F32, AR + 32768)
        T = at("t", [P, NB * H, P], F32, AR + 40960)
        TT = at("tt", [P, NB * H, P], F32, AR + 49152)
        QKT = at("qkt", [P, NB * H, P], F32, AR + 57344)
        R4 = at("r4", [P, H, S], F32, AR + 57344)
        EB = at("eb", [P, NB * H, P], F32, AR + 65536)
        SQ4 = at("sq4", [P, H, S], F32, AR + 65536)
        XZ = at("xz", [P, NB, H, P], F32, AR + 73728)
        LB = at("lb", [P, NB * H, P], F32, AR + 73728)
        RR = at("rr", [P, H, S], F32, AR + 73728)
        VB = at("vb", [P, H, P], F32, AR + 81920)
        KB = at("kb", [P, H, P], F32, AR + 83968)
        KD = at("kd", [P, H, P], F32, AR + 86016)
        NW = at("nw", [P, H, P], F32, AR + 88064)
        UU = at("uu", [P, H, P], F32, AR + 90112)
        QD = at("qd", [P, H, P], F32, AR + 92160)
        ST8 = at("state", [P, H, P], F32, AR + 94208)
        CS = at("cos_sin", [P, 2, S], F32, AR + 96256)
        DR = at("ret_decay", [P, H, S], F32, AR + 100352)
        RQ = at("rq", [P, 2, S], F32, AR + 108544)
        RK = at("rk", [P, 2, S], F32, AR + 112640)
        RS = at("ret_s", [P, 2, S], F32, AR + 116736)
        PAD = at("pad", [P, 2, S + 4], F32, AR + 120832)
        SC = at("scratch", [P, 4, S], F32, AR + 124960)
        MASK = at("masks", [P, 3 * P + 6 * 64], F32, AR + 133152)
        AB = at("ab", [8, S], F32, AR + 136224)
        ABR = at("ab_raw", [P, KT, 8], F32, AR + 138272)
        SM = at("small", [P, 12, 16], F32, G + 7264)
        ABH = at("ab_hi", [P, KT, 8], F32R, AR + 116736)
        ABL = at("ab_lo", [P, KT, 8], F32R, AR + 116736 + 256)
        ABT = SM[:, 0:2, :].rearrange("p a b -> p (a b)").rearrange("p (c e) -> p c e", e=8)
        UPPER = MASK[:, 0:P]
        LOWER = MASK[:, P:2 * P]
        PAIRM = MASK[:, 2 * P:3 * P]
        GG = SM[:, 2, :]
        BETA = SM[:, 3, :]
        GC = SM[:, 4, :]
        EGC = SM[:, 5, :]
        BEN = SM[:, 6, :]
        KDC = SM[:, 7, :]
        SPR = SM[:, 8, :]
        SPM = SM[:, 9, :]
        SPB = SM[:, 10, :]
        ALD = SM[:, 11, 0:8]

        RES = at("res", [P, KT, S], F32, AR)
        XB = at("x_b", [P, KT, 2, S], F32R, AR + 16384)
        ACTS = at("mlp_act", [P, FT, 2, S], F32R, AR + 49152)
        XTOK2 = at("x_tok2", [P, NB, D], F32, AR + 49152)
        XT2 = at("x_t2", [P, 2, S], F32, AR + 65536)
        SQ2 = at("sq2", [P, 2, S], F32, AR + 69632)
        PADF = at("pad_f", [P, 4, S + 4], F32, 32768)
        CF = at("conv_f", [P, 4, S], F32, 32768 + 8256)
        PRODF = at("prod_f", [P, 2, S], F32, 32768 + 16448)
        SQ4B = at("sq4b", [P, 2, S], F32, 32768 + 20544)

        A3 = AR + 49152
        QS = at("q_s", [P, 4, S], F32, A3)
        KS = at("k_s", [P, S], F32, A3 + 8192)
        VS = at("v_s", [P, NB, P], F32, A3 + 10240)
        GA = at("ga", [P, 4, S], F32, A3 + 12288)
        GB = at("gb", [P, 4, S], F32, A3 + 20480)
        PL = at("pooled", [P, 4, S], F32, A3 + 28672)
        ALI = at("alibi", [P, QH, 256], F32, A3 + 36864)
        SB = at("scores", [P, 2, 4, 256], F32, A3 + 45056)
        PTS = at("probs_t", [P, 4, 2, P], F32, A3 + 53248)
        MIXF = at("mix_f", [P, 8, S], F32, A3 + 57344)
        PW = at("pool_w", [P, 4, P], F32, A3 + 73728)
        UPD = at("u_pad", [P, 3, S + 16], F32, A3 + 75776)
        ITAB = at("inv_cnt", [P, 4, 16], F32, A3 + 82112)
        AS = at("att_small", [P, 8, 8], F32, A3 + 82368)
        SINK = at("sink", [P, QH], F32, A3 + 82624)
        SQ3 = at("sq3", [P, 2, S], F32, A3 + 82656)
        Y = at("y", [P, KT, S], F32, A3 + 57344)
        YT = at("y_t", [P, 2, S], F32, A3 + 75776)
        GPW = S + CK - 1
        GLU = at("glu", [P, KT, GPW], F32, A3)
        CV = at("conv", [P, KT, S], F32, A3 + 17344)
        GT3 = at("gate3", [P, KT, S], F32, A3 + 57344)
        PA = at("pool_acc", [P, 2, S], F32, A3 + 33728)
        PP = at("products", [P, 2, S], F32, A3 + 37824)
        ABUF = at("a_buf", [P, 4, S], F32, A3 + 41920)
        CT = at("c_t", [P, 2, S], F32, A3 + 50112)
        OTOK = at("out_tok", [P, NB, D], F32, A3 + 17344)

        PS = ctx.enter_context(nc.psum_tensor("ps", [P, 8, S], F32))
        MX = PS[:, 4:8, :]

        raw_in = [sem("raw_in0"), sem("raw_in1")]
        w_hi, w_lo = sem("w_hi_ready"), sem("w_lo_ready")
        half_done = sem("half_done")
        bank_free = sem("bank_free")
        op_src, op_hi, op_lo = sem("op_src"), sem("op_hi"), sem("op_lo")
        sq_ready, acc_done = sem("sq_ready"), sem("acc_done")
        stat_filled, rstd_ready = sem("stat_filled"), sem("rstd_ready")
        dchain, achain, gchain = sem("dve_step"), sem("act_step"), sem("pool_step")
        x_in, c_in, out_done = sem("x_in"), sem("const_in"), sem("out_done")
        c2_in, x2_in, ali_in = sem("const2_in"), sem("x2_in"), sem("alibi_in")
        xt_filled, xt_taken = sem("xt_filled"), sem("xt_taken")
        par_filled, par_ready = sem("par_filled"), sem("par_ready")
        ones_ready = sem("ones_ready")
        conv_ready, silu_done = sem("gdn_conv_ready"), sem("gdn_silu_done")
        ab_split, ab_filled, ab_rows = sem("ab_split"), sem("ab_filled"), sem("ab_rows")
        abt_filled, abt_ready, rcol_ready = sem("abt_filled"), sem("abt_ready"), sem("rcol_ready")
        sp_in, sp_done, gb_ready = sem("softplus_in"), sem("softplus_exp"), sem("g_beta_ready")
        sqk, ssq_filled, r4_ready = sem("kq_squares"), sem("kq_ssq_filled"), sem("kq_norm_ready")
        kq_normed, gu_ready = sem("kq_normed"), sem("gu_ready")
        gc_filled, gc_ready, lb_ready = sem("gc_filled"), sem("gc_ready"), sem("lb_ready")
        gcb_filled, eb_ready, x1_ready = sem("gcb_filled"), sem("eb_ready"), sem("x1_ready")
        dmm_ready, dexp, dt_ready = sem("dmm_ready"), sem("decay_exp"), sem("dt_ready")
        g_filled, m_ready, qk_filled = sem("g_filled"), sem("m_ready"), sem("qk_filled")
        qkt_ready, t2_ready = sem("qkt_ready"), sem("t2_ready")
        tt_filled, tt_ready = sem("tt_filled"), sem("tt_ready")
        xp_filled, xs_ready, xz_ready = sem("xp_filled"), sem("xs_ready"), sem("xz_ready")
        txp_filled, upd_done = sem("txp_filled"), sem("upd_done")
        rot_ready = sem("ret_rotated")
        rs_filled, rs_ready = sem("ret_s_filled"), sem("ret_s_ready")
        ro_filled, ro_ready = sem("ret_o_filled"), sem("ret_o_ready")
        rsq_ready, rssq_filled, rr_ready = sem("ret_sq"), sem("ret_ssq_filled"), sem("ret_rstd")
        tok_filled, tokv_ready, tokk_ready = sem("tok_filled"), sem("tok_v_ready"), sem("tok_k_ready")
        nw_filled, nw_ready = sem("nw_filled"), sem("nw_ready")
        u_filled, u_ready = sem("u_filled"), sem("u_ready")
        qd_ready = sem("qd_ready")
        so_filled, o_ready, s_ready = sem("so_filled"), sem("gdn_o_ready"), sem("state_ready")
        gate_done = sem("gate_silu")
        ff_conv, ff_silu = sem("ff_conv"), sem("ff_silu")
        sc_filled, sc_ready, p_exp, p_ready = (sem("scores_filled"), sem("scores_max"),
                                               sem("probs_exp"), sem("probs_ready"))
        pt_filled, pt_ready = sem("pt_filled"), sem("pt_ready")
        ov_filled, ov_taken = sem("att_o_filled"), sem("att_o_taken")
        pool_ready, py_filled, py_taken = sem("pooled_ready"), sem("pool_y_filled"), sem("pool_y_taken")
        ff_prod, ff_hi, ff_lo = sem("ff_product"), sem("ff_hi"), sem("ff_lo")
        sig_done = sem("sigmoid_done")
        ln_sum = sem("ln_sum")
        ln_in, ln_done = sem("ln_in"), sem("ln_silu")
        cm_filled, cm_taken = sem("mean_filled"), sem("mean_taken")
        ot_filled, ot_ready = sem("out_t_filled"), sem("out_t_ready")

        block = ctx.enter_context(nc.Block())

        def f32(ap):
            return ap.bitcast(F32)

        def vec(name, k=0):
            c = VEC_AT[name] + k
            return VEC[:, c:c + 1]

        @block.sync
        def _(sp):
            def rows(w, r0, n, c0):
                return w[r0:r0 + n * P, bass.ds(c0, 256)].rearrange("(k p) c -> p k c", p=P)

            def free_slot(p):
                sp.wait_ge(w_lo, 4 * (p - 1))

            def pair(p, slot, w, c0, r0=0, n=8):
                m = n // 2
                for k0, kn in ((0, m), (m, n - m)):
                    sp.dma_start(RAW[:, slot, k0:k0 + kn, :], rows(w, r0 + k0 * P, kn, c0)) \
                        .then_inc(raw_in[slot], 16)

            for b in range(NB):
                sp.dma_start(XTOK[:, b, :], a["x"][0, b * P:(b + 1) * P, :]).then_inc(x_in, 16)
            sp.dma_start(IDENT[:, :], const["ident"]).then_inc(c_in, 16)
            r = 0
            srcs = {"pre0": a["pre_norm_2"][0], "pre1": a["pre_norm_2"][1],
                    "post0": a["post_norm_2"][0], "post1": a["post_norm_2"][1],
                    "attn_norm_w": a["attn_norm_w"][0], "mlp_norm_w": a["mlp_norm_w"][0],
                    "final_norm_w": a["final_norm_w"], "pool_scale": a["b_pool_scale_2"][0],
                    "dw_b": a["c_dw_b_2"][0], "ln_g": a["c_ln_g_2"][0], "ln_b": a["c_ln_b_2"][0],
                    "gdn_norm_w": a["gdn_norm_w"][0]}
            for name, n in VECS:
                sp.dma_start(ROWS[r:r + n, 0, :], srcs[name].rearrange("(k p) -> k p", p=P)) \
                    .then_inc(c_in, 16)
                r += n
            w_in = a["w_in"][0]
            pair(0, 0, w_in, 512)
            sp.dma_start(ROWS[0:48, 1, :], a["gdn_conv_w"][0].rearrange("i (t p) -> (i t) p", p=P)) \
                .then_inc(c_in, 16)
            mc = a["mlp_conv_w"][0].rearrange("i (t p) -> (i t) p", p=P)
            dc = a["c_dw_w_2"][0, :, 0, :].rearrange("i (t p) -> (i t) p", p=P)
            sp.dma_start(ROWS[0:66, 2, :], mc[0:66, :]).then_inc(c_in, 16)
            sp.dma_start(ROWS[0:66, 5, :], mc[66:132, :]).then_inc(c_in, 16)
            sp.dma_start(ROWS[0:124, 3, :], dc[0:124, :]).then_inc(c_in, 16)
            sp.dma_start(ROWS[0:124, 4, :], dc[124:248, :]).then_inc(c_in, 16)
            pair(1, 1, w_in, 768)
            sp.dma_start(ABR[:, :, :], w_in[:, 4 * GW:4 * GW + 8].rearrange("(k p) c -> p k c", p=P)) \
                .then_inc(c2_in, 16)
            sp.dma_start(ALD[:, 0:4], a["gdn_a_log"][0].rearrange("(a n) -> a n", a=1)
                         .broadcast_to([P, 4])).then_inc(c2_in, 16)
            sp.dma_start(ALD[:, 4:8], a["gdn_dt_bias"][0].rearrange("(a n) -> a n", a=1)
                         .broadcast_to([P, 4])).then_inc(c2_in, 16)
            sp.dma_start(MASK[:, :], const["masks"]).then_inc(c2_in, 16)
            sp.dma_start(CS[:, :, :], const["cos_sin"]).then_inc(c2_in, 16)
            sp.dma_start(DR[:, :, :], const["ret_decay"]).then_inc(c2_in, 16)
            R = 4 * GW + 8
            starts = [512, 768, 0, 256, 1024, 1280, R + 1024, R + 1280, R, R + 512, R + 256, R + 768,
                      R + 1536, R + 1792, 1536, 1792]
            for p in range(2, 16):
                free_slot(p)
                pair(p, p % 2, w_in, starts[p])
            w_out = a["w_out"][0]
            for p in range(16, 20):
                free_slot(p)
                c0 = (p - 16) * 256
                for k0, r0 in ((0, GW), (4, 0)):
                    sp.dma_start(RAW[:, p % 2, k0:k0 + 4, :], rows(w_out, r0, 4, c0)) \
                        .then_inc(raw_in[p % 2], 16)
                if p == 17:
                    sp.wait_ge(op_lo, 16)
                    for b in range(NB):
                        sp.dma_start(XTOK2[:, b, :], a["x"][0, b * P:(b + 1) * P, :]).then_inc(x2_in, 16)
            w_up = a["w_up"][0]
            with sp.Fori(0, 11) as i:
                for s in range(2):
                    sp.wait_ge(w_lo, i * 8 + 4 * (U3 // 2 + s - 1))
                    pair(0, s, w_up, i * 256 + s * DFF)
            w_down = a["w_down"][0]
            with sp.Fori(0, 2) as i:
                for j in range(6):
                    sp.wait_ge(w_lo, i * 24 + 4 * (U4 // 2 + j - 1))
                    g = j % 3
                    pair(0, j % 2, w_down, i * 512 + 256 * (j // 3), r0=g * D, n=8 if g < 2 else 6)
            w5 = a["a_w_in_2"][0]
            for p in range(U5 // 2, U6 // 2):
                free_slot(p)
                j = p - U5 // 2
                if j in (0, 1, 3, 4):
                    c0 = (0 if j < 2 else 768) + 128 * ((j + 1) % 2 if j > 2 else j)
                    for kv in range(2):
                        sp.dma_start(RAW[:, p % 2, :, kv * P:(kv + 1) * P],
                                     w5[:, c0 + kv * 256:c0 + kv * 256 + P]
                                     .rearrange("(k p) c -> p k c", p=P)).then_inc(raw_in[p % 2], 16)
                else:
                    pair(p, p % 2, w5, {2: 512, 5: 1280, 6: 1536, 7: 1792, 8: 2048}[j])
                if j == 0:
                    sp.wait_ge(half_done, 2 * U5)
                    sp.dma_start(ALI[:, :, :], const["alibi"]).then_inc(ali_in, 16)
                    sp.dma_start(PW[:, :, :], a["b_pool_w_2"][0].rearrange("g c d -> c g d")) \
                        .then_inc(ali_in, 16)
                    sp.dma_start(ITAB[:, :, :], const["inv_cnt"]).then_inc(ali_in, 16)
                    sp.dma_start(SINK[:, :], a["a_sinks_2"][0].rearrange("(a n) -> a n", a=1)
                                 .broadcast_to([P, QH])).then_inc(ali_in, 16)
            w6 = a["ab_w_out_2"][0]
            for p in range(U6 // 2, U7 // 2):
                free_slot(p)
                c0 = (p - U6 // 2) * 256
                for kv in range(2):
                    sp.dma_start(RAW[kv * 64:(kv + 1) * 64, p % 2, 0:4, :],
                                 w6[kv * 256:(kv + 1) * 256, c0:c0 + 256]
                                 .rearrange("(t d) c -> d t c", d=HD2)).then_inc(raw_in[p % 2], 16)
                sp.dma_start(RAW[:, p % 2, 4:8, :], rows(w6, 512, 4, c0)).then_inc(raw_in[p % 2], 16)
            w7 = a["c_w_in_2"][0]
            with sp.Fori(0, 4) as i:
                for s in range(2):
                    sp.wait_ge(w_lo, i * 8 + 4 * (U7 // 2 + s - 1))
                    pair(0, (U7 // 2 + s) % 2, w7, i * 256 + s * D)
            for p in range(U7 // 2 + 8, U8 // 2):
                free_slot(p)
                pair(p, p % 2, w7, 2 * D + (p - U7 // 2 - 8) * 256)
            w8 = a["c_w_out_2"][0]
            for p in range(U8 // 2, PAIRS):
                free_slot(p)
                pair(p, p % 2, w8, (p - U8 // 2) * 256)
            for b in range(NB):
                sp.wait_ge(ot_ready, KT)
                sp.dma_start(out[0, b * P:(b + 1) * P, :], OTOK[:, b, :]).then_inc(out_done, 16)
            sp.wait_ge(out_done, 16 * NB)

        def half_k(n):
            u = n // 2
            return 3 if U4 <= u < U5 and ((u - U4) // 2) % 3 == 2 else 4

        def by_heads(n):
            u = n // 2
            return U5 <= u < U5 + 4 or U5 + 6 <= u < U5 + 10

        def raw_half(n):
            kn = half_k(n)
            r = RAW[:, (n // 4) % 2, kn * (n % 2):kn * (n % 2) + kn, :]
            t = (n // 2) % 2
            if by_heads(n):
                return r.rearrange("p k (v t d) -> p k v t d", v=2, t=2)[:, :, :, t, :]
            return r[:, :, t * P:(t + 1) * P]

        def ring_half(w, n):
            w = w[:, n % 4, 0:half_k(n), :]
            return w.rearrange("p k (v d) -> p k v d", v=2) if by_heads(n) else w

        @block.gpsimd
        def _(gp):
            def split_lo(n, later=0):
                gp.wait_ge(w_hi, later + n + 1)
                nc.gpsimd.tensor_tensor(ring_half(WL, n), raw_half(n), f32(ring_half(WH, n)), SUB) \
                    .then_inc(w_lo, 1)

            def unit(u):
                split_lo(2 * u)
                split_lo(2 * u + 1)

            def zero(level, c):
                x = XZ[:, c, :, :].rearrange("p h (b two s) -> p h b two s", two=2, s=2 << level)
                nc.gpsimd.memset(x[:, :, :, 0, :], 0.0).then_inc(xz_ready, 1)

            nc.gpsimd.memset(ONES[:, :], 1.0).then_inc(ones_ready, 1)
            nc.gpsimd.memset(CB[:, 0:1], EPS).then_inc(ones_ready, 1)
            nc.gpsimd.memset(CB[:, 1:2], math.log(P ** -0.5)).then_inc(ones_ready, 1)
            nc.gpsimd.memset(CB[:, 2:3], 1.0).then_inc(ones_ready, 1)
            nc.gpsimd.memset(PAD[:, :, 0:3], 0.0).then_inc(ones_ready, 1)
            for u in range(14):
                unit(u)
            gp.wait_ge(gb_ready, 1)
            gp.wait_ge(c2_in, 96)
            nc.gpsimd.tensor_tensor(LB[:, :, :], LOWER.unsqueeze(1).broadcast_to([P, 16, P]),
                                    BETA.unsqueeze(2).broadcast_to([P, 16, P]), MUL).then_inc(lb_ready, 1)
            unit(14)
            unit(15)
            gp.wait_ge(dexp, 1)
            nc.gpsimd.tensor_tensor(T[:, :, :], T[:, :, :], UPPER.unsqueeze(1).broadcast_to([P, 16, P]),
                                    MUL).then_inc(dt_ready, 1)
            unit(16)
            gp.wait_ge(m_ready, 1)
            for c in range(NB):
                zero(0, c)
            unit(17)
            unit(18)
            for level in range(5):
                unit(19 + level)
                for c in range(NB):
                    gp.wait_ge(txp_filled, 4 * level + c + 1)
                    zero(level + 1, c)
            for u in range(24, U3):
                unit(u)
            with gp.Fori(0, 11) as i:
                for j in range(8):
                    split_lo(2 * U3 + j, i * 8)
            for u in range(U4, UNITS):
                unit(u)

        @block.scalar
        def _(act):
            steps = [0]

            def step(ins):
                steps[0] += 1
                ins.then_inc(achain, 1)
                act.wait_ge(achain, steps[0])

            def split_hi(n, i=None):
                p = n // 4
                if n >= UNITS * 2:
                    return
                if i is None:
                    act.wait_ge(raw_in[p % 2], 16 * loads_before(p))
                    if n >= 4:
                        act.wait_ge(half_done, n - 3)
                else:
                    act.wait_ge(raw_in[p % 2], i * 32 + 16 * loads_before(p))
                    act.wait_ge(half_done, i * 8 + n - 3)
                nc.scalar.activation(ring_half(WH, n), raw_half(n), ACT.Copy).then_inc(w_hi, 1)

            def splits(u):
                split_hi(2 * u + 3)
                split_hi(2 * u + 4)

            def operand_hi(src, dst, scale):
                nc.scalar.activation(dst, src, ACT.Copy, scale=scale).then_inc(op_hi, 1)

            def square(st, k, src, dst):
                if k >= 2:
                    act.wait_ge(acc_done, 8 * st + k - 1)
                nc.scalar.activation(dst, src, ACT.Square).then_inc(sq_ready, 1)

            def stat(st):
                act.wait_ge(stat_filled, st + 1)
                step(nc.scalar.activation(RSTD[:, :], PS[:, 7, :], ACT.Ln, bias=CB[:, 0:1], scale=1.0 / D))
                nc.scalar.activation(RSTD[:, :], RSTD[:, :], ACT.Exp, scale=-0.5).then_inc(rstd_ready, 1)

            act.wait_ge(par_ready, 1)
            act.wait_ge(ones_ready, 5)
            for k in range(KT):
                act.wait_ge(op_src, k + 1)
                operand_hi(SC[:, k % 2, :], XA[:, k, 0, :], vec("attn_norm_w", k))
                square(0, k, SC[:, k % 2, :], SC[:, 2 + k % 2, :])
                if k % 2 == 1 and k < 7:
                    split_hi(k // 2)

            def tile_silu(u):
                act.wait_ge(conv_ready, u + 1)
                d = KQ[:, u % 4, u // 4, :] if u < 8 else V[:, u - 8, :]
                nc.scalar.activation(d, d, ACT.Silu).then_inc(silu_done, 1)

            def values(c):
                act.wait_ge(tok_filled, 2 * c + 2)
                for h in range(H):
                    nc.scalar.activation(VB[:, h, :], PS[:, 5, h * P:(h + 1) * P], ACT.Copy,
                                         scale=BETA[:, 4 * c + h:4 * c + h + 1]).then_inc(tokv_ready, 1)

            def new_values(c):
                act.wait_ge(u_filled, c + 1)
                nc.scalar.activation(UU[:, :, :], PS[:, 7, :].rearrange("p (h v) -> p h v", h=H), ACT.Copy) \
                    .then_inc(u_ready, 1)

            def outputs(c):
                act.wait_ge(so_filled, 2 * c + 1)
                nc.scalar.activation(KQ[:, :, 1, c * P:(c + 1) * P],
                                     PS[:, 6, :].rearrange("p (h i) -> p h i", h=H), ACT.Copy) \
                    .then_inc(o_ready, 1)

            def weights_t(c):
                act.wait_ge(nw_filled, c)
                nc.scalar.activation(NW[:, :, :], PS[:, 6, :].rearrange("p (h c) -> p h c", h=H), ACT.Copy) \
                    .then_inc(nw_ready, 1)

            def ret_out(h):
                act.wait_ge(ro_filled, h + 1)
                nc.scalar.activation(RV[:, h, :, :].rearrange("p b i -> p (b i)"), PS[:, 6, :], ACT.Copy) \
                    .then_inc(ro_ready, 1)

            def ret_norm(r):
                act.wait_ge(rssq_filled, r + 1)
                rr = RR[:, 2 * r:2 * r + 2, :]
                step(nc.scalar.activation(rr, MX[:, 0:2, :], ACT.Ln, bias=CB[:, 0:1], scale=1.0 / P))
                nc.scalar.activation(rr, rr, ACT.Exp, scale=-0.5).then_inc(rr_ready, 1)

            for u in range(U1, U2):
                splits(u)
                if u == 0:
                    stat(0)
                if 1 <= u <= 12:
                    tile_silu(u - 1)
                if u == 12:
                    act.wait_ge(silu_done, 8)
                    nc.scalar.activation(SQ4[:, :, :], KQ[:, :, 0, :], ACT.Square).then_inc(sqk, 1)
                    act.wait_ge(sp_in, 1)
                    step(nc.scalar.activation(SPM, SPM, ACT.Exp))
                    step(nc.scalar.activation(SPM, SPM, ACT.Ln, bias=CB[:, 2:3]))
                    step(nc.scalar.activation(ALD[:, 0:4], ALD[:, 0:4], ACT.Exp))
                    nc.scalar.activation(SPB, SPB, ACT.Exp, scale=-1.0).then_inc(sp_done, 1)
                    act.wait_ge(ssq_filled, 1)
                    step(nc.scalar.activation(R4[:, :, :], MX, ACT.Ln, bias=CB[:, 0:1]))
                    nc.scalar.activation(R4[:, :, :], R4[:, :, :], ACT.Exp, scale=-0.5).then_inc(r4_ready, 1)
                    nc.scalar.activation(SQ4[:, :, :], KQ[:, :, 1, :], ACT.Square).then_inc(sqk, 1)
                if u == 13:
                    act.wait_ge(ssq_filled, 2)
                    act.wait_ge(kq_normed, 1)
                    step(nc.scalar.activation(R4[:, :, :], MX, ACT.Ln, bias=CB[:, 0:1]))
                    nc.scalar.activation(R4[:, :, :], R4[:, :, :], ACT.Exp, scale=-0.5, bias=CB[:, 1:2]) \
                        .then_inc(r4_ready, 1)
                if u == 14:
                    act.wait_ge(gc_ready, 1)
                    nc.scalar.activation(EGC, GC, ACT.Exp).then_inc(eb_ready, 1)
                    act.wait_ge(gcb_filled, 1)
                    nc.scalar.activation(EB[:, :, :].rearrange("p a i -> p (a i)"),
                                         MX.rearrange("p b s -> p (b s)"), ACT.Exp).then_inc(eb_ready, 1)
                    act.wait_ge(dmm_ready, 1)
                    nc.scalar.activation(T[:, :, :], T[:, :, :], ACT.Exp).then_inc(dexp, 1)
                    act.wait_ge(dmm_ready, 2)
                    nc.scalar.activation(M[:, :, :], M[:, :, :], ACT.Exp, scale=-1.0).then_inc(dexp, 1)
                if u == 17:
                    act.wait_ge(tt_filled, 1)
                    nc.scalar.activation(TT[:, :, :].rearrange("p a i -> p (a i)"),
                                         MX.rearrange("p b s -> p (b s)"), ACT.Copy).then_inc(tt_ready, 1)
                if u in RET_GAP:
                    ret_out(RET_GAP.index(u))
                if u == 24:
                    values(0)
                if u == 25:
                    act.wait_ge(ro_ready, 4)
                    nc.scalar.activation(RR[:, :, :], RV[:, :, :, :].rearrange("p h b i -> p h (b i)"),
                                         ACT.Square).then_inc(rsq_ready, 1)
                    ret_norm(0)
                if u == 26:
                    new_values(0)
                    values(1)
                    outputs(0)
                if u == 27:
                    weights_t(1)
                    ret_norm(1)
                if u == 28:
                    new_values(1)
                    values(2)
                    outputs(1)
                if u == 29:
                    act.wait_ge(bank_free, M1 + 28)
                    nc.scalar.activation(GT[:, 0:4, :], GT[:, 0:4, :], ACT.Silu).then_inc(gate_done, 1)
                    weights_t(2)
                if u == 30:
                    new_values(2)
                    values(3)
                    outputs(2)
                if u == 31:
                    weights_t(3)
                    new_values(3)
                    outputs(3)
            act.wait_ge(half_done, 2 * U2)
            for h in range(H):
                act.wait_ge(op_src, 8 + h + 1)
                operand_hi(RV[:, h, :, :].rearrange("p b i -> p (b i)"), XA[:, h, 0, :], 1.0)
            act.wait_ge(o_ready, 4)
            nc.scalar.activation(RR[:, :, :], KQ[:, :, 1, :], ACT.Square).then_inc(rsq_ready, 1)
            act.wait_ge(rssq_filled, 3)
            step(nc.scalar.activation(RR[:, :, :], MX, ACT.Ln, bias=CB[:, 0:1], scale=1.0 / P))
            nc.scalar.activation(RR[:, :, :], RR[:, :, :], ACT.Exp, scale=-0.5).then_inc(rr_ready, 1)
            act.wait_ge(bank_free, M1 + 32)
            nc.scalar.activation(GT[:, 4:8, :], GT[:, 4:8, :], ACT.Silu).then_inc(gate_done, 1)
            for h in range(H):
                act.wait_ge(op_src, 12 + h + 1)
                operand_hi(KQ[:, h, 1, :], XA[:, 4 + h, 0, :], 1.0)

            def from_residual(k):
                act.wait_ge(bank_free, M2 + k + 1)
                operand_hi(RES[:, k, :], XB[:, k, 0, :], vec("mlp_norm_w", k))
                square(1, k, RES[:, k, :], SQ2[:, k % 2, :])

            for u in range(U2, U3):
                k = u - U2
                splits(u)
                act.wait_ge(xt_filled, 8 + k + 1)
                if k >= 2:
                    act.wait_ge(bank_free, M2 + k - 1)
                nc.scalar.activation(XT2[:, k % 2, :], PS[:, 4 + k % 4, :], ACT.Copy).then_inc(xt_taken, 1)
                if k >= 1:
                    from_residual(k - 1)
            from_residual(KT - 1)
            stat(1)
            with act.Fori(0, 11) as i:
                for j in range(4):
                    split_hi(2 * (U3 + j) + 3, i)
                    split_hi(2 * (U3 + j) + 4, i)
                    if j < 2:
                        act.wait_ge(ff_conv, i * 2 + j + 1)
                        nc.scalar.activation(CF[:, j, :], CF[:, j, :], ACT.Silu).then_inc(ff_silu, 1)
                    else:
                        act.wait_ge(ff_prod, i * 2 + j - 1)
                        nc.scalar.activation(ACTS[:, bass.ds(i * 2 + (j - 2), 1), 0, :]
                                             .rearrange("p a s -> p (a s)"), PRODF[:, j - 2, :], ACT.Copy) \
                            .then_inc(ff_hi, 1)

            for u in range(U4, U5 + 1):
                if u > U4 and (u - U4) % 6 == 0:
                    for k in (2 * ((u - U4) // 6) - 2, 2 * ((u - U4) // 6) - 1):
                        act.wait_ge(bank_free, M4 + k + 1)
                        square(2, k, RES[:, k, :], SQ4B[:, k % 2, :])
                if u < U5:
                    splits(u)
            stat(2)
            for k in range(KT):
                act.wait_ge(op_src, 16 + k + 1)
                operand_hi(RES[:, k, :], XA[:, k, 0, :], vec("pre0", k))
                square(3, k, RES[:, k, :], SQ3[:, k % 2, :])

            def probs(j):
                act.wait_ge(sc_ready, j + 1)
                lo = P if j < 2 else 0
                for t in range(4):
                    nc.scalar.activation(SB[:, j % 2, t, lo:256], SB[:, j % 2, t, lo:256], ACT.Exp,
                                         bias=AS[:, 1, t:t + 1], accum_out=AS[:, 2, t:t + 1]) \
                        .then_inc(p_exp, 1)
                nc.scalar.activation(AS[:, 3, 0:4], AS[:, 3, 0:4], ACT.Exp).then_inc(p_exp, 1)

            for u in range(U5, U6):
                splits(u)
                if u == U5:
                    stat(3)
                j = u - (U5 + 6)
                if 1 <= j <= 8:
                    act.wait_ge(pt_filled, j)
                    lo = 1 if j - 1 < 2 else 0
                    nc.scalar.activation(PTS[:, :, lo:2, :],
                                         PS[:, 6:8, :].rearrange("p b (t w i) -> p (b t) w i", t=2, w=2)
                                         [:, :, lo:2, :], ACT.Copy).then_inc(pt_ready, 1)
                if 0 <= j < 8:
                    probs(j)
                if 1 <= j <= 8:
                    b, kv = (j - 1) // 2, (j - 1) % 2
                    act.wait_ge(ov_filled, j)
                    nc.scalar.activation(MIXF[kv * HD2:(kv + 1) * HD2, 0:4, b * P:(b + 1) * P],
                                         PS[kv * HD2:(kv + 1) * HD2, 6, :]
                                         .rearrange("p (t i) -> p t i", t=4), ACT.Copy).then_inc(ov_taken, 1)
                if j == 9:
                    act.wait_ge(py_filled, 1)
                    for g in range(4):
                        nc.scalar.activation(PL[:, g, :], MX[:, g, :], ACT.Copy,
                                             scale=vec("pool_scale", g)).then_inc(py_taken, 1)
                    act.wait_ge(bank_free, M5 + 10)
                    nc.scalar.activation(GA[:, :, :], GA[:, :, :], ACT.Silu).then_inc(gate_done, 1)
                if j == 10:
                    for t in range(4):
                        act.wait_ge(op_src, 24 + t + 1)
                        operand_hi(MIXF[:, t, :], XB[:, t, 0, :], 1.0)
                if j >= 9:
                    g = j - 9
                    act.wait_ge(bank_free, M5 + 14 + g + 1)
                    nc.scalar.activation(GB[:, g, :], GB[:, g, :], ACT.Silu).then_inc(gate_done, 1)
            act.wait_ge(bank_free, M5 + 18)
            nc.scalar.activation(GB[:, 3, :], GB[:, 3, :], ACT.Silu).then_inc(gate_done, 1)
            for g in range(4):
                act.wait_ge(op_src, 28 + g + 1)
                operand_hi(MIXF[:, 4 + g, :], XB[:, 4 + g, 0, :], 1.0)

            for u in range(U6, U7):
                splits(u)
                k = u - U6
                if k >= 1:
                    act.wait_ge(bank_free, M6 + k)
                    square(4, k - 1, Y[:, k - 1, :], SQ3[:, (k - 1) % 2, :])
            act.wait_ge(bank_free, M6 + KT)
            square(4, KT - 1, Y[:, KT - 1, :], SQ3[:, 1, :])
            stat(4)
            for k in range(KT):
                act.wait_ge(op_src, 32 + k + 1)
                operand_hi(RES[:, k, :], XA[:, k, 0, :], vec("pre1", k))
                square(5, k, RES[:, k, :], SQ3[:, k % 2, :])
            stat(5)
            for u in range(U7, U8):
                splits(u)
                j = u - U7
                if j < 16 and j % 4 >= 2:
                    act.wait_ge(bank_free, M7 + j + 1)
                    nc.scalar.activation(ABUF[:, j % 4, :], ABUF[:, j % 4, :], ACT.Sigmoid) \
                        .then_inc(sig_done, 1)
            for k in range(KT):
                act.wait_ge(bank_free, M7 + 16 + k + 1)
                nc.scalar.activation(GT3[:, k, :], GT3[:, k, :], ACT.Silu).then_inc(gate_done, 1)
            for k in range(KT):
                act.wait_ge(cm_taken, k + 1)
                square(6, k, CV[:, k, :], CT[:, k % 2, :])
            stat(6)
            for k in range(KT + 1):
                if k < KT:
                    act.wait_ge(ln_in, k + 1)
                    nc.scalar.activation(CV[:, k, :], CV[:, k, :], ACT.Silu, bias=vec("ln_b", k)) \
                        .then_inc(ln_done, 1)
                if k >= 1:
                    act.wait_ge(op_src, 40 + k)
                    operand_hi(CV[:, k - 1, :], XB[:, k - 1, 0, :], 1.0)
            for u in range(U8, UNITS):
                splits(u)
                k = u - U8
                if k >= 1:
                    act.wait_ge(bank_free, M8 + k)
                    square(7, k - 1, Y[:, k - 1, :], CT[:, (k - 1) % 2, :])
            act.wait_ge(bank_free, M8 + KT)
            square(7, KT - 1, Y[:, KT - 1, :], CT[:, 1, :])
            stat(7)
            for k in range(KT):
                act.wait_ge(ot_filled, k + 1)
                nc.scalar.activation(OTOK[:, :, k * P:(k + 1) * P],
                                     PS[:, 4 + k % 4, :].rearrange("p (b f) -> p b f", b=NB), ACT.Copy) \
                    .then_inc(ot_ready, 1)

        @block.vector
        def _(dve):
            v = nc.vector
            steps = [0]
            late = [None]

            def step(ins):
                steps[0] += 1
                ins.then_inc(dchain, 1)
                dve.wait_ge(dchain, steps[0] if late[0] is None else late[0] + steps[0])

            def tile_done(u):
                dve.wait_ge(half_done, 2 * (u + 1))

            def operand_lo(f, src, dst_lo, dst_hi, scale=1.0):
                dve.wait_ge(op_hi, f + 1)
                v.scalar_tensor_tensor(out=dst_lo, in0=src, scalar=scale, in1=f32(dst_hi), op0=MUL, op1=SUB) \
                    .then_inc(op_lo, 1)

            def accumulate(st, k, sq):
                n = 8 * st + k
                dve.wait_ge(sq_ready, n + 1)
                if k == 0:
                    v.tensor_copy(ACC[:, :], sq).then_inc(acc_done, 1)
                else:
                    dve.wait_ge(acc_done, n)
                    v.tensor_tensor(ACC[:, :], ACC[:, :], sq, ADD).then_inc(acc_done, 1)

            MX16 = MX.rearrange("p b (h i) -> p (b h) i", h=H)

            def lastdim(ap):
                return ap.unsqueeze(2).broadcast_to([P, 16, P])

            dve.wait_ge(par_filled, 1)
            v.tensor_copy(VEC[:, :], PS[:, 0, 0:NVEC]).then_inc(par_ready, 1)
            v.tensor_copy(GCW[:, :, :].rearrange("p a b -> p (a b)"), PS[:, 0, NVEC:NVEC + 48]) \
                .then_inc(par_ready, 1)
            v.tensor_copy(MCW[:, :, :].rearrange("p a b -> p (a b)"), PS[:, 0, NVEC + 48:NVEC + 180]) \
                .then_inc(par_ready, 1)
            v.tensor_copy(DCW[:, :, :].rearrange("p a b -> p (a b)"), PS[:, 1, 0:248]).then_inc(par_ready, 1)
            dve.wait_ge(par_ready, 4)
            for k in range(KT + 1):
                if k < KT:
                    dve.wait_ge(xt_filled, k + 1)
                    if k >= 2:
                        dve.wait_ge(op_lo, k - 1)
                    v.tensor_copy(SC[:, k % 2, :], PS[:, 4 + k % 4, :]).then_inc(op_src, 1)
                if k >= 1:
                    q = k - 1
                    dve.wait_ge(op_src, q + 1)
                    operand_lo(q, SC[:, q % 2, :], XA[:, q, 1, :], XA[:, q, 0, :], vec("attn_norm_w", q))
                    accumulate(0, q, SC[:, 2 + q % 2, :])

            def conv_tile(u):
                t = {0: 4, 1: 0, 2: 8}[u // 4] + u % 4
                d = KQ[:, u % 4, u // 4, :] if u < 8 else V[:, u - 8, :]
                x = PAD[:, u % 2, :]
                v.tensor_tensor(x[:, 3:3 + S], PS[:, u % 4, :], RSTD[:, :], MUL).then_inc(bank_free, 1)
                dve.wait_ge(bank_free, u + 1)
                step(v.tensor_scalar(d, x[:, 3:3 + S], GCW[:, 3, t:t + 1], None, MUL))
                for i in (2, 1):
                    step(v.scalar_tensor_tensor(out=d, in0=x[:, i:i + S], scalar=GCW[:, i, t:t + 1],
                                                in1=d, op0=MUL, op1=ADD))
                v.scalar_tensor_tensor(out=d, in0=x[:, 0:S], scalar=GCW[:, 0, t:t + 1], in1=d,
                                       op0=MUL, op1=ADD).then_inc(conv_ready, 1)

            SWAP = [i ^ 1 for i in range(32)]

            def rotate_tile(u):
                h = u % 2 + 2 * ((u - 16) // 4)
                d = (RQ if (u - 16) % 4 < 2 else RK)[:, h % 2, :]
                if h >= 2:
                    dve.wait_ge(rs_filled, 4 * (h - 1))
                step(v.tensor_tensor(d, PS[:, u % 4, :], CS[:, 0, :], MUL))
                v.stream_shuffle(SC[:, u % 2, :], PS[:, u % 4, :], SWAP).then_inc(bank_free, 1)
                dve.wait_ge(bank_free, u + 1)
                step(v.tensor_tensor(SC[:, u % 2, :], SC[:, u % 2, :], CS[:, 1, :], MUL))
                v.tensor_tensor(d, d, SC[:, u % 2, :], ADD).then_inc(rot_ready, 1)

            def level(l):
                s = 2 << l
                def half(ap, two):
                    return ap.rearrange("p h (b two s) -> p h b two s", two=2, s=s)[:, :, :, two, :]
                def part(bank, off):
                    return PS[:, bank, off:off + 256].rearrange("p (h b s) -> p h b s", h=H, s=s)
                mask = MASK[:, 3 * P + 64 * l:3 * P + 64 * (l + 1)].rearrange("p (b s) -> p b s", s=s) \
                    .unsqueeze(1).broadcast_to([P, H, 64 // s, s])
                for c in range(NB):
                    dve.wait_ge(xp_filled, 4 * l + c + 1)
                    v.tensor_tensor(half(XZ[:, c, :, :], 1), part(4 + c, 0), mask, MUL).then_inc(xs_ready, 1)
                for c in range(NB):
                    dve.wait_ge(txp_filled, 4 * l + c + 1)
                    u_ = half(TT[:, 4 * c:4 * c + 4, :], 1)
                    ins = v.tensor_tensor(u_, u_, part(4 + c, 256), SUB)
                    if l < 5:
                        t_ = half(T[:, 4 * c:4 * c + 4, :], 0)
                        ins = v.tensor_tensor(t_, t_, part(4 + c, 0), SUB)
                    ins.then_inc(upd_done, 1)

            def ret_scores(h):
                for jb in range(NB):
                    n = S - jb * P
                    dve.wait_ge(rs_filled, 4 * h + jb + 1)
                    v.tensor_tensor(RS[:, jb % 2, 0:n], PS[:, 4 + jb % 2, 0:n], DR[:, h, 0:n], MUL) \
                        .then_inc(rs_ready, 1)

            def keys(c):
                kt = PS[:, 4, :].rearrange("p (h d) -> p h d", h=H)
                dve.wait_ge(tok_filled, 2 * c + 1)
                if c > 0:
                    step(v.tensor_tensor(KB[:, :, :], kt, BEN[:, 4 * c:4 * c + 4].unsqueeze(2)
                                         .broadcast_to([P, H, P]), MUL))
                    state(c - 1)
                v.tensor_tensor(KD[:, :, :], kt, KDC[:, 4 * c:4 * c + 4].unsqueeze(2)
                                .broadcast_to([P, H, P]), MUL).then_inc(tokk_ready, 1)
                if c > 0:
                    v.tensor_tensor(QD[:, :, :], KQ[:, :, 1, c * P:(c + 1) * P],
                                    EB[:, 4 * c:4 * c + 4, :], MUL).then_inc(qd_ready, 1)

            def state(c):
                dve.wait_ge(so_filled, 2 * c + 2)
                for h in range(H):
                    ps = PS[:, 7, h * P:(h + 1) * P]
                    if c == 0:
                        ins = v.tensor_copy(ST8[:, h, :], ps)
                    else:
                        ins = v.scalar_tensor_tensor(out=ST8[:, h, :], in0=ST8[:, h, :],
                                                     scalar=EB[:, 4 * c + h, P - 1:P], in1=ps,
                                                     op0=MUL, op1=ADD)
                ins.then_inc(s_ready, 1)

            for u in range(U1, U2):
                if u == 3:
                    tile_done(u)
                    dve.wait_ge(ab_filled, 1)
                    v.tensor_tensor(AB[:, :], PS[0:8, 7, :], RSTD[0:8, :], MUL).then_inc(ab_rows, 1)
                if u == 4:
                    dve.wait_ge(abt_filled, 1)
                    step(v.tensor_copy(ABT, PS[:, 7, 0:32].rearrange("p (c e) -> p c e", e=8)))
                    v.tensor_copy(RCOL[:, :], PS[:, 6, 0:NB]).then_inc(rcol_ready, 1)
                    spm, spr, spb = (x.rearrange("p (c h) -> p c h", h=H) for x in (SPM, SPR, SPB))
                    step(v.tensor_tensor(spr, ABT[:, :, 0:4],
                                         ALD[:, 4:8].unsqueeze(1).broadcast_to([P, NB, H]), ADD))
                    step(v.scalar_tensor_tensor(out=SPM, in0=SPR, scalar=-1.0, in1=SPR, op0=MUL, op1=ALU.min))
                    step(v.tensor_scalar(SPR, SPR, 0.0, None, ALU.max))
                    v.tensor_copy(spb, ABT[:, :, 4:8]).then_inc(sp_in, 1)
                if u == 12:
                    dve.wait_ge(sp_done, 1)
                    gg = GG.rearrange("p (c h) -> p c h", h=H)
                    spr = SPR.rearrange("p (c h) -> p c h", h=H)
                    step(v.tensor_tensor(SPR, SPR, SPM, ADD))
                    step(v.scalar_tensor_tensor(out=gg, in0=spr, scalar=-1.0,
                                                in1=ALD[:, 0:4].unsqueeze(1).broadcast_to([P, NB, H]),
                                                op0=MUL, op1=MUL))
                    step(v.tensor_scalar(SPB, SPB, 1.0, None, ADD))
                    v.reciprocal(BETA, SPB).then_inc(gb_ready, 1)
                    v.tensor_tensor(T[:, :, :], UPPER.unsqueeze(1).broadcast_to([P, 16, P]), lastdim(GG), MUL) \
                        .then_inc(gu_ready, 1)
                    dve.wait_ge(r4_ready, 1)
                    v.tensor_tensor(KQ[:, :, 0, :], KQ[:, :, 0, :], R4[:, :, :], MUL).then_inc(kq_normed, 1)
                if u == 13:
                    dve.wait_ge(gc_filled, 1)
                    v.tensor_copy(GC, PS[:, 4, 0:16]).then_inc(gc_ready, 1)
                    dve.wait_ge(r4_ready, 2)
                    v.tensor_tensor(KQ[:, :, 1, :], KQ[:, :, 1, :], R4[:, :, :], MUL).then_inc(kq_normed, 1)
                if u == 14:
                    dve.wait_ge(eb_ready, 1)
                    step(v.scalar_tensor_tensor(out=BEN, in0=BETA, scalar=-1.0, in1=EGC, op0=MUL, op1=MUL))
                    dve.wait_ge(eb_ready, 2)
                    v.tensor_tensor(TT[:, :, :], MX16, lastdim(GC), SUB).then_inc(x1_ready, 1)
                    dve.wait_ge(x1_ready, 1)
                    v.tensor_scalar(T[:, :, :], TT[:, :, :], 0.0, None, ALU.min).then_inc(dmm_ready, 1)
                    v.tensor_scalar(M[:, :, :], TT[:, :, :], 0.0, None, ALU.max).then_inc(dmm_ready, 1)
                    dve.wait_ge(lb_ready, 1)
                    dve.wait_ge(dexp, 2)
                    step(v.tensor_tensor(M[:, :, :], M[:, :, :], LB[:, :, :], MUL))
                if u == 15:
                    dve.wait_ge(g_filled, 1)
                    v.tensor_tensor(M[:, :, :], MX16, M[:, :, :], MUL).then_inc(m_ready, 1)
                if u == 16:
                    dve.wait_ge(dt_ready, 1)
                    v.tensor_copy(KDC.unsqueeze(2), T[:, :, P - 1:P])
                    dve.wait_ge(qk_filled, 1)
                    v.tensor_tensor(QKT[:, :, :], MX16, T[:, :, :], MUL).then_inc(qkt_ready, 1)
                    dve.wait_ge(qkt_ready, 1)
                    dve.wait_ge(m_ready, 1)
                    step(v.tensor_tensor(T[:, :, :], M[:, :, :], PAIRM.unsqueeze(1).broadcast_to([P, 16, P]), MUL))
                    v.scalar_tensor_tensor(out=T[:, :, :], in0=T[:, :, :], scalar=-1.0,
                                           in1=IDENT[:, :].unsqueeze(1).broadcast_to([P, 16, P]),
                                           op0=MUL, op1=ADD).then_inc(t2_ready, 1)
                if 18 <= u <= 23:
                    level(u - 18)
                if u in RET_GAP:
                    ret_scores(RET_GAP.index(u))
                if u in (24, 26, 28, 30):
                    keys((u - 24) // 2)

                tile_done(u)
                if u == 0:
                    dve.wait_ge(rstd_ready, 1)
                if u < 12:
                    conv_tile(u)
                elif u < 16:
                    if u == 12:
                        dve.wait_ge(rcol_ready, 1)
                    v.tensor_tensor(RV[:, u - 12, :, :], PS[:, u % 4, :].rearrange("p (b d) -> p b d", b=NB),
                                    RCOL[:, :].unsqueeze(2).broadcast_to([P, NB, P]), MUL) \
                        .then_inc(bank_free, 1)
                elif u < 24:
                    rotate_tile(u)
                else:
                    v.tensor_tensor(GT[:, u - 24, :], PS[:, u % 4, :], RSTD[:, :], MUL).then_inc(bank_free, 1)
                if u == 1:
                    dve.wait_ge(c2_in, 96)
                    v.tensor_copy(ABH[:, :, :], ABR[:, :, :]).then_inc(ab_split, 1)
                    dve.wait_ge(ab_split, 1)
                    v.tensor_tensor(ABL[:, :, :], ABR[:, :, :], f32(ABH[:, :, :]), SUB).then_inc(ab_split, 1)
                    v.tensor_tensor(CS[:, 0, :], CS[:, 0, :], RSTD[:, :], MUL)
                    step(v.tensor_tensor(CS[:, 1, :], CS[:, 1, :], RSTD[:, :], MUL))
                if u == 30:
                    dve.wait_ge(rr_ready, 2)
                    for h in range(H):
                        o = RV[:, h, :, :].rearrange("p b i -> p (b i)")
                        step(v.tensor_tensor(o, o, RR[:, h, :], MUL))
                        if h == 0:
                            dve.wait_ge(gate_done, 1)
                        v.tensor_tensor(o, o, GT[:, h, :], MUL).then_inc(op_src, 1)
            for h in range(H):
                operand_lo(8 + h, RV[:, h, :, :].rearrange("p b i -> p (b i)"), XA[:, h, 1, :], XA[:, h, 0, :])
            dve.wait_ge(rr_ready, 3)
            for h in range(H + 1):
                if h < H:
                    o = KQ[:, h, 1, :]
                    step(v.scalar_tensor_tensor(out=o, in0=o, scalar=vec("gdn_norm_w"), in1=RR[:, h, :],
                                                op0=MUL, op1=MUL))
                    if h == 0:
                        dve.wait_ge(gate_done, 2)
                    v.tensor_tensor(o, o, GT[:, 4 + h, :], MUL).then_inc(op_src, 1)
                if h >= 1:
                    operand_lo(12 + h - 1, KQ[:, h - 1, 1, :], XA[:, 3 + h, 1, :], XA[:, 3 + h, 0, :])

            def after_residual(k):
                operand_lo(16 + k, RES[:, k, :], XB[:, k, 1, :], XB[:, k, 0, :], vec("mlp_norm_w", k))
                accumulate(1, k, SQ2[:, k % 2, :])

            for k in range(KT):
                tile_done(U2 + k)
                dve.wait_ge(xt_taken, k + 1)
                v.tensor_tensor(RES[:, k, :], PS[:, (M2 + k) % 4, :], XT2[:, k % 2, :], ADD) \
                    .then_inc(bank_free, 1)
                if k >= 1:
                    after_residual(k - 1)
            dve.wait_ge(bank_free, M2 + KT)
            after_residual(KT - 1)

            dve.wait_ge(half_done, 2 * U3)
            step(v.memset(PADF[:, :, 0:3], 0.0))
            dve.wait_ge(rstd_ready, 2)
            base_steps = steps[0]
            PER = 10
            with dve.Fori(0, 11) as i:
                late[0] = i * PER
                for j in range(4):
                    dve.wait_ge(half_done, i * 8 + 2 * (U3 + j + 1))
                    x = PADF[:, j, :]
                    d = CF[:, j, :]
                    t = i * 2 + (j % 2 + FT * (j // 2))
                    w = [MCW[:, q, bass.ds(t, 1)] for q in range(3)]
                    v.tensor_tensor(x[:, 3:3 + S], PS[:, j, :], RSTD[:, :], MUL).then_inc(bank_free, 1)
                    dve.wait_ge(bank_free, i * 4 + (M3 + j + 1))
                    step(v.tensor_scalar(d, x[:, 3:3 + S], w[2], None, MUL))
                    step(v.scalar_tensor_tensor(out=d, in0=x[:, 2:2 + S], scalar=w[1], in1=d,
                                                op0=MUL, op1=ADD))
                    ins = v.scalar_tensor_tensor(out=d, in0=x[:, 1:1 + S], scalar=w[0], in1=d,
                                                 op0=MUL, op1=ADD)
                    if j < 2:
                        ins.then_inc(ff_conv, 1)
                    else:
                        step(ins)
                        dve.wait_ge(ff_silu, i * 2 + (j - 1))
                        v.tensor_tensor(PRODF[:, j - 2, :], CF[:, j - 2, :], d, MUL).then_inc(ff_prod, 1)
                for j in range(2):
                    dve.wait_ge(ff_hi, i * 2 + (j + 1))
                    act_hi, act_lo = (ACTS[:, bass.ds(i * 2 + j, 1), q, :].rearrange("p a s -> p (a s)")
                                      for q in range(2))
                    v.tensor_tensor(act_lo, PRODF[:, j, :], f32(act_hi), SUB).then_inc(ff_lo, 1)
            assert steps[0] - base_steps == PER
            late[0] = None
            steps[0] = base_steps + 11 * PER

            for k in range(KT):
                tile_done(U4 + 6 * (k // 2) + 4 + k % 2)
                v.tensor_tensor(RES[:, k, :], PS[:, (M4 + k) % 4, :], RES[:, k, :], ADD).then_inc(bank_free, 1)
                if k >= 1:
                    accumulate(2, k - 1, SQ4B[:, (k - 1) % 2, :])
            accumulate(2, KT - 1, SQ4B[:, (KT - 1) % 2, :])
            dve.wait_ge(rstd_ready, 3)
            for k in range(KT + 1):
                if k < KT:
                    v.scalar_tensor_tensor(out=RES[:, k, :], in0=RES[:, k, :], scalar=vec("final_norm_w", k),
                                           in1=RSTD[:, :], op0=MUL, op1=MUL).then_inc(op_src, 1)
                if k >= 1:
                    dve.wait_ge(op_src, 16 + k)
                    operand_lo(24 + k - 1, RES[:, k - 1, :], XA[:, k - 1, 1, :], XA[:, k - 1, 0, :],
                               vec("pre0", k - 1))
                    accumulate(3, k - 1, SQ3[:, (k - 1) % 2, :])

            step(v.memset(UPD[:, :, 0:16], 0.0))

            def scores(j):
                b, kv = j // 2, j % 2
                lo = P if b == 0 else 0
                sb = SB[:, j % 2, :, lo:256]
                dve.wait_ge(sc_filled, j + 1)
                step(v.scalar_tensor_tensor(out=sb, in0=PS[:, 4:6, :].rearrange("p a (t k) -> p (a t) k", t=2)
                                            [:, :, lo:256], scalar=HD2 ** -0.5,
                                            in1=ALI[:, 4 * kv:4 * kv + 4, lo:256], op0=MUL, op1=ADD))
                step(v.tensor_reduce(AS[:, 0, 0:4], sb, AX.X, ALU.max))
                sink = SINK[:, 4 * kv:4 * kv + 4]
                step(v.tensor_tensor(AS[:, 0, 0:4], AS[:, 0, 0:4], sink, ALU.max))
                step(v.tensor_tensor(AS[:, 3, 0:4], sink, AS[:, 0, 0:4], SUB))
                v.tensor_scalar(AS[:, 1, 0:4], AS[:, 0, 0:4], -1.0, None, MUL).then_inc(sc_ready, 1)
                dve.wait_ge(p_exp, 5 * (j + 1))
                step(v.tensor_tensor(AS[:, 4, 0:4], AS[:, 2, 0:4], AS[:, 3, 0:4], ADD))
                step(v.reciprocal(AS[:, 4, 0:4], AS[:, 4, 0:4]))
                v.tensor_tensor(sb, sb, AS[:, 4, 0:4].unsqueeze(2).broadcast_to([P, 4, 256 - lo]), MUL) \
                    .then_inc(p_ready, 1)

            def pool(g):
                src = UPD[:, 0, :]
                for i in range(g + 1):
                    dst = UPD[:, 1 + i % 2, :]
                    sh = 1 << i
                    step(v.tensor_tensor(dst[:, 16:], src[:, 16:], src[:, 16 - sh:16 + S - sh], ADD))
                    src = dst
                step(v.scalar_tensor_tensor(out=PL[:, g, :], in0=src[:, 16:], scalar=0.5 ** (g + 1),
                                            in1=UPD[:, 0, 16:], op0=MUL, op1=SUB))
                step(v.tensor_tensor(src[:, 16:32], src[:, 16:32], ITAB[:, g, :], MUL))
                v.tensor_tensor(PL[:, g, 0:16], src[:, 16:32], UPD[:, 0, 16:32], SUB).then_inc(pool_ready, 1)

            dve.wait_ge(ali_in, 64)
            for u in range(U5, U6):
                n = u - U5
                j = n - 6
                if n == 1:
                    dve.wait_ge(abt_filled, 2)
                    v.tensor_copy(RCOL[:, :], PS[:, 6, 0:NB]).then_inc(rcol_ready, 1)
                if 0 <= j < 8:
                    scores(j)
                tile_done(u)
                if n == 0:
                    dve.wait_ge(rstd_ready, 4)
                bank = PS[:, (M5 + n) % 4, :]
                if n == 5:
                    dve.wait_ge(rcol_ready, 2)
                    v.tensor_tensor(VS[:, :, :], bank.rearrange("p (b d) -> p b d", b=NB),
                                    RCOL[:, :].unsqueeze(2).broadcast_to([P, NB, P]), MUL) \
                        .then_inc(bank_free, 1)
                else:
                    dst = (QS[:, n, :] if n < 4 else KS[:, :] if n == 4 else GA[:, n - 6, :] if n < 10 else
                           UPD[:, 0, 16:] if n < 14 else GB[:, n - 14, :])
                    v.tensor_tensor(dst, bank, RSTD[:, :], MUL).then_inc(bank_free, 1)
                if 10 <= n < 14:
                    dve.wait_ge(bank_free, M5 + n + 1)
                    pool(n - 10)
                if n == 16:
                    dve.wait_ge(ov_taken, 8)
                    dve.wait_ge(gate_done, 3)
                    for t in range(4):
                        v.tensor_tensor(MIXF[:, t, :], MIXF[:, t, :], GA[:, t, :], MUL).then_inc(op_src, 1)
                    for t in range(4):
                        operand_lo(32 + t, MIXF[:, t, :], XB[:, t, 1, :], XB[:, t, 0, :])
            dve.wait_ge(py_taken, 4)
            for g in range(5):
                if g < 4:
                    dve.wait_ge(gate_done, 4 + g)
                    v.tensor_tensor(MIXF[:, 4 + g, :], PL[:, g, :], GB[:, g, :], MUL).then_inc(op_src, 1)
                if g >= 1:
                    operand_lo(36 + g - 1, MIXF[:, 3 + g, :], XB[:, 3 + g, 1, :], XB[:, 3 + g, 0, :])

            def post(st, name, f, yt, last):
                dve.wait_ge(rstd_ready, st + 1)
                for k in range(KT + 1):
                    if k < KT:
                        step(v.scalar_tensor_tensor(out=yt[:, k % 2, :], in0=Y[:, k, :], scalar=vec(name, k),
                                                    in1=RSTD[:, :], op0=MUL, op1=MUL))
                        v.tensor_tensor(RES[:, k, :], RES[:, k, :], yt[:, k % 2, :], ADD).then_inc(op_src, 1)
                    if k >= 1 and not last:
                        q = k - 1
                        dve.wait_ge(op_src, 32 + k)
                        operand_lo(f + q, RES[:, q, :], XA[:, q, 1, :], XA[:, q, 0, :], vec("pre1", q))
                        accumulate(5, q, SQ3[:, q % 2, :])

            for k in range(KT):
                tile_done(U6 + k)
                v.tensor_copy(Y[:, k, :], PS[:, (M6 + k) % 4, :]).then_inc(bank_free, 1)
                if k >= 1:
                    accumulate(4, k - 1, SQ3[:, (k - 1) % 2, :])
            accumulate(4, KT - 1, SQ3[:, (KT - 1) % 2, :])
            post(4, "post0", 40, YT, False)

            step(v.memset(GLU[:, :, 0:CK - 1], 0.0))
            tap_at = [0]

            def taps(n, tiles):
                for _ in range(n):
                    k, i = divmod(tap_at[0], CK)
                    if k >= tiles:
                        return
                    x = GLU[:, k, i:i + S]
                    w = DCW[:, i, k:k + 1]
                    if i == 0:
                        step(v.tensor_scalar(CV[:, k, :], x, w, vec("dw_b", k), MUL, ADD))
                    else:
                        step(v.scalar_tensor_tensor(out=CV[:, k, :], in0=x, scalar=w, in1=CV[:, k, :],
                                                    op0=MUL, op1=ADD))
                    tap_at[0] += 1

            for u in range(U7, U8):
                n = u - U7
                tile_done(u)
                if n == 0:
                    dve.wait_ge(rstd_ready, 6)
                bank = PS[:, (M7 + n) % 4, :]
                dst = ABUF[:, n % 4, :] if n < 16 else GT3[:, n - 16, :]
                if n < 16 and n % 4 >= 2:
                    v.tensor_tensor(dst, bank, RSTD[:, :], MUL).then_inc(bank_free, 1)
                    dve.wait_ge(bank_free, M7 + n + 1)
                    k = 2 * (n // 4) + n % 4 - 2
                    dve.wait_ge(sig_done, k + 1)
                    step(v.tensor_tensor(GLU[:, k, CK - 1:], ABUF[:, n % 4 - 2, :], dst, MUL))
                else:
                    v.tensor_tensor(dst, bank, RSTD[:, :], MUL).then_inc(bank_free, 1)
                taps(7, 2 * (n // 4) if n < 16 else KT)
            taps(CK * KT, KT)
            for k in range(KT):
                if k == 0:
                    step(v.tensor_copy(ACC[:, :], CV[:, 0, :]))
                elif k < KT - 1:
                    step(v.tensor_tensor(ACC[:, :], ACC[:, :], CV[:, k, :], ADD))
                else:
                    v.tensor_tensor(ACC[:, :], ACC[:, :], CV[:, k, :], ADD).then_inc(ln_sum, 1)
            dve.wait_ge(cm_filled, 1)
            for k in range(KT):
                v.scalar_tensor_tensor(out=CV[:, k, :], in0=PS[:, 7, :], scalar=-1.0 / D, in1=CV[:, k, :],
                                       op0=MUL, op1=ADD).then_inc(cm_taken, 1)
                if k >= 1:
                    accumulate(6, k - 1, CT[:, (k - 1) % 2, :])
            accumulate(6, KT - 1, CT[:, 1, :])
            dve.wait_ge(rstd_ready, 7)
            dve.wait_ge(gate_done, 16 - 1)
            for k in range(KT + 2):
                if k < KT:
                    v.scalar_tensor_tensor(out=CV[:, k, :], in0=CV[:, k, :], scalar=vec("ln_g", k),
                                           in1=RSTD[:, :], op0=MUL, op1=MUL).then_inc(ln_in, 1)
                if 1 <= k <= KT:
                    dve.wait_ge(ln_done, k)
                    v.tensor_tensor(CV[:, k - 1, :], CV[:, k - 1, :], GT3[:, k - 1, :], MUL) \
                        .then_inc(op_src, 1)
                if k >= 2:
                    operand_lo(48 + k - 2, CV[:, k - 2, :], XB[:, k - 2, 1, :], XB[:, k - 2, 0, :])

            for k in range(KT):
                tile_done(U8 + k)
                v.tensor_copy(Y[:, k, :], PS[:, (M8 + k) % 4, :]).then_inc(bank_free, 1)
                if k >= 1:
                    accumulate(7, k - 1, CT[:, (k - 1) % 2, :])
            accumulate(7, KT - 1, CT[:, 1, :])
            post(7, "post1", 0, ABUF, True)

        @block.tensor
        def _(pe):
            mm, tr = nc.tensor.matmul, nc.tensor.transpose

            def operand(f):
                pe.wait_ge(op_hi, f + 1)
                pe.wait_ge(op_lo, f + 1)

            def three(out, w_hi_, w_lo_, x_hi_, x_lo_, first, last):
                mm(out, w_hi_, x_hi_, start=first, stop=False)
                mm(out, w_hi_, x_lo_, start=False, stop=False)
                return mm(out, w_lo_, x_hi_, start=False, stop=last)

            def half_unit(n, out, X, k0, kn, first, last, fill=None, later=None):
                for s_ in (w_hi, w_lo):
                    pe.wait_ge(s_, n + 1 if later is None else later + (n + 1))
                for k in range(kn):
                    if fill is not None:
                        operand(8 * fill + k0 + k)
                    ins = three(out, WH[:, n % 4, k, :], WL[:, n % 4, k, :],
                                X[:, k0 + k, 0, :], X[:, k0 + k, 1, :],
                                first and k == 0, last and k == kn - 1)
                ins.then_inc(half_done, 1)

            def unit(u, m, X, fill=None, later=None, mlater=None):
                if m >= 4:
                    pe.wait_ge(bank_free, m - 3 if mlater is None else mlater + (m - 3))
                out = PS[:, m % 4, :]
                half_unit(2 * u, out, X, 0, 4, True, False, fill, later)
                half_unit(2 * u + 1, out, X, 4, 4, False, True, fill, later)

            def unit_by_token(u, m, X):
                pe.wait_ge(bank_free, m - 3)
                for s_ in (w_hi, w_lo):
                    pe.wait_ge(s_, 2 * u + 2)
                for b in range(NB):
                    out = PS[:, m % 4, b * P:(b + 1) * P]
                    for k in range(KT):
                        r = (2 * u + k // 4) % 4
                        xh, xl = (X[:, k, q, b * P:(b + 1) * P] for q in range(2))
                        ins = three(out, xh, xl, WH[:, r, k % 4, :], WL[:, r, k % 4, :], k == 0, k == KT - 1)
                        if b == NB - 1 and k % 4 == 3:
                            ins.then_inc(half_done, 1)

            def stat(st):
                pe.wait_ge(acc_done, 8 * (st + 1))
                mm(PS[:, 7, :], ONES[:, :], ACC[:, :], start=True, stop=True).then_inc(stat_filled, 1)

            def rstd_columns(n):
                pe.wait_ge(rstd_ready, n)
                for b in range(NB):
                    ins = mm(PS[:, 6, b:b + 1], RSTD[0:1, b * P:(b + 1) * P], ONES[0:1, 0:1],
                             start=True, stop=True)
                return ins

            pe.wait_ge(c_in, 16 * 18)
            pe.wait_ge(ones_ready, 5)
            c = 0
            for slot, n, bank in ((0, NVEC, 0), (1, 48, 0), (2, 66, 0), (5, 66, 0), (3, 124, 1), (4, 124, 1)):
                if slot == 3:
                    c = 0
                ins = tr(PS[:, bank, c:c + n], ROWS[0:n, slot, :], IDENT[0:n, 0:n])
                c += n
            ins.then_inc(par_filled, 1)
            pe.wait_ge(x_in, 16 * NB)
            for k in range(KT):
                if k >= 4:
                    pe.wait_ge(op_src, k - 3)
                for b in range(NB):
                    ins = tr(PS[:, 4 + k % 4, b * P:(b + 1) * P], XTOK[:, b, k * P:(k + 1) * P], IDENT[:, :])
                ins.then_inc(xt_filled, 1)
            pe.wait_ge(par_ready, 4)

            def ret_head(h):
                if h >= 1:
                    pe.wait_ge(ro_ready, h)
                if h == 0 or h == 2:
                    pe.wait_ge(rot_ready, 3 if h == 0 else 7)
                if h == 1 or h == 3:
                    pe.wait_ge(rot_ready, 4 if h == 1 else 8)

                def score(jb):
                    if 4 * h + jb >= 2:
                        pe.wait_ge(rs_ready, 4 * h + jb - 1)
                    mm(PS[:, 4 + jb % 2, 0:S - jb * P], RK[:, h % 2, jb * P:(jb + 1) * P],
                       RQ[:, h % 2, jb * P:], start=True, stop=True).then_inc(rs_filled, 1)

                def value(jb):
                    pe.wait_ge(rs_ready, 4 * h + jb + 1)
                    ins = mm(PS[:, 6, jb * P:], RV[:, h, jb, :], RS[:, jb % 2, 0:S - jb * P],
                             start=(jb == 0), stop=(jb == NB - 1))
                    if jb == NB - 1:
                        ins.then_inc(ro_filled, 1)

                score(0)
                for jb in range(1, NB):
                    score(jb)
                    value(jb - 1)
                value(NB - 1)

            def level(l):
                s = 2 << l
                def half(ap, two):
                    return ap.rearrange("p (b two s) -> p b two s", two=2, s=s)[:, :, two, :]
                for c in range(NB):
                    if l == 0 and c == 0:
                        pe.wait_ge(t2_ready, 1)
                        pe.wait_ge(tt_ready, 1)
                    if l > 0:
                        pe.wait_ge(upd_done, 4 * (l - 1) + c + 1)
                    for h in range(H):
                        a_ = 4 * c + h
                        ins = mm(PS[:, 4 + c, h * 64:(h + 1) * 64], M[:, a_, :], half(TT[:, a_, :], 1),
                                 start=True, stop=True)
                    ins.then_inc(xp_filled, 1)
                for c in range(NB):
                    pe.wait_ge(xs_ready, 4 * l + c + 1)
                    pe.wait_ge(xz_ready, 4 * l + c + 1)
                    for h in range(H):
                        a_ = 4 * c + h
                        ins = mm(PS[:, 4 + c, 256 + h * 64:256 + (h + 1) * 64], T[:, a_, :],
                                 half(XZ[:, c, h, :], 1), start=True, stop=True)
                        if l < 5:
                            ins = mm(PS[:, 4 + c, h * 64:(h + 1) * 64], XZ[:, c, h, :],
                                     half(T[:, a_, :], 0), start=True, stop=True)
                    ins.then_inc(txp_filled, 1)

            def by_token(c):
                if c >= 1:
                    pe.wait_ge(tokk_ready, c)
                    pe.wait_ge(tokv_ready, 4 * c)
                for j, bank in ((0, 4), (1, 5)):
                    for h in range(H):
                        src = KQ[:, h, 0, c * P:(c + 1) * P] if j == 0 else V[:, h, c * P:(c + 1) * P]
                        ins = tr(PS[:, bank, h * P:(h + 1) * P], src, IDENT[:, :])
                    ins.then_inc(tok_filled, 1)

            def weights_t(c):
                pe.wait_ge(tokk_ready, c + 1)
                pe.wait_ge(o_ready, c)
                for h in range(H):
                    ins = mm(PS[:, 6, h * P:(h + 1) * P], KB[:, h, :], TT[:, 4 * c + h, :], start=True, stop=True)
                ins.then_inc(nw_filled, 1)

            def new_values(c):
                pe.wait_ge(tokv_ready, 4 * (c + 1))
                if c >= 1:
                    pe.wait_ge(nw_ready, c)
                    pe.wait_ge(s_ready, c)
                for h in range(H):
                    o = PS[:, 7, h * P:(h + 1) * P]
                    ins = mm(o, TT[:, 4 * c + h, :], VB[:, h, :], start=True, stop=(c == 0))
                    if c >= 1:
                        ins = mm(o, NW[:, h, :], ST8[:, h, :], start=False, stop=True)
                ins.then_inc(u_filled, 1)

            def out_and_state(c):
                pe.wait_ge(u_ready, c + 1)
                if c >= 1:
                    pe.wait_ge(qd_ready, c)
                    pe.wait_ge(nw_ready, c)
                else:
                    pe.wait_ge(ro_ready, 4)
                for h in range(H):
                    o = PS[:, 6, h * P:(h + 1) * P]
                    ins = mm(o, UU[:, h, :], QKT[:, 4 * c + h, :], start=True, stop=(c == 0))
                    if c >= 1:
                        ins = mm(o, ST8[:, h, :], QD[:, h, :], start=False, stop=True)
                ins.then_inc(so_filled, 1)
                if c < NB - 1:
                    if c == 0:
                        pe.wait_ge(tokk_ready, 1)
                    for h in range(H):
                        ins = mm(PS[:, 7, h * P:(h + 1) * P], KD[:, h, :], UU[:, h, :], start=True, stop=True)
                    ins.then_inc(so_filled, 1)

            def ret_ssq(r):
                pe.wait_ge(rsq_ready, 1)
                pe.wait_ge(tokk_ready, r + 1)
                pe.wait_ge(tokv_ready, 4 * (r + 1))
                for h in range(2):
                    ins = mm(PS[:, 4 + h, :], ONES[:, :], RR[:, 2 * r + h, :], start=True, stop=True)
                ins.then_inc(rssq_filled, 1)

            for u in range(U1, U2):
                if 12 <= u < 16:
                    unit_by_token(u, u, XA)
                else:
                    unit(u, u, XA, fill=0 if u == 0 else None)
                if u == 0:
                    stat(0)
                if u == 3:
                    pe.wait_ge(ab_split, 2)
                    pe.wait_ge(rstd_ready, 1)
                    for k in range(KT):
                        ins = three(PS[0:8, 7, :], ABH[:, k, :], ABL[:, k, :], XA[:, k, 0, :], XA[:, k, 1, :],
                                    k == 0, k == KT - 1)
                    ins.then_inc(ab_filled, 1)
                if u == 4:
                    pe.wait_ge(ab_rows, 1)
                    rstd_columns(1)
                    for c in range(NB):
                        ins = tr(PS[:, 7, 8 * c:8 * c + 8], AB[:, c * P:(c + 1) * P], IDENT[0:8, 0:8])
                    ins.then_inc(abt_filled, 1)
                if u == 12 or u == 13:
                    pe.wait_ge(sqk, u - 11)
                    pe.wait_ge(sp_in, 1)
                    pe.wait_ge(rcol_ready, 1)
                    if u == 13:
                        pe.wait_ge(r4_ready, 1)
                        pe.wait_ge(gu_ready, 1)
                        mm(PS[:, 4, 0:16], UPPER, GG, start=True, stop=True).then_inc(gc_filled, 1)
                    for h in (1, 2, 3, 0):
                        if h == 0 and u == 13:
                            pe.wait_ge(gc_ready, 1)
                        ins = mm(PS[:, 4 + h, :], ONES[:, :], SQ4[:, h, :], start=True, stop=True)
                    ins.then_inc(ssq_filled, 1)
                if u == 14:
                    pe.wait_ge(r4_ready, 2)
                    for c in range(NB):
                        ins = mm(PS[:, 4 + c, :], ONES[:, :],
                                 T[:, 4 * c:4 * c + 4, :].rearrange("p h i -> p (h i)"), start=True, stop=True)
                    ins.then_inc(gcb_filled, 1)
                if u == 15 or u == 16:
                    if u == 15:
                        pe.wait_ge(x1_ready, 1)
                        pe.wait_ge(kq_normed, 2)
                    else:
                        pe.wait_ge(m_ready, 1)
                    for c in range(NB):
                        for h in range(H):
                            ins = mm(PS[:, 4 + c, h * P:(h + 1) * P], KQ[:, h, 0, c * P:(c + 1) * P],
                                     KQ[:, h, u - 15, c * P:(c + 1) * P], start=True, stop=True)
                    ins.then_inc(g_filled if u == 15 else qk_filled, 1)
                if u == 17:
                    pe.wait_ge(qkt_ready, 1)
                    pe.wait_ge(t2_ready, 1)
                    for a_ in range(16):
                        ins = tr(PS[:, 4 + a_ // 4, (a_ % 4) * P:(a_ % 4 + 1) * P], T[:, a_, :], IDENT[:, :])
                    ins.then_inc(tt_filled, 1)
                if 18 <= u <= 23:
                    heads = sum(g < u for g in RET_GAP)
                    if heads:
                        pe.wait_ge(ro_ready, heads)
                        pe.wait_ge(rs_ready, 4 * heads)
                    level(u - 18)
                if u in RET_GAP:
                    pe.wait_ge(upd_done, 4 * min(u - 17, 6))
                    ret_head(RET_GAP.index(u))
                if u == 24:
                    pe.wait_ge(rs_ready, 16)
                    by_token(0)
                if u == 25:
                    ret_ssq(0)
                if u == 26:
                    new_values(0)
                    pe.wait_ge(rr_ready, 1)
                    by_token(1)
                    out_and_state(0)
                if u == 27:
                    weights_t(1)
                    ret_ssq(1)
                if u == 28:
                    new_values(1)
                    pe.wait_ge(rr_ready, 2)
                    by_token(2)
                    out_and_state(1)
                if u == 29:
                    weights_t(2)
                if u == 30:
                    new_values(2)
                    by_token(3)
                    out_and_state(2)
                if u == 31:
                    weights_t(3)
                    new_values(3)
                    out_and_state(3)
            pe.wait_ge(rsq_ready, 2)
            pe.wait_ge(tokk_ready, 4)
            pe.wait_ge(tokv_ready, 16)
            pe.wait_ge(o_ready, 4)
            for h in range(H):
                ins = mm(PS[:, 4 + h, :], ONES[:, :], RR[:, h, :], start=True, stop=True)
            ins.then_inc(rssq_filled, 1)

            for k in range(KT):
                unit(U2 + k, M2 + k, XA, fill=1 if k == 0 else None)
                if k == 0:
                    pe.wait_ge(x2_in, 16 * NB)
                    pe.wait_ge(rr_ready, 3)
                if k >= 4:
                    pe.wait_ge(xt_taken, k - 3)
                for b in range(NB):
                    ins = tr(PS[:, 4 + k % 4, b * P:(b + 1) * P], XTOK2[:, b, k * P:(k + 1) * P], IDENT[:, :])
                ins.then_inc(xt_filled, 1)
            pe.wait_ge(xt_taken, KT)
            stat(1)
            operand(23)
            with pe.Fori(0, 11) as i:
                for j in range(4):
                    unit(U3 + j, M3 + j, XB, later=i * 8, mlater=i * 4)
            pe.wait_ge(ff_hi, FT)
            pe.wait_ge(ff_lo, FT)
            with pe.Fori(0, 2) as i:
                for j in range(12):
                    g, t, o = j // 2 % 3, j % 2, j // 6
                    m = M4 + 2 * o + t
                    if g == 0:
                        pe.wait_ge(bank_free, i * 4 + (m - 3))
                    kn = 4 if g < 2 else 3
                    for hf in range(2):
                        half_unit(2 * (U4 + j) + hf, PS[:, m % 4, :], ACTS, 8 * g + kn * hf, kn,
                                  g == 0 and hf == 0, g == 2 and hf == 1, later=i * 24)
            stat(2)

            def probs_t(j):
                pe.wait_ge(p_ready, j + 1)
                if j >= 1:
                    pe.wait_ge(ov_taken, j)
                for t in range(4):
                    for w in range(1 if j < 2 else 0, 2):
                        ins = tr(PS[:, 6 + t // 2, (2 * (t % 2) + w) * P:(2 * (t % 2) + w + 1) * P],
                                 SB[:, j % 2, t, w * P:(w + 1) * P], IDENT[:, :])
                ins.then_inc(pt_filled, 1)

            def scores(j):
                b, kv = j // 2, j % 2
                r = slice(kv * HD2, (kv + 1) * HD2)
                if j >= 1:
                    pe.wait_ge(sc_ready, j)
                for t in range(4):
                    lo = 0 if b else P
                    ins = mm(PS[:, 4 + t // 2, (t % 2) * 256 + lo:(t % 2 + 1) * 256],
                             QS[r, t, b * P:(b + 1) * P], KS[r, (b - 1) * P + lo:(b + 1) * P],
                             start=True, stop=True)
                ins.then_inc(sc_filled, 1)

            def values(j):
                b, kv = j // 2, j % 2
                r = slice(kv * HD2, (kv + 1) * HD2)
                pe.wait_ge(pt_ready, j + 1)
                for w in range(0 if b else 1, 2):
                    ins = mm(PS[r, 6, :], VS[:, b - 1 + w, r], PTS[:, :, w, :],
                             start=(w == (0 if b else 1)), stop=(w == 1))
                ins.then_inc(ov_filled, 1)

            for u in range(U5, U6):
                n = u - U5
                if n == 5:
                    unit_by_token(u, M5 + n, XA)
                else:
                    unit(u, M5 + n, XA, fill=3 if n == 0 else None)
                if n == 0:
                    stat(3)
                if n == 1:
                    rstd_columns(4).then_inc(abt_filled, 1)
                j = n - 6
                if j == 0:
                    pe.wait_ge(bank_free, M5 + 6)
                    pe.wait_ge(rcol_ready, 2)
                if 1 <= j <= 8:
                    probs_t(j - 1)
                if 0 <= j < 8:
                    scores(j)
                if 1 <= j <= 8:
                    values(j - 1)
                if j == 9:
                    pe.wait_ge(ali_in, 64)
                    pe.wait_ge(pool_ready, 4)
                    pe.wait_ge(ov_taken, 8)
                    for g in range(4):
                        ins = mm(PS[:, 4 + g, :], PW[:, g, :], PL[:, g, :], start=True, stop=True)
                    ins.then_inc(py_filled, 1)
            for k in range(KT):
                unit(U6 + k, M6 + k, XB, fill=4 if k == 0 else None)
            pe.wait_ge(py_taken, 4)
            stat(4)
            for n in range(24):
                unit(U7 + n, M7 + n, XA, fill=5 if n == 0 else None)
                if n == 0:
                    stat(5)
            pe.wait_ge(ln_sum, 1)
            mm(PS[:, 7, :], ONES[:, :], ACC[:, :], start=True, stop=True).then_inc(cm_filled, 1)
            stat(6)
            for k in range(KT):
                unit(U8 + k, M8 + k, XB, fill=6 if k == 0 else None)
            stat(7)
            for k in range(KT):
                pe.wait_ge(op_src, 48 + k + 1)
                if k >= 4:
                    pe.wait_ge(ot_ready, k - 3)
                if k == 3:
                    pe.wait_ge(rstd_ready, 8)
                for b in range(NB):
                    ins = tr(PS[:, 4 + k % 4, b * P:(b + 1) * P], RES[:, k, b * P:(b + 1) * P], IDENT[:, :])
                ins.then_inc(ot_filled, 1)


def constants():
    f = np.float32
    i, j = np.arange(P)[:, None], np.arange(P)[None, :]
    masks = [(i <= j).astype(f), (j < i).astype(f), ((i % 2 == 1) & (j == i - 1)).astype(f)]
    for level in range(6):
        s = 2 << level
        second = np.array([c for c in range(P) if c // s % 2 == 1])[None, :]
        masks.append(((i // s % 2 == 0) & (i // (2 * s) == second // (2 * s))).astype(f))
    angle = f(1.0) / f(10000.0) ** np.linspace(0.0, 1.0, P // 2, dtype=f)
    phase = (np.arange(S, dtype=f)[None, :] * np.repeat(angle, 2)[:, None]).astype(f).astype(np.float64)
    sign = np.where(np.arange(P) % 2 == 0, -1.0, 1.0)[:, None]
    log_gamma = np.log(1.0 - 2.0 ** (-5.0 - np.arange(H)))
    off = np.arange(S)[None, :] - np.arange(P)[:, None]
    decay = np.where(off >= 0, np.exp(np.maximum(off, 0)[None] * log_gamma[:, None, None]), 0.0) * P ** -0.5
    dist = np.arange(P)[:, None] + P - np.arange(256)[None, :]
    slopes = 2.0 ** (-np.arange(1, QH + 1, dtype=np.float64))
    ok = (dist >= 0) & (dist < P)
    alibi = np.where(ok[:, None, :], -slopes[None, :, None] * dist[:, None, :], NEG)
    cnt = np.minimum(np.arange(16)[None, :] + 1, np.array([2, 4, 8, 16])[:, None])
    return {
        "ident": np.eye(P, dtype=f),
        "masks": np.concatenate(masks, 1),
        "cos_sin": np.stack([np.cos(phase), np.sin(phase) * sign], 1).astype(f),
        "ret_decay": decay.transpose(1, 0, 2).astype(f),
        "alibi": alibi.astype(f),
        "inv_cnt": np.broadcast_to((1.0 / cnt).astype(f)[None], (P, 4, 16)).copy(),
    }


_INS = ["x", "attn_norm_w", "w_in", "gdn_conv_w", "gdn_a_log", "gdn_dt_bias", "gdn_norm_w", "w_out",
        "mlp_norm_w", "w_up", "mlp_conv_w", "w_down", "final_norm_w", "pre_norm_2", "post_norm_2",
        "a_w_in_2", "a_sinks_2", "b_pool_w_2", "b_pool_scale_2", "ab_w_out_2", "c_w_in_2", "c_dw_w_2",
        "c_dw_b_2", "c_ln_g_2", "c_ln_b_2", "c_w_out_2"]


def kernel(**inputs):
    import concourse.bacc as bacc
    from concourse.bass_utils import run_bass_kernel_spmd as run

    nc = bacc.Bacc("TRN2", target_bir_lowering=False, num_devices=1)
    arrays, a, const = {}, {}, {}
    for name in _INS:
        x = np.ascontiguousarray(inputs[name])
        arrays["in_" + name] = x
        a[name] = nc.dram_tensor("in_" + name, x.shape, F32, kind="ExternalInput").ap()
    for name, x in constants().items():
        arrays["const_" + name] = x
        const[name] = nc.dram_tensor("const_" + name, x.shape, F32, kind="ExternalInput").ap()
    out = nc.dram_tensor("result", (1, S, D), F32, kind="ExternalOutput").ap()
    build(nc, a, const, out)
    r = run(nc, [arrays], core_ids=[0])
    return r.results[0]["result"]
```

```python
import math
from contextlib import ExitStack

import numpy as np

import concourse.bass as bass
from concourse import mybir

P = 128
S = 512
D = 1024
KT = D // P
NB = S // P
H = 4
GW = H * P
IN_COLS = 8 * GW + 2 * H
DFF = 2816
FT = DFF // P
EPS = 1e-6
LN_EXP_SET = 6
SILU_SET = 18
EVEN_IN = 2304
QH = 8
HD2 = 64
CK = 31
NEG = -1e30

F32 = mybir.dt.float32
F32R = mybir.dt.float32r
ACT = mybir.ActivationFunctionType
ALU = mybir.AluOpType
AX = mybir.AxisListType
MUL, ADD, SUB = ALU.mult, ALU.add, ALU.subtract

VECS = [("attn_norm_w", 8), ("mlp_norm_w", 8), ("final_norm_w", 8), ("pre0", 8), ("pre1", 8),
        ("post0", 8), ("post1", 8), ("pool_scale", 4), ("dw_b", 8), ("ln_g", 8), ("ln_b", 8),
        ("gdn_norm_w", 1)]
VEC_AT, _n = {}, 0
for _name, _rows in VECS:
    VEC_AT[_name] = _n
    _n += _rows
NVEC = _n

U1, U2, U3, U4, U5, U6, U7, U8 = 0, 32, 40, 84, 108, 126, 134, 158
UNITS = 166
M1, M2, M3, M4, M5, M6, M7, M8 = 0, 32, 40, 84, 92, 110, 118, 142
PAIRS = UNITS // 2
FILL = {1: 0, 2: 1, 3: 2, 5: 3, 6: 4, 7: 5, 8: 6}
PE_TAPS = [6, 6, 7, 7, 7, 7, 8, 8]
REST_BANK = [4, 5, 7, 6]
RET_GAP = [19, 20, 23, 24]


QUADS = (U2, U5, U6, U7)
WIDE = (12, U8, U8 + 4)


def unit_half(n):
    for q in QUADS:
        if 0 <= n - 2 * q < 8:
            return q + (n - 2 * q) % 4, (n - 2 * q) // 4
    return n // 2, n % 2


def halves_when_done(u):
    for q in QUADS:
        if 0 <= u - q < 4:
            return 2 * q + 5 + u - q
    for q in WIDE:
        if 0 <= u - q < 4:
            return 2 * q + 8
    return 2 * u + 2


def wide(u):
    return any(0 <= u - q < 4 for q in WIDE)


def split_when_free(p):
    return 4 * p - 2 if 2 * (p - 2) in QUADS else 4 * (p - 1)


def loads_before(p):
    n = 0
    for q in range(p % 2, p + 1, 2):
        n += 3 if U6 <= 2 * q < U7 else 2
    return n


def acc_round(st):
    return st - (st > 6)


def build(nc, a, const, out):
    ctx = ExitStack()
    with ctx:
        base = (nc.sbuf_base + 31) // 32 * 32

        def at(name, shape, dt, off):
            return nc.alloc_sbuf_tensor_at(name, shape, dt, offset=base + off)

        def sem(name):
            return ctx.enter_context(nc.semaphore(name))

        RAW = at("raw", [P, 2, KT, 256], F32, 0)
        WH = at("w_hi", [P, 4, 4, P], F32R, 16384)
        WL = at("w_lo", [P, 4, 4, P], F32R, 24576)
        XA = at("x_a", [P, KT, 2, S], F32R, 32768)
        AR = 65536
        G = 204800
        IDENT = at("ident", [P, P], F32, G)
        ONES = at("ones", [P, P], F32, G + 512)
        RSTD = at("rstd", [P, S], F32, G + 1024)
        ACC = at("acc", [P, S], F32, G + 3072)
        VEC = at("vec", [P, NVEC], F32, G + 5120)
        GCW = at("gdn_conv", [P, 4, 12], F32, G + 5120 + 352)
        MCW = at("mlp_conv", [P, 3, 44], F32, G + 5664)
        DCW = at("dw_conv", [P, CK, KT], F32, G + 6208)
        RCOL = at("rstd_col", [P, NB], F32, G + 7200)
        CB = at("const_bias", [P, 4], F32, G + 7232)

        KQ = at("kq", [P, H, 2, S], F32, AR)
        ROWS = at("rows", [P, 6, P], F32, AR)
        V = at("v", [P, H, S], F32, AR + 16384)
        RV = at("ret_v", [P, H, NB, P], F32, AR + 24576)
        XTOK = at("x_tok", [P, NB, D], F32, AR + 32768)
        GT = at("gates", [P, 8, S], F32, AR + 32768)
        M = at("m", [P, NB * H, P], F32, AR + 32768)
        T = at("t", [P, NB * H, P], F32, AR + 40960)
        TT = at("tt", [P, NB * H, P], F32, AR + 49152)
        QKT = at("qkt", [P, NB * H, P], F32, AR + 57344)
        R4 = at("r4", [P, H, S], F32, AR + 57344)
        EB = at("eb", [P, NB * H, P], F32, AR + 65536)
        SQ4 = at("sq4", [P, H, S], F32, AR + 65536)
        XZ = at("xz", [P, NB, H, P], F32, AR + 73728)
        LB = at("lb", [P, NB * H, P], F32, AR + 73728)
        RR = at("rr", [P, H, S], F32, AR + 73728)
        VB = at("vb", [P, H, P], F32, AR + 81920)
        KB = at("kb", [P, H, P], F32, AR + 83968)
        KD = at("kd", [P, H, P], F32, AR + 86016)
        NW = at("nw", [P, H, P], F32, AR + 88064)
        UU = at("uu", [P, H, P], F32, AR + 90112)
        QD = at("qd", [P, H, P], F32, AR + 92160)
        ST8 = at("state", [P, H, P], F32, AR + 94208)
        CS = at("cos_sin", [P, 2, S], F32, AR + 96256)
        DR = at("ret_decay", [P, H, S], F32, AR + 100352)
        RQ = at("rq", [P, 2, S], F32, AR + 108544)
        RK = at("rk", [P, 2, S], F32, AR + 112640)
        RS = at("ret_s", [P, 2, S], F32, AR + 116736)
        PAD = at("pad", [P, 2, S + 4], F32, AR + 120832)
        SC = at("scratch", [P, 4, S], F32, AR + 124960)
        MASK = at("masks", [P, 3 * P + 6 * 64], F32, AR + 133152)
        AB = at("ab", [8, S], F32, AR + 136224)
        ABR = at("ab_raw", [P, KT, 8], F32, AR + 138272)
        SM = at("small", [P, 12, 16], F32, G + 7264)
        ABH = at("ab_hi", [P, KT, 8], F32R, AR + 116736)
        ABL = at("ab_lo", [P, KT, 8], F32R, AR + 116736 + 256)
        ABT = SM[:, 0:2, :].rearrange("p a b -> p (a b)").rearrange("p (c e) -> p c e", e=8)
        UPPER = MASK[:, 0:P]
        LOWER = MASK[:, P:2 * P]
        PAIRM = MASK[:, 2 * P:3 * P]
        GG = SM[:, 2, :]
        BETA = SM[:, 3, :]
        GC = SM[:, 4, :]
        EGC = SM[:, 5, :]
        BEN = SM[:, 6, :]
        KDC = SM[:, 7, :]
        SPR = SM[:, 8, :]
        SPM = SM[:, 9, :]
        SPB = SM[:, 10, :]
        ALD = SM[:, 11, 0:8]

        RES = at("res", [P, KT, S], F32, AR)
        XB = at("x_b", [P, KT, 2, S], F32R, AR + 16384)
        ACTS = at("mlp_act", [P, FT, 2, S], F32R, AR + 49152)
        XTOK2 = at("x_tok2", [P, NB, D], F32, AR + 96256)
        XT2 = at("x_t2", [P, 2, S], F32, AR + 65536)
        SQ2 = at("sq2", [P, 2, S], F32, AR + 69632)
        PADF = at("pad_f", [P, 4, S + 4], F32, 32768)
        CF = at("conv_f", [P, 4, S], F32, 32768 + 8256)
        PRODF = at("prod_f", [P, 2, S], F32, 32768 + 16448)
        SQ4B = at("sq4b", [P, 2, S], F32, 32768 + 20544)

        A3 = AR + 49152
        QS = at("q_s", [P, 4, S], F32, A3)
        KS = at("k_s", [P, S], F32, A3 + 8192)
        VS = at("v_s", [P, NB, P], F32, A3 + 10240)
        GA = at("ga", [P, 4, S], F32, A3 + 12288)
        GB = at("gb", [P, 4, S], F32, A3 + 20480)
        PL = at("pooled", [P, 4, S], F32, A3 + 28672)
        ALI = at("alibi", [P, QH, 256], F32, A3 + 36864)
        SB = at("scores", [P, 2, 4, 256], F32, A3 + 45056)
        PTS = at("probs_t", [P, 4, 2, P], F32, A3 + 53248)
        MIXF = at("mix_f", [P, 8, S], F32, A3 + 57344)
        PW = at("pool_w", [P, 4, P], F32, A3 + 73728)
        UPD = at("u_pad", [P, 3, S + 16], F32, A3 + 75776)
        ITAB = at("inv_cnt", [P, 4, 16], F32, A3 + 82112)
        AS = at("att_small", [P, 8, 8], F32, A3 + 82368)
        SINK = at("sink", [P, QH], F32, A3 + 82624)
        SQ3 = at("sq3", [P, 2, S], F32, A3 + 82656)
        Y = at("y", [P, KT, S], F32, A3 + 57344)
        YT = at("y_t", [P, 2, S], F32, A3 + 75776)
        GPW = S + CK - 1
        GLU = at("glu", [P, KT, GPW], F32, A3)
        CV = at("conv", [P, KT, S], F32, A3 + 17344)
        GT3 = at("gate3", [P, KT, S], F32, A3 + 57344)
        DG = at("tap_diag", [P, sum(PE_TAPS), P], F32, AR + 16384)
        ABUF = at("a_buf", [P, 4, S], F32, A3 + 41920)
        CT = at("c_t", [P, 2, S], F32, A3 + 50112)
        REST = at("x_by_token", [P, NB, D], F32, A3)
        YTOK = at("y_by_token", [P, NB, D], F32, A3 + 57344)
        WPOST = at("post_w", [P, D], F32, A3 + 75776)

        PS = ctx.enter_context(nc.psum_tensor("ps", [P, 8, S], F32))
        MX = PS[:, 4:8, :]

        raw_in = [sem("raw_in0"), sem("raw_in1")]
        w_hi, w_lo = sem("w_hi_ready"), sem("w_lo_ready")
        half_done = sem("half_done")
        bank_free = sem("bank_free")
        op_src, op_hi, op_lo = sem("op_src"), sem("op_hi"), sem("op_lo")
        sq_ready, acc_done = sem("sq_ready"), sem("acc_done")
        stat_filled, rstd_ready = sem("stat_filled"), sem("rstd_ready")
        dchain, achain, gchain = sem("dve_step"), sem("act_step"), sem("pool_step")
        x_in, c_in, out_done = sem("x_in"), sem("const_in"), sem("out_done")
        c2_in, x2_in, ali_in = sem("const2_in"), sem("x2_in"), sem("alibi_in")
        xt_filled, xt_taken = sem("xt_filled"), sem("xt_taken")
        par_filled, par_ready = sem("par_filled"), sem("par_ready")
        ones_ready = sem("ones_ready")
        conv_ready, silu_done = sem("gdn_conv_ready"), sem("gdn_silu_done")
        ab_split, ab_filled, ab_rows = sem("ab_split"), sem("ab_filled"), sem("ab_rows")
        abt_filled, abt_ready, rcol_ready = sem("abt_filled"), sem("abt_ready"), sem("rcol_ready")
        sp_in, sp_done, gb_ready = sem("softplus_in"), sem("softplus_exp"), sem("g_beta_ready")
        sqk, ssq_filled, r4_ready = sem("kq_squares"), sem("kq_ssq_filled"), sem("kq_norm_ready")
        kq_normed, gu_ready = sem("kq_normed"), sem("gu_ready")
        gc_filled, gc_ready, lb_ready = sem("gc_filled"), sem("gc_ready"), sem("lb_ready")
        gcb_filled, eb_ready, x1_ready = sem("gcb_filled"), sem("eb_ready"), sem("x1_ready")
        dmm_ready, dexp, dt_ready = sem("dmm_ready"), sem("decay_exp"), sem("dt_ready")
        g_filled, m_ready, qk_filled = sem("g_filled"), sem("m_ready"), sem("qk_filled")
        qkt_ready, t2_ready = sem("qkt_ready"), sem("t2_ready")
        tt_filled, tt_ready = sem("tt_filled"), sem("tt_ready")
        xp_filled, xs_ready, xz_ready = sem("xp_filled"), sem("xs_ready"), sem("xz_ready")
        txp_filled, upd_done = sem("txp_filled"), sem("upd_done")
        rot_ready = sem("ret_rotated")
        rs_filled, rs_ready = sem("ret_s_filled"), sem("ret_s_ready")
        ro_filled, ro_ready = sem("ret_o_filled"), sem("ret_o_ready")
        rsq_ready, rssq_filled, rr_ready = sem("ret_sq"), sem("ret_ssq_filled"), sem("ret_rstd")
        tok_filled, tokv_ready, tokk_ready = sem("tok_filled"), sem("tok_v_ready"), sem("tok_k_ready")
        nw_filled, nw_ready = sem("nw_filled"), sem("nw_ready")
        u_filled, u_ready = sem("u_filled"), sem("u_ready")
        qd_ready = sem("qd_ready")
        so_filled, o_ready, s_ready = sem("so_filled"), sem("gdn_o_ready"), sem("state_ready")
        gate_done = sem("gate_silu")
        ff_conv, ff_silu = sem("ff_conv"), sem("ff_silu")
        sc_filled, sc_ready, p_exp, p_ready = (sem("scores_filled"), sem("scores_max"),
                                               sem("probs_exp"), sem("probs_ready"))
        pt_filled, pt_ready = sem("pt_filled"), sem("pt_ready")
        ov_filled, ov_taken = sem("att_o_filled"), sem("att_o_taken")
        pool_ready, py_filled, py_taken = sem("pooled_ready"), sem("pool_y_filled"), sem("pool_y_taken")
        ff_prod, ff_hi, ff_lo = sem("ff_product"), sem("ff_hi"), sem("ff_lo")
        sig_done = sem("sigmoid_done")
        diag_ready, glu_ready = sem("tap_diag_ready"), sem("glu_ready")
        cv_filled, cv_ready = sem("conv_part_filled"), sem("conv_ready")
        ln_added = sem("ln_square_added")
        ln_in, ln_done = sem("ln_in"), sem("ln_silu")
        cm_filled, cm_taken = sem("mean_filled"), sem("mean_taken")
        vt_filled, vt_ready = sem("att_v_filled"), sem("att_v_ready")
        wpost_in, y_done, ysq_done = sem("post_w_in"), sem("y_block_done"), sem("y_squared")
        yss_ready, ysd_ready = sem("y_sum_ready"), sem("y_deviation_ready")
        rest_filled, rest_taken, ot_ready = sem("x_t_filled"), sem("x_t_taken"), sem("out_ready")

        block = ctx.enter_context(nc.Block())

        def f32(ap):
            return ap.bitcast(F32)

        def vec(name, k=0):
            c = VEC_AT[name] + k
            return VEC[:, c:c + 1]

        @block.sync
        def _(sp):
            def rows(w, r0, n, c0):
                return w[r0:r0 + n * P, bass.ds(c0, 256)].rearrange("(k p) c -> p k c", p=P)

            def free_slot(p):
                sp.wait_ge(w_lo, split_when_free(p))

            def wide_pair(p, w, r0, c0):
                for k in (0, 2):
                    sp.dma_start(RAW[:, p % 2, 2 * k:2 * k + 4, :].rearrange("p (k t) c -> p k (t c)", t=2),
                                 w[r0 + k * P:r0 + (k + 2) * P, c0:c0 + 512]
                                 .rearrange("(k p) c -> p k c", p=P)).then_inc(raw_in[p % 2], 16)

            def pair(p, slot, w, c0, r0=0, n=8):
                m = n // 2
                for k0, kn in ((0, m), (m, n - m)):
                    sp.dma_start(RAW[:, slot, k0:k0 + kn, :], rows(w, r0 + k0 * P, kn, c0)) \
                        .then_inc(raw_in[slot], 16)

            for b in range(NB):
                sp.dma_start(XTOK[:, b, :], a["x"][0, b * P:(b + 1) * P, :]).then_inc(x_in, 16)
            sp.dma_start(IDENT[:, :], const["ident"]).then_inc(c_in, 16)
            r = 0
            srcs = {"pre0": a["pre_norm_2"][0], "pre1": a["pre_norm_2"][1],
                    "post0": a["post_norm_2"][0], "post1": a["post_norm_2"][1],
                    "attn_norm_w": a["attn_norm_w"][0], "mlp_norm_w": a["mlp_norm_w"][0],
                    "final_norm_w": a["final_norm_w"], "pool_scale": a["b_pool_scale_2"][0],
                    "dw_b": a["c_dw_b_2"][0], "ln_g": a["c_ln_g_2"][0], "ln_b": a["c_ln_b_2"][0],
                    "gdn_norm_w": a["gdn_norm_w"][0]}
            for name, n in VECS:
                sp.dma_start(ROWS[r:r + n, 0, :], srcs[name].rearrange("(k p) -> k p", p=P)) \
                    .then_inc(c_in, 16)
                r += n
            w_in = a["w_in"][0]
            pair(0, 0, w_in, 512)
            sp.dma_start(ROWS[0:48, 1, :], a["gdn_conv_w"][0].rearrange("i (t p) -> (i t) p", p=P)) \
                .then_inc(c_in, 16)
            mc = a["mlp_conv_w"][0].rearrange("i (t p) -> (i t) p", p=P)
            dc = a["c_dw_w_2"][0, :, 0, :].rearrange("i (t p) -> (i t) p", p=P)
            sp.dma_start(ROWS[0:66, 2, :], mc[0:66, :]).then_inc(c_in, 16)
            sp.dma_start(ROWS[0:66, 5, :], mc[66:132, :]).then_inc(c_in, 16)
            sp.dma_start(ROWS[0:124, 3, :], dc[0:124, :]).then_inc(c_in, 16)
            sp.dma_start(ROWS[0:124, 4, :], dc[124:248, :]).then_inc(c_in, 16)
            pair(1, 1, w_in, 768)
            sp.dma_start(ABR[:, :, :], w_in[:, 4 * GW:4 * GW + 8].rearrange("(k p) c -> p k c", p=P)) \
                .then_inc(c2_in, 16)
            sp.dma_start(ALD[:, 0:4], a["gdn_a_log"][0].rearrange("(a n) -> a n", a=1)
                         .broadcast_to([P, 4])).then_inc(c2_in, 16)
            sp.dma_start(ALD[:, 4:8], a["gdn_dt_bias"][0].rearrange("(a n) -> a n", a=1)
                         .broadcast_to([P, 4])).then_inc(c2_in, 16)
            sp.dma_start(MASK[:, :], const["masks"]).then_inc(c2_in, 16)
            sp.dma_start(CS[:, :, :], const["cos_sin"]).then_inc(c2_in, 16)
            sp.dma_start(DR[:, :, :], const["ret_decay"]).then_inc(c2_in, 16)
            R = 4 * GW + 8
            starts = [512, 768, 0, 256, 1024, 1280, R + 1024, R + 1280, R, R + 512, R + 256, R + 768,
                      R + 1536, R + 1792, 1536, 1792]
            for p in range(2, 16):
                free_slot(p)
                if wide(2 * p):
                    wide_pair(p, w_in, (p - 6) * 512, starts[6])
                else:
                    pair(p, p % 2, w_in, starts[p])
                if p in (13, 14):
                    sp.wait_ge(ro_ready, 4)
                    for b in range(2 * (p - 13), 2 * (p - 13) + 2):
                        sp.dma_start(XTOK2[:, b, :], a["x"][0, b * P:(b + 1) * P, :]).then_inc(x2_in, 16)
            w_out = a["w_out"][0]
            for p in range(16, 20):
                free_slot(p)
                c0 = (p - 16) * 256
                for k0, r0 in ((0, GW), (4, 0)):
                    sp.dma_start(RAW[:, p % 2, k0:k0 + 4, :], rows(w_out, r0, 4, c0)) \
                        .then_inc(raw_in[p % 2], 16)
            w_up = a["w_up"][0]
            with sp.Fori(0, 11) as i:
                for s in range(2):
                    sp.wait_ge(w_lo, i * 8 + 4 * (U3 // 2 + s - 1))
                    pair(0, s, w_up, i * 256 + s * DFF)
            w_down = a["w_down"][0]
            with sp.Fori(0, 2) as i:
                for j in range(6):
                    sp.wait_ge(w_lo, i * 24 + 4 * (U4 // 2 + j - 1))
                    g = j % 3
                    pair(0, j % 2, w_down, i * 512 + 256 * (j // 3), r0=g * D, n=8 if g < 2 else 6)
            w5 = a["a_w_in_2"][0]
            for p in range(U5 // 2, U6 // 2):
                free_slot(p)
                j = p - U5 // 2
                if j in (0, 1, 3, 4):
                    c0 = (0 if j < 2 else 768) + 128 * ((j + 1) % 2 if j > 2 else j)
                    for kv in range(2):
                        sp.dma_start(RAW[:, p % 2, :, kv * P:(kv + 1) * P],
                                     w5[:, c0 + kv * 256:c0 + kv * 256 + P]
                                     .rearrange("(k p) c -> p k c", p=P)).then_inc(raw_in[p % 2], 16)
                else:
                    pair(p, p % 2, w5, {2: 512, 5: 1280, 6: 1536, 7: 1792, 8: 2048}[j])
                if j == 0:
                    sp.wait_ge(half_done, 2 * U5)
                    sp.dma_start(ALI[:, :, :], const["alibi"]).then_inc(ali_in, 16)
                    sp.dma_start(PW[:, :, :], a["b_pool_w_2"][0].rearrange("g c d -> c g d")) \
                        .then_inc(ali_in, 16)
                    sp.dma_start(ITAB[:, :, :], const["inv_cnt"]).then_inc(ali_in, 16)
                    sp.dma_start(SINK[:, :], a["a_sinks_2"][0].rearrange("(a n) -> a n", a=1)
                                 .broadcast_to([P, QH])).then_inc(ali_in, 16)
            w6 = a["ab_w_out_2"][0]
            for p in range(U6 // 2, U7 // 2):
                free_slot(p)
                c0 = (p - U6 // 2) * 256
                for kv in range(2):
                    sp.dma_start(RAW[kv * 64:(kv + 1) * 64, p % 2, 0:4, :],
                                 w6[kv * 256:(kv + 1) * 256, c0:c0 + 256]
                                 .rearrange("(t d) c -> d t c", d=HD2)).then_inc(raw_in[p % 2], 16)
                sp.dma_start(RAW[:, p % 2, 4:8, :], rows(w6, 512, 4, c0)).then_inc(raw_in[p % 2], 16)
            w7 = a["c_w_in_2"][0]
            for p in range(U7 // 2, U7 // 2 + 8):
                free_slot(p)
                j = p - U7 // 2
                pair(p, p % 2, w7, (j // 2) * 256 + (j % 2) * D)
                if j == 2:
                    sp.wait_ge(op_src, 40)
                    sp.dma_start(WPOST[:, :], a["post_norm_2"][1:2, :].broadcast_to([P, D])) \
                        .then_inc(wpost_in, 16)
            for p in range(U7 // 2 + 8, U8 // 2):
                free_slot(p)
                pair(p, p % 2, w7, 2 * D + (p - U7 // 2 - 8) * 256)
            w8 = a["c_w_out_2"][0]
            for p in range(U8 // 2, PAIRS):
                free_slot(p)
                j = p - U8 // 2
                wide_pair(p, w8, (j % 2) * 512, (j // 2) * 512)
            for b in range(NB):
                for g in range(2):
                    sp.wait_ge(ot_ready, 2 * b + g + 1)
                    sp.dma_start(out[0, b * P:(b + 1) * P, g * 512:(g + 1) * 512],
                                 YTOK[:, b, g * 512:(g + 1) * 512]).then_inc(out_done, 16)
            sp.wait_ge(out_done, 32 * NB)

        def half_k(n):
            u = unit_half(n)[0]
            return 3 if U4 <= u < U5 and ((u - U4) // 2) % 3 == 2 else 4

        def by_heads(n):
            u = unit_half(n)[0]
            return U5 <= u < U5 + 4 or U5 + 6 <= u < U5 + 10

        def raw_half(n):
            kn = half_k(n)
            u, hf = unit_half(n)
            if wide(u):
                return RAW[:, (u // 2) % 2, 2 * (n % 4):2 * (n % 4) + 2, :].rearrange("p k (t c) -> p (k t) c", t=2)
            r = RAW[:, (u // 2) % 2, kn * hf:kn * hf + kn, :]
            t = u % 2
            if by_heads(n):
                return r.rearrange("p k (v t d) -> p k v t d", v=2, t=2)[:, :, :, t, :]
            return r[:, :, t * P:(t + 1) * P]

        def ring_half(w, n):
            w = w[:, n % 4, 0:half_k(n), :]
            return w.rearrange("p k (v d) -> p k v d", v=2) if by_heads(n) else w

        @block.gpsimd
        def _(gp):
            def split_lo(n, later=0):
                gp.wait_ge(w_hi, later + n + 1)
                nc.gpsimd.tensor_tensor(ring_half(WL, n), raw_half(n), f32(ring_half(WH, n)), SUB) \
                    .then_inc(w_lo, 1)

            def unit(u):
                split_lo(2 * u)
                split_lo(2 * u + 1)

            def zero(level, c):
                x = XZ[:, c, :, :].rearrange("p h (b two s) -> p h b two s", two=2, s=2 << level)
                nc.gpsimd.memset(x[:, :, :, 0, :], 0.0).then_inc(xz_ready, 1)

            nc.gpsimd.memset(ONES[:, :], 1.0).then_inc(ones_ready, 1)
            nc.gpsimd.memset(CB[:, 0:1], EPS).then_inc(ones_ready, 1)
            nc.gpsimd.memset(CB[:, 1:2], math.log(P ** -0.5)).then_inc(ones_ready, 1)
            nc.gpsimd.memset(CB[:, 2:3], 1.0).then_inc(ones_ready, 1)
            nc.gpsimd.memset(PAD[:, :, 0:3], 0.0).then_inc(ones_ready, 1)
            for u in range(14):
                unit(u)
            gp.wait_ge(gb_ready, 1)
            gp.wait_ge(c2_in, 96)
            nc.gpsimd.tensor_tensor(LB[:, :, :], LOWER.unsqueeze(1).broadcast_to([P, 16, P]),
                                    BETA.unsqueeze(2).broadcast_to([P, 16, P]), MUL).then_inc(lb_ready, 1)
            unit(14)
            unit(15)
            gp.wait_ge(dexp, 1)
            nc.gpsimd.tensor_tensor(T[:, :, :], T[:, :, :], UPPER.unsqueeze(1).broadcast_to([P, 16, P]),
                                    MUL).then_inc(dt_ready, 1)
            unit(16)
            gp.wait_ge(m_ready, 1)
            for c in range(NB):
                zero(0, c)
            unit(17)
            unit(18)
            for level in range(5):
                unit(19 + level)
                for c in range(NB):
                    gp.wait_ge(txp_filled, 4 * level + c + 1)
                    zero(level + 1, c)
            for u in range(24, U3):
                unit(u)
            with gp.Fori(0, 11) as i:
                for j in range(8):
                    split_lo(2 * U3 + j, i * 8)
            for u in range(U4, UNITS):
                unit(u)
                k = u - U7 - 2
                if 0 <= k < KT:
                    if k == 0:
                        gp.wait_ge(half_done, 2 * U7)
                        gp.wait_ge(par_ready, 4)
                    n0, n1 = sum(PE_TAPS[:k]), sum(PE_TAPS[:k + 1])
                    nc.gpsimd.tensor_tensor(DG[:, n0:n1, :],
                                            IDENT[:, :].unsqueeze(1).broadcast_to([P, n1 - n0, P]),
                                            DCW[:, CK - (n1 - n0):CK, k].unsqueeze(2)
                                            .broadcast_to([P, n1 - n0, P]), MUL).then_inc(diag_ready, 1)

        @block.scalar
        def _(act):
            steps = [0]

            def table(n):
                nc.scalar.add_instruction(mybir.InstLoadActFuncSet(
                    name=nc.get_next_instruction_name(), act_func_set_id=n,
                    engine=mybir.EngineType.Activation, ins=[], outs=[]))

            def step(ins):
                steps[0] += 1
                ins.then_inc(achain, 1)
                act.wait_ge(achain, steps[0])

            def split_hi(n, i=None):
                p = unit_half(n)[0] // 2
                if n >= UNITS * 2:
                    return
                if i is None:
                    act.wait_ge(raw_in[p % 2], 16 * loads_before(p))
                    if n >= 4:
                        act.wait_ge(half_done, n - 3)
                else:
                    act.wait_ge(raw_in[p % 2], i * 32 + 16 * loads_before(p))
                    act.wait_ge(half_done, i * 8 + n - 3)
                nc.scalar.activation(ring_half(WH, n), raw_half(n), ACT.Copy).then_inc(w_hi, 1)

            def splits(u):
                if u not in QUADS:
                    split_hi(2 * u + 3)
                if u not in QUADS and u + 1 not in QUADS:
                    split_hi(2 * u + 4)

            def operand_hi(src, dst, scale):
                nc.scalar.activation(dst, src, ACT.Copy, scale=scale).then_inc(op_hi, 1)

            def square(st, k, src, dst):
                if k >= 2:
                    if st == 6:
                        act.wait_ge(ln_added, k - 1)
                    else:
                        act.wait_ge(acc_done, 8 * acc_round(st) + k - 1)
                nc.scalar.activation(dst, src, ACT.Square).then_inc(sq_ready, 1)

            def stat(st):
                table(LN_EXP_SET)
                if st == 6:
                    act.wait_ge(ln_added, KT)
                else:
                    act.wait_ge(stat_filled, acc_round(st) + 1)
                step(nc.scalar.activation(RSTD[:, :], PS[:, 6 if st == 6 else 7, :], ACT.Ln,
                                          bias=CB[:, 0:1], scale=1.0 / D))
                nc.scalar.activation(RSTD[:, :], RSTD[:, :], ACT.Exp, scale=-0.5).then_inc(rstd_ready, 1)

            act.wait_ge(par_ready, 1)
            act.wait_ge(ones_ready, 5)
            for k in range(KT):
                act.wait_ge(op_src, k + 1)
                operand_hi(SC[:, k % 2, :], XA[:, k, 0, :], vec("attn_norm_w", k))
                square(0, k, SC[:, k % 2, :], SC[:, 2 + k % 2, :])
                if k % 2 == 1 and k < 7:
                    split_hi(k // 2)

            def tile_silu(u):
                act.wait_ge(conv_ready, u + 1)
                d = KQ[:, u % 4, u // 4, :] if u < 8 else V[:, u - 8, :]
                nc.scalar.activation(d, d, ACT.Silu).then_inc(silu_done, 1)

            def values(c):
                act.wait_ge(tok_filled, 2 * c + 2)
                for h in range(H):
                    nc.scalar.activation(VB[:, h, :], PS[:, 5, h * P:(h + 1) * P], ACT.Copy,
                                         scale=BETA[:, 4 * c + h:4 * c + h + 1]).then_inc(tokv_ready, 1)

            def new_values(c):
                act.wait_ge(u_filled, c + 1)
                nc.scalar.activation(UU[:, :, :], PS[:, 7, :].rearrange("p (h v) -> p h v", h=H), ACT.Copy) \
                    .then_inc(u_ready, 1)

            def outputs(c):
                act.wait_ge(so_filled, 2 * c + 1)
                nc.scalar.activation(KQ[:, :, 1, c * P:(c + 1) * P],
                                     PS[:, 6, :].rearrange("p (h i) -> p h i", h=H), ACT.Copy) \
                    .then_inc(o_ready, 1)

            def weights_t(c):
                act.wait_ge(nw_filled, c)
                nc.scalar.activation(NW[:, :, :], PS[:, 6, :].rearrange("p (h c) -> p h c", h=H), ACT.Copy) \
                    .then_inc(nw_ready, 1)

            def ret_out(h):
                act.wait_ge(ro_filled, h + 1)
                nc.scalar.activation(RV[:, h, :, :].rearrange("p b i -> p (b i)"), PS[:, 6, :], ACT.Copy) \
                    .then_inc(ro_ready, 1)

            def ret_norm(r):
                table(LN_EXP_SET)
                act.wait_ge(rssq_filled, r + 1)
                rr = RR[:, 2 * r:2 * r + 2, :]
                step(nc.scalar.activation(rr, MX[:, 0:2, :], ACT.Ln, bias=CB[:, 0:1], scale=1.0 / P))
                nc.scalar.activation(rr, rr, ACT.Exp, scale=-0.5).then_inc(rr_ready, 1)

            def ret_operand(h):
                act.wait_ge(op_src, 8 + h + 1)
                operand_hi(RV[:, h, :, :].rearrange("p b i -> p (b i)"), XA[:, h, 0, :], 1.0)

            for u in range(U1, U2):
                splits(u)
                if u == 0:
                    stat(0)
                if 1 <= u <= 12:
                    tile_silu(u - 1)
                if u == 12:
                    act.wait_ge(silu_done, 8)
                    nc.scalar.activation(SQ4[:, :, :], KQ[:, :, 0, :], ACT.Square).then_inc(sqk, 1)
                    table(LN_EXP_SET)
                    act.wait_ge(sp_in, 1)
                    step(nc.scalar.activation(SPM, SPM, ACT.Exp))
                    step(nc.scalar.activation(SPM, SPM, ACT.Ln, bias=CB[:, 2:3]))
                    step(nc.scalar.activation(ALD[:, 0:4], ALD[:, 0:4], ACT.Exp))
                    nc.scalar.activation(SPB, SPB, ACT.Exp, scale=-1.0).then_inc(sp_done, 1)
                    act.wait_ge(ssq_filled, 1)
                    step(nc.scalar.activation(R4[:, :, :], MX, ACT.Ln, bias=CB[:, 0:1]))
                    nc.scalar.activation(R4[:, :, :], R4[:, :, :], ACT.Exp, scale=-0.5).then_inc(r4_ready, 1)
                    nc.scalar.activation(SQ4[:, :, :], KQ[:, :, 1, :], ACT.Square).then_inc(sqk, 1)
                if u == 13:
                    act.wait_ge(ssq_filled, 2)
                    act.wait_ge(kq_normed, 1)
                    step(nc.scalar.activation(R4[:, :, :], MX, ACT.Ln, bias=CB[:, 0:1]))
                    nc.scalar.activation(R4[:, :, :], R4[:, :, :], ACT.Exp, scale=-0.5, bias=CB[:, 1:2]) \
                        .then_inc(r4_ready, 1)
                if u == 14:
                    act.wait_ge(gc_ready, 1)
                    nc.scalar.activation(EGC, GC, ACT.Exp).then_inc(eb_ready, 1)
                    act.wait_ge(gcb_filled, 1)
                    nc.scalar.activation(EB[:, :, :].rearrange("p a i -> p (a i)"),
                                         MX.rearrange("p b s -> p (b s)"), ACT.Exp).then_inc(eb_ready, 1)
                    act.wait_ge(dmm_ready, 1)
                    nc.scalar.activation(T[:, :, :], T[:, :, :], ACT.Exp).then_inc(dexp, 1)
                    act.wait_ge(dmm_ready, 2)
                    nc.scalar.activation(M[:, :, :], M[:, :, :], ACT.Exp, scale=-1.0).then_inc(dexp, 1)
                if u == 17:
                    act.wait_ge(tt_filled, 1)
                    nc.scalar.activation(TT[:, :, :].rearrange("p a i -> p (a i)"),
                                         MX.rearrange("p b s -> p (b s)"), ACT.Copy).then_inc(tt_ready, 1)
                if u in RET_GAP:
                    ret_out(RET_GAP.index(u))
                if u == 24:
                    values(0)
                if u == 25:
                    act.wait_ge(ro_ready, 4)
                    nc.scalar.activation(RR[:, :, :], RV[:, :, :, :].rearrange("p h b i -> p h (b i)"),
                                         ACT.Square).then_inc(rsq_ready, 1)
                    ret_norm(0)
                if u == 26:
                    new_values(0)
                    values(1)
                    outputs(0)
                if u == 27:
                    weights_t(1)
                    ret_norm(1)
                if u == 28:
                    new_values(1)
                    values(2)
                    outputs(1)
                if u == 29:
                    act.wait_ge(bank_free, M1 + 28)
                    nc.scalar.activation(GT[:, 0:4, :], GT[:, 0:4, :], ACT.Silu).then_inc(gate_done, 1)
                    weights_t(2)
                if u == 30:
                    new_values(2)
                    values(3)
                    outputs(2)
                if u == 31:
                    weights_t(3)
                    act.wait_ge(half_done, 2 * U2)
                    ret_operand(0)
                    new_values(3)
                    ret_operand(1)
                    outputs(3)
                    ret_operand(2)
                    ret_operand(3)
                    act.wait_ge(o_ready, 4)
                    act.wait_ge(op_src, 12)
                    nc.scalar.activation(RR[:, :, :], KQ[:, :, 1, :], ACT.Square).then_inc(rsq_ready, 1)
                    act.wait_ge(bank_free, M1 + 32)
                    nc.scalar.activation(GT[:, 4:8, :], GT[:, 4:8, :], ACT.Silu).then_inc(gate_done, 1)
            split_hi(2 * U2 + 2)
            split_hi(2 * U2 + 3)
            table(LN_EXP_SET)
            act.wait_ge(rssq_filled, 3)
            step(nc.scalar.activation(RR[:, :, :], MX, ACT.Ln, bias=CB[:, 0:1], scale=1.0 / P))
            nc.scalar.activation(RR[:, :, :], RR[:, :, :], ACT.Exp, scale=-0.5).then_inc(rr_ready, 1)
            split_hi(2 * U2 + 4)
            for h in range(H):
                act.wait_ge(op_src, 12 + h + 1)
                operand_hi(KQ[:, h, 1, :], XA[:, 4 + h, 0, :], 1.0)

            def from_residual(k):
                act.wait_ge(bank_free, M2 + k + 1)
                operand_hi(RES[:, k, :], XB[:, k, 0, :], vec("mlp_norm_w", k))
                square(1, k, RES[:, k, :], SQ2[:, k % 2, :])

            for u in range(U2, U3):
                k = u - U2
                splits(u)
                act.wait_ge(xt_filled, 8 + k + 1)
                if k >= 2:
                    act.wait_ge(bank_free, M2 + k - 1)
                nc.scalar.activation(XT2[:, k % 2, :], PS[:, 4 + k % 4, :], ACT.Copy).then_inc(xt_taken, 1)
                if k >= 1:
                    from_residual(k - 1)
            from_residual(KT - 1)
            stat(1)
            table(SILU_SET)
            with act.Fori(0, 11) as i:
                for j in range(4):
                    split_hi(2 * (U3 + j) + 3, i)
                    split_hi(2 * (U3 + j) + 4, i)
                    if j < 2:
                        act.wait_ge(ff_conv, i * 2 + j + 1)
                        nc.scalar.activation(CF[:, j, :], CF[:, j, :], ACT.Silu).then_inc(ff_silu, 1)
                    else:
                        act.wait_ge(ff_prod, i * 2 + j - 1)
                        nc.scalar.activation(ACTS[:, bass.ds(i * 2 + (j - 2), 1), 0, :]
                                             .rearrange("p a s -> p (a s)"), PRODF[:, j - 2, :], ACT.Copy) \
                            .then_inc(ff_hi, 1)

            for u in range(U4, U5 + 1):
                if u > U4 and (u - U4) % 6 == 0:
                    for k in (2 * ((u - U4) // 6) - 2, 2 * ((u - U4) // 6) - 1):
                        act.wait_ge(bank_free, M4 + k + 1)
                        square(2, k, RES[:, k, :], SQ4B[:, k % 2, :])
                if u < U5:
                    splits(u)
            stat(2)
            split_hi(2 * U5 + 2)
            for k in range(KT):
                if k == 4:
                    split_hi(2 * U5 + 3)
                if k == 7:
                    split_hi(2 * U5 + 4)
                act.wait_ge(op_src, 16 + k + 1)
                operand_hi(RES[:, k, :], XA[:, k, 0, :], vec("pre0", k))
                square(3, k, RES[:, k, :], SQ3[:, k % 2, :])

            def probs(j):
                act.wait_ge(sc_ready, j + 1)
                lo = P if j < 2 else 0
                for t in range(4):
                    nc.scalar.activation(SB[:, j % 2, t, lo:256], SB[:, j % 2, t, lo:256], ACT.Exp,
                                         bias=AS[:, 1, t:t + 1], accum_out=AS[:, 2, t:t + 1]) \
                        .then_inc(p_exp, 1)
                nc.scalar.activation(AS[:, 3, 0:4], AS[:, 3, 0:4], ACT.Exp).then_inc(p_exp, 1)

            for u in range(U5, U6):
                splits(u)
                if u == U5:
                    stat(3)
                j = u - (U5 + 6)
                if j == 0:
                    act.wait_ge(vt_filled, 1)
                    nc.scalar.activation(VS[:, :, :], PS[:, 7, :].rearrange("p (b d) -> p b d", b=NB),
                                         ACT.Copy).then_inc(vt_ready, 1)
                if 1 <= j <= 8:
                    act.wait_ge(pt_filled, j)
                    lo = 1 if j - 1 < 2 else 0
                    nc.scalar.activation(PTS[:, :, lo:2, :],
                                         PS[:, 6:8, :].rearrange("p b (t w i) -> p (b t) w i", t=2, w=2)
                                         [:, :, lo:2, :], ACT.Copy).then_inc(pt_ready, 1)
                if 0 <= j < 8:
                    probs(j)
                if 1 <= j <= 8:
                    b, kv = (j - 1) // 2, (j - 1) % 2
                    act.wait_ge(ov_filled, j)
                    nc.scalar.activation(MIXF[kv * HD2:(kv + 1) * HD2, 0:4, b * P:(b + 1) * P],
                                         PS[kv * HD2:(kv + 1) * HD2, 6, :]
                                         .rearrange("p (t i) -> p t i", t=4), ACT.Copy).then_inc(ov_taken, 1)
                if j == 9:
                    act.wait_ge(py_filled, 1)
                    for g in range(4):
                        nc.scalar.activation(PL[:, g, :], MX[:, g, :], ACT.Copy,
                                             scale=vec("pool_scale", g)).then_inc(py_taken, 1)
                    act.wait_ge(bank_free, M5 + 10)
                    nc.scalar.activation(GA[:, :, :], GA[:, :, :], ACT.Silu).then_inc(gate_done, 1)
                if j == 10:
                    for t in range(4):
                        act.wait_ge(op_src, 24 + t + 1)
                        operand_hi(MIXF[:, t, :], XB[:, t, 0, :], 1.0)
                if j >= 9:
                    g = j - 9
                    act.wait_ge(bank_free, M5 + 14 + g + 1)
                    nc.scalar.activation(GB[:, g, :], GB[:, g, :], ACT.Silu).then_inc(gate_done, 1)
            split_hi(2 * U6 + 2)
            split_hi(2 * U6 + 3)
            act.wait_ge(bank_free, M5 + 18)
            nc.scalar.activation(GB[:, 3, :], GB[:, 3, :], ACT.Silu).then_inc(gate_done, 1)
            for g in range(4):
                act.wait_ge(op_src, 28 + g + 1)
                operand_hi(MIXF[:, 4 + g, :], XB[:, 4 + g, 0, :], 1.0)
            split_hi(2 * U6 + 4)

            for u in range(U6, U7):
                splits(u)
                k = u - U6
                if k >= 1:
                    act.wait_ge(bank_free, M6 + k)
                    square(4, k - 1, Y[:, k - 1, :], SQ3[:, (k - 1) % 2, :])
            act.wait_ge(bank_free, M6 + KT)
            square(4, KT - 1, Y[:, KT - 1, :], SQ3[:, 1, :])
            stat(4)
            split_hi(2 * U7 + 2)
            for k in range(KT):
                if k == 4:
                    split_hi(2 * U7 + 3)
                if k == 7:
                    split_hi(2 * U7 + 4)
                act.wait_ge(op_src, 32 + k + 1)
                operand_hi(RES[:, k, :], XA[:, k, 0, :], vec("pre1", k))
                square(5, k, RES[:, k, :], SQ3[:, k % 2, :])
            stat(5)
            for u in range(U7, U8):
                splits(u)
                j = u - U7
                if j < 16 and j % 4 >= 2:
                    act.wait_ge(bank_free, M7 + j + 1)
                    nc.scalar.activation(ABUF[:, j % 4, :], ABUF[:, j % 4, :], ACT.Sigmoid) \
                        .then_inc(sig_done, 1)
            split_hi(2 * U8 + 3)
            for k in range(KT):
                act.wait_ge(bank_free, M7 + 16 + k + 1)
                nc.scalar.activation(GT3[:, k, :], GT3[:, k, :], ACT.Silu).then_inc(gate_done, 1)
            for k in range(KT):
                act.wait_ge(cm_taken, k + 1)
                square(6, k, CV[:, k, :], CT[:, k % 2, :])
            stat(6)
            for k in range(KT + 1):
                if k < KT:
                    act.wait_ge(ln_in, k + 1)
                    nc.scalar.activation(CV[:, k, :], CV[:, k, :], ACT.Silu, bias=vec("ln_b", k)) \
                        .then_inc(ln_done, 1)
                if k >= 1:
                    act.wait_ge(op_src, 40 + k)
                    operand_hi(CV[:, k - 1, :], XB[:, k - 1, 0, :], 1.0)
                if k >= 2:
                    split_hi(2 * U8 + k + 2)

            def x_by_token(k):
                act.wait_ge(rest_filled, k + 1)
                nc.scalar.activation(REST[:, :, k * P:(k + 1) * P],
                                     PS[:, REST_BANK[k % 4], :].rearrange("p (b f) -> p b f", b=NB),
                                     ACT.Copy).then_inc(rest_taken, 1)

            def squares_by_token(g):
                for b in range(NB):
                    if b < NB - 1:
                        act.wait_ge(y_done, 3 * g + b + 1)
                    else:
                        act.wait_ge(half_done, 2 * U8 + 8 * (g + 1))
                    if 4 * g + b >= 2:
                        act.wait_ge(ysq_done, 4 * g + b - 1)
                    nc.scalar.activation(CT[:, b % 2, :], PS[:, (M8 + b) % 4, :], ACT.Square,
                                         accum_out=AS[:, 0, 4 * g + b:4 * g + b + 1]).then_inc(ysq_done, 1)

            for k in range(4):
                x_by_token(k)
            split_hi(2 * U8 + 11)
            squares_by_token(0)
            for k in range(4):
                split_hi(2 * U8 + 12 + k)
                x_by_token(4 + k)
            squares_by_token(1)
            act.wait_ge(yss_ready, 1)
            nc.scalar.activation(AS[:, 2, 0:4], AS[:, 1, 0:4], ACT.Sqrt, bias=CB[:, 0:1], scale=1.0 / D) \
                .then_inc(ysd_ready, 1)

        @block.vector
        def _(dve):
            v = nc.vector
            steps = [0]
            late = [None]

            def step(ins):
                steps[0] += 1
                ins.then_inc(dchain, 1)
                dve.wait_ge(dchain, steps[0] if late[0] is None else late[0] + steps[0])

            def tile_done(u):
                dve.wait_ge(half_done, halves_when_done(u))

            def operand_lo(f, src, dst_lo, dst_hi, scale=1.0):
                dve.wait_ge(op_hi, f + 1)
                v.scalar_tensor_tensor(out=dst_lo, in0=src, scalar=scale, in1=f32(dst_hi), op0=MUL, op1=SUB) \
                    .then_inc(op_lo, 1)

            def accumulate(st, k, sq):
                n = 8 * acc_round(st) + k
                dve.wait_ge(sq_ready, 8 * st + k + 1)
                if k == 0:
                    v.tensor_copy(ACC[:, :], sq).then_inc(acc_done, 1)
                else:
                    dve.wait_ge(acc_done, n)
                    v.tensor_tensor(ACC[:, :], ACC[:, :], sq, ADD).then_inc(acc_done, 1)

            MX16 = MX.rearrange("p b (h i) -> p (b h) i", h=H)

            def lastdim(ap):
                return ap.unsqueeze(2).broadcast_to([P, 16, P])

            dve.wait_ge(par_filled, 1)
            v.tensor_copy(VEC[:, :], PS[:, 0, 0:NVEC]).then_inc(par_ready, 1)
            v.tensor_copy(GCW[:, :, :].rearrange("p a b -> p (a b)"), PS[:, 0, NVEC:NVEC + 48]) \
                .then_inc(par_ready, 1)
            v.tensor_copy(MCW[:, :, :].rearrange("p a b -> p (a b)"), PS[:, 0, NVEC + 48:NVEC + 180]) \
                .then_inc(par_ready, 1)
            v.tensor_copy(DCW[:, :, :].rearrange("p a b -> p (a b)"), PS[:, 1, 0:248]).then_inc(par_ready, 1)
            dve.wait_ge(par_ready, 4)
            for k in range(KT + 1):
                if k < KT:
                    dve.wait_ge(xt_filled, k + 1)
                    if k >= 2:
                        dve.wait_ge(op_lo, k - 1)
                    v.tensor_copy(SC[:, k % 2, :], PS[:, 4 + k % 4, :]).then_inc(op_src, 1)
                if k >= 1:
                    q = k - 1
                    dve.wait_ge(op_src, q + 1)
                    operand_lo(q, SC[:, q % 2, :], XA[:, q, 1, :], XA[:, q, 0, :], vec("attn_norm_w", q))
                    accumulate(0, q, SC[:, 2 + q % 2, :])

            def conv_tile(u):
                t = {0: 4, 1: 0, 2: 8}[u // 4] + u % 4
                d = KQ[:, u % 4, u // 4, :] if u < 8 else V[:, u - 8, :]
                x = PAD[:, u % 2, :]
                v.tensor_tensor(x[:, 3:3 + S], PS[:, u % 4, :], RSTD[:, :], MUL).then_inc(bank_free, 1)
                dve.wait_ge(bank_free, u + 1)
                step(v.tensor_scalar(d, x[:, 3:3 + S], GCW[:, 3, t:t + 1], None, MUL))
                for i in (2, 1):
                    step(v.scalar_tensor_tensor(out=d, in0=x[:, i:i + S], scalar=GCW[:, i, t:t + 1],
                                                in1=d, op0=MUL, op1=ADD))
                v.scalar_tensor_tensor(out=d, in0=x[:, 0:S], scalar=GCW[:, 0, t:t + 1], in1=d,
                                       op0=MUL, op1=ADD).then_inc(conv_ready, 1)

            SWAP = [i ^ 1 for i in range(32)]

            def rotate_tile(u):
                h = u % 2 + 2 * ((u - 16) // 4)
                d = (RQ if (u - 16) % 4 < 2 else RK)[:, h % 2, :]
                if h >= 2:
                    dve.wait_ge(rs_filled, 4 * (h - 1))
                step(v.tensor_tensor(d, PS[:, u % 4, :], CS[:, 0, :], MUL))
                v.stream_shuffle(SC[:, u % 2, :], PS[:, u % 4, :], SWAP).then_inc(bank_free, 1)
                dve.wait_ge(bank_free, u + 1)
                step(v.tensor_tensor(SC[:, u % 2, :], SC[:, u % 2, :], CS[:, 1, :], MUL))
                v.tensor_tensor(d, d, SC[:, u % 2, :], ADD).then_inc(rot_ready, 1)

            def level(l):
                s = 2 << l
                def half(ap, two):
                    return ap.rearrange("p h (b two s) -> p h b two s", two=2, s=s)[:, :, :, two, :]
                def part(bank, off):
                    return PS[:, bank, off:off + 256].rearrange("p (h b s) -> p h b s", h=H, s=s)
                mask = MASK[:, 3 * P + 64 * l:3 * P + 64 * (l + 1)].rearrange("p (b s) -> p b s", s=s) \
                    .unsqueeze(1).broadcast_to([P, H, 64 // s, s])
                for c in range(NB):
                    dve.wait_ge(xp_filled, 4 * l + c + 1)
                    v.tensor_tensor(half(XZ[:, c, :, :], 1), part(4 + c, 0), mask, MUL).then_inc(xs_ready, 1)
                for c in range(NB):
                    dve.wait_ge(txp_filled, 4 * l + c + 1)
                    u_ = half(TT[:, 4 * c:4 * c + 4, :], 1)
                    ins = v.tensor_tensor(u_, u_, part(4 + c, 256), SUB)
                    if l < 5:
                        t_ = half(T[:, 4 * c:4 * c + 4, :], 0)
                        ins = v.tensor_tensor(t_, t_, part(4 + c, 0), SUB)
                    ins.then_inc(upd_done, 1)

            def ret_scores(h):
                for jb in range(NB):
                    n = S - jb * P
                    dve.wait_ge(rs_filled, 4 * h + jb + 1)
                    v.tensor_tensor(RS[:, jb % 2, 0:n], PS[:, 4 + jb % 2, 0:n], DR[:, h, 0:n], MUL) \
                        .then_inc(rs_ready, 1)

            def keys(c):
                kt = PS[:, 4, :].rearrange("p (h d) -> p h d", h=H)
                dve.wait_ge(tok_filled, 2 * c + 1)
                if c > 0:
                    step(v.tensor_tensor(KB[:, :, :], kt, BEN[:, 4 * c:4 * c + 4].unsqueeze(2)
                                         .broadcast_to([P, H, P]), MUL))
                    state(c - 1)
                v.tensor_tensor(KD[:, :, :], kt, KDC[:, 4 * c:4 * c + 4].unsqueeze(2)
                                .broadcast_to([P, H, P]), MUL).then_inc(tokk_ready, 1)
                if c > 0:
                    v.tensor_tensor(QD[:, :, :], KQ[:, :, 1, c * P:(c + 1) * P],
                                    EB[:, 4 * c:4 * c + 4, :], MUL).then_inc(qd_ready, 1)

            def state(c):
                dve.wait_ge(so_filled, 2 * c + 2)
                for h in range(H):
                    ps = PS[:, 7, h * P:(h + 1) * P]
                    if c == 0:
                        ins = v.tensor_copy(ST8[:, h, :], ps)
                    else:
                        ins = v.scalar_tensor_tensor(out=ST8[:, h, :], in0=ST8[:, h, :],
                                                     scalar=EB[:, 4 * c + h, P - 1:P], in1=ps,
                                                     op0=MUL, op1=ADD)
                ins.then_inc(s_ready, 1)

            for u in range(U1, U2):
                if u == 3:
                    tile_done(u)
                    dve.wait_ge(ab_filled, 1)
                    v.tensor_tensor(AB[:, :], PS[0:8, 7, :], RSTD[0:8, :], MUL).then_inc(ab_rows, 1)
                if u == 4:
                    dve.wait_ge(abt_filled, 1)
                    step(v.tensor_copy(ABT, PS[:, 7, 0:32].rearrange("p (c e) -> p c e", e=8)))
                    v.tensor_copy(RCOL[:, :], PS[:, 6, 0:NB]).then_inc(rcol_ready, 1)
                    spm, spr, spb = (x.rearrange("p (c h) -> p c h", h=H) for x in (SPM, SPR, SPB))
                    step(v.tensor_tensor(spr, ABT[:, :, 0:4],
                                         ALD[:, 4:8].unsqueeze(1).broadcast_to([P, NB, H]), ADD))
                    step(v.scalar_tensor_tensor(out=SPM, in0=SPR, scalar=-1.0, in1=SPR, op0=MUL, op1=ALU.min))
                    step(v.tensor_scalar(SPR, SPR, 0.0, None, ALU.max))
                    v.tensor_copy(spb, ABT[:, :, 4:8]).then_inc(sp_in, 1)
                if u == 12:
                    dve.wait_ge(sp_done, 1)
                    gg = GG.rearrange("p (c h) -> p c h", h=H)
                    spr = SPR.rearrange("p (c h) -> p c h", h=H)
                    step(v.tensor_tensor(SPR, SPR, SPM, ADD))
                    step(v.scalar_tensor_tensor(out=gg, in0=spr, scalar=-1.0,
                                                in1=ALD[:, 0:4].unsqueeze(1).broadcast_to([P, NB, H]),
                                                op0=MUL, op1=MUL))
                    step(v.tensor_scalar(SPB, SPB, 1.0, None, ADD))
                    v.reciprocal(BETA, SPB).then_inc(gb_ready, 1)
                    v.tensor_tensor(T[:, :, :], UPPER.unsqueeze(1).broadcast_to([P, 16, P]), lastdim(GG), MUL) \
                        .then_inc(gu_ready, 1)
                    dve.wait_ge(r4_ready, 1)
                    v.tensor_tensor(KQ[:, :, 0, :], KQ[:, :, 0, :], R4[:, :, :], MUL).then_inc(kq_normed, 1)
                if u == 13:
                    dve.wait_ge(gc_filled, 1)
                    v.tensor_copy(GC, PS[:, 4, 0:16]).then_inc(gc_ready, 1)
                    dve.wait_ge(r4_ready, 2)
                    v.tensor_tensor(KQ[:, :, 1, :], KQ[:, :, 1, :], R4[:, :, :], MUL).then_inc(kq_normed, 1)
                if u == 14:
                    dve.wait_ge(eb_ready, 1)
                    step(v.scalar_tensor_tensor(out=BEN, in0=BETA, scalar=-1.0, in1=EGC, op0=MUL, op1=MUL))
                    dve.wait_ge(eb_ready, 2)
                    v.tensor_tensor(TT[:, :, :], MX16, lastdim(GC), SUB).then_inc(x1_ready, 1)
                    dve.wait_ge(x1_ready, 1)
                    v.tensor_scalar(T[:, :, :], TT[:, :, :], 0.0, None, ALU.min).then_inc(dmm_ready, 1)
                    v.tensor_scalar(M[:, :, :], TT[:, :, :], 0.0, None, ALU.max).then_inc(dmm_ready, 1)
                    dve.wait_ge(lb_ready, 1)
                    dve.wait_ge(dexp, 2)
                    step(v.tensor_tensor(M[:, :, :], M[:, :, :], LB[:, :, :], MUL))
                if u == 16:
                    dve.wait_ge(dt_ready, 1)
                    v.tensor_copy(KDC.unsqueeze(2), T[:, :, P - 1:P])
                    dve.wait_ge(qk_filled, 1)
                    v.tensor_tensor(QKT[:, :, :], MX16, T[:, :, :], MUL).then_inc(qkt_ready, 1)
                    dve.wait_ge(qkt_ready, 1)
                    dve.wait_ge(m_ready, 1)
                    step(v.tensor_tensor(T[:, :, :], M[:, :, :], PAIRM.unsqueeze(1).broadcast_to([P, 16, P]), MUL))
                    v.scalar_tensor_tensor(out=T[:, :, :], in0=T[:, :, :], scalar=-1.0,
                                           in1=IDENT[:, :].unsqueeze(1).broadcast_to([P, 16, P]),
                                           op0=MUL, op1=ADD).then_inc(t2_ready, 1)
                if 18 <= u <= 23:
                    level(u - 18)
                if u in RET_GAP:
                    ret_scores(RET_GAP.index(u))
                if u in (24, 26, 28, 30):
                    keys((u - 24) // 2)

                if not 12 <= u < 15:
                    tile_done(u)
                if u == 0:
                    dve.wait_ge(rstd_ready, 1)
                if u < 12:
                    conv_tile(u)
                elif u < 15:
                    pass
                elif u == 15:
                    dve.wait_ge(rcol_ready, 1)
                    for b in range(NB):
                        v.tensor_scalar(RV[:, :, b, :], PS[:, b, :].rearrange("p (h d) -> p h d", h=H),
                                        RCOL[:, b:b + 1], None, MUL).then_inc(bank_free, 1)
                    dve.wait_ge(g_filled, 1)
                    v.tensor_tensor(M[:, :, :], MX16, M[:, :, :], MUL).then_inc(m_ready, 1)
                elif u < 24:
                    rotate_tile(u)
                else:
                    v.tensor_tensor(GT[:, u - 24, :], PS[:, u % 4, :], RSTD[:, :], MUL).then_inc(bank_free, 1)
                if u == 1:
                    dve.wait_ge(c2_in, 96)
                    v.tensor_copy(ABH[:, :, :], ABR[:, :, :]).then_inc(ab_split, 1)
                    dve.wait_ge(ab_split, 1)
                    v.tensor_tensor(ABL[:, :, :], ABR[:, :, :], f32(ABH[:, :, :]), SUB).then_inc(ab_split, 1)
                    v.tensor_tensor(CS[:, 0, :], CS[:, 0, :], RSTD[:, :], MUL)
                    step(v.tensor_tensor(CS[:, 1, :], CS[:, 1, :], RSTD[:, :], MUL))
                if u == 30:
                    dve.wait_ge(rr_ready, 2)
                    for h in range(H):
                        o = RV[:, h, :, :].rearrange("p b i -> p (b i)")
                        step(v.tensor_tensor(o, o, RR[:, h, :], MUL))
                        if h == 0:
                            dve.wait_ge(gate_done, 1)
                        v.tensor_tensor(o, o, GT[:, h, :], MUL).then_inc(op_src, 1)
            for h in range(H):
                operand_lo(8 + h, RV[:, h, :, :].rearrange("p b i -> p (b i)"), XA[:, h, 1, :], XA[:, h, 0, :])
            dve.wait_ge(rr_ready, 3)
            for h in range(H + 1):
                if h < H:
                    o = KQ[:, h, 1, :]
                    step(v.scalar_tensor_tensor(out=o, in0=o, scalar=vec("gdn_norm_w"), in1=RR[:, h, :],
                                                op0=MUL, op1=MUL))
                    if h == 0:
                        dve.wait_ge(gate_done, 2)
                    v.tensor_tensor(o, o, GT[:, 4 + h, :], MUL).then_inc(op_src, 1)
                if h >= 1:
                    operand_lo(12 + h - 1, KQ[:, h - 1, 1, :], XA[:, 3 + h, 1, :], XA[:, 3 + h, 0, :])

            def after_residual(k):
                operand_lo(16 + k, RES[:, k, :], XB[:, k, 1, :], XB[:, k, 0, :], vec("mlp_norm_w", k))
                accumulate(1, k, SQ2[:, k % 2, :])

            for k in range(KT):
                tile_done(U2 + k)
                dve.wait_ge(xt_taken, k + 1)
                v.tensor_tensor(RES[:, k, :], PS[:, (M2 + k) % 4, :], XT2[:, k % 2, :], ADD) \
                    .then_inc(bank_free, 1)
                if k >= 1:
                    after_residual(k - 1)
            dve.wait_ge(bank_free, M2 + KT)
            after_residual(KT - 1)

            dve.wait_ge(half_done, 2 * U3)
            step(v.memset(PADF[:, :, 0:3], 0.0))
            dve.wait_ge(rstd_ready, 2)
            base_steps = steps[0]
            PER = 10
            with dve.Fori(0, 11) as i:
                late[0] = i * PER
                for j in range(4):
                    dve.wait_ge(half_done, i * 8 + 2 * (U3 + j + 1))
                    x = PADF[:, j, :]
                    d = CF[:, j, :]
                    t = i * 2 + (j % 2 + FT * (j // 2))
                    w = [MCW[:, q, bass.ds(t, 1)] for q in range(3)]
                    v.tensor_tensor(x[:, 3:3 + S], PS[:, j, :], RSTD[:, :], MUL).then_inc(bank_free, 1)
                    dve.wait_ge(bank_free, i * 4 + (M3 + j + 1))
                    step(v.tensor_scalar(d, x[:, 3:3 + S], w[2], None, MUL))
                    step(v.scalar_tensor_tensor(out=d, in0=x[:, 2:2 + S], scalar=w[1], in1=d,
                                                op0=MUL, op1=ADD))
                    ins = v.scalar_tensor_tensor(out=d, in0=x[:, 1:1 + S], scalar=w[0], in1=d,
                                                 op0=MUL, op1=ADD)
                    if j < 2:
                        ins.then_inc(ff_conv, 1)
                    else:
                        step(ins)
                        dve.wait_ge(ff_silu, i * 2 + (j - 1))
                        v.tensor_tensor(PRODF[:, j - 2, :], CF[:, j - 2, :], d, MUL).then_inc(ff_prod, 1)
                for j in range(2):
                    dve.wait_ge(ff_hi, i * 2 + (j + 1))
                    act_hi, act_lo = (ACTS[:, bass.ds(i * 2 + j, 1), q, :].rearrange("p a s -> p (a s)")
                                      for q in range(2))
                    v.tensor_tensor(act_lo, PRODF[:, j, :], f32(act_hi), SUB).then_inc(ff_lo, 1)
            assert steps[0] - base_steps == PER
            late[0] = None
            steps[0] = base_steps + 11 * PER

            for k in range(KT):
                tile_done(U4 + 6 * (k // 2) + 4 + k % 2)
                v.tensor_tensor(RES[:, k, :], PS[:, (M4 + k) % 4, :], RES[:, k, :], ADD).then_inc(bank_free, 1)
                if k >= 1:
                    accumulate(2, k - 1, SQ4B[:, (k - 1) % 2, :])
            accumulate(2, KT - 1, SQ4B[:, (KT - 1) % 2, :])
            dve.wait_ge(rstd_ready, 3)
            for k in range(KT + 1):
                if k < KT:
                    v.scalar_tensor_tensor(out=RES[:, k, :], in0=RES[:, k, :], scalar=vec("final_norm_w", k),
                                           in1=RSTD[:, :], op0=MUL, op1=MUL).then_inc(op_src, 1)
                if k >= 1:
                    dve.wait_ge(op_src, 16 + k)
                    operand_lo(24 + k - 1, RES[:, k - 1, :], XA[:, k - 1, 1, :], XA[:, k - 1, 0, :],
                               vec("pre0", k - 1))
                    accumulate(3, k - 1, SQ3[:, (k - 1) % 2, :])

            step(v.memset(UPD[:, :, 0:16], 0.0))

            def scores(j):
                b, kv = j // 2, j % 2
                lo = P if b == 0 else 0
                sb = SB[:, j % 2, :, lo:256]
                dve.wait_ge(sc_filled, j + 1)
                step(v.scalar_tensor_tensor(out=sb, in0=PS[:, 4:6, :].rearrange("p a (t k) -> p (a t) k", t=2)
                                            [:, :, lo:256], scalar=HD2 ** -0.5,
                                            in1=ALI[:, 4 * kv:4 * kv + 4, lo:256], op0=MUL, op1=ADD))
                step(v.tensor_reduce(AS[:, 0, 0:4], sb, AX.X, ALU.max))
                sink = SINK[:, 4 * kv:4 * kv + 4]
                step(v.tensor_tensor(AS[:, 0, 0:4], AS[:, 0, 0:4], sink, ALU.max))
                step(v.tensor_tensor(AS[:, 3, 0:4], sink, AS[:, 0, 0:4], SUB))
                v.tensor_scalar(AS[:, 1, 0:4], AS[:, 0, 0:4], -1.0, None, MUL).then_inc(sc_ready, 1)
                dve.wait_ge(p_exp, 5 * (j + 1))
                step(v.tensor_tensor(AS[:, 4, 0:4], AS[:, 2, 0:4], AS[:, 3, 0:4], ADD))
                step(v.reciprocal(AS[:, 4, 0:4], AS[:, 4, 0:4]))
                v.tensor_tensor(sb, sb, AS[:, 4, 0:4].unsqueeze(2).broadcast_to([P, 4, 256 - lo]), MUL) \
                    .then_inc(p_ready, 1)

            def pool(g):
                src = UPD[:, 0, :]
                for i in range(g + 1):
                    dst = UPD[:, 1 + i % 2, :]
                    sh = 1 << i
                    step(v.tensor_tensor(dst[:, 16:], src[:, 16:], src[:, 16 - sh:16 + S - sh], ADD))
                    src = dst
                step(v.scalar_tensor_tensor(out=PL[:, g, :], in0=src[:, 16:], scalar=0.5 ** (g + 1),
                                            in1=UPD[:, 0, 16:], op0=MUL, op1=SUB))
                step(v.tensor_tensor(src[:, 16:32], src[:, 16:32], ITAB[:, g, :], MUL))
                v.tensor_tensor(PL[:, g, 0:16], src[:, 16:32], UPD[:, 0, 16:32], SUB).then_inc(pool_ready, 1)

            dve.wait_ge(ali_in, 64)
            for u in range(U5, U6):
                n = u - U5
                j = n - 6
                if 0 <= j < 8:
                    scores(j)
                tile_done(u)
                if n == 0:
                    dve.wait_ge(rstd_ready, 4)
                bank = PS[:, (M5 + n) % 4, :]
                dst = (QS[:, n, :] if n < 4 else KS[:, :] if n == 4 else SQ3[:, 0, :] if n == 5 else
                       GA[:, n - 6, :] if n < 10 else UPD[:, 0, 16:] if n < 14 else GB[:, n - 14, :])
                v.tensor_tensor(dst, bank, RSTD[:, :], MUL).then_inc(bank_free, 1)
                if 10 <= n < 14:
                    dve.wait_ge(bank_free, M5 + n + 1)
                    pool(n - 10)
                if n == 16:
                    dve.wait_ge(ov_taken, 8)
                    dve.wait_ge(gate_done, 3)
                    for t in range(4):
                        v.tensor_tensor(MIXF[:, t, :], MIXF[:, t, :], GA[:, t, :], MUL).then_inc(op_src, 1)
                    for t in range(4):
                        operand_lo(32 + t, MIXF[:, t, :], XB[:, t, 1, :], XB[:, t, 0, :])
            dve.wait_ge(py_taken, 4)
            for g in range(5):
                if g < 4:
                    dve.wait_ge(gate_done, 4 + g)
                    v.tensor_tensor(MIXF[:, 4 + g, :], PL[:, g, :], GB[:, g, :], MUL).then_inc(op_src, 1)
                if g >= 1:
                    operand_lo(36 + g - 1, MIXF[:, 3 + g, :], XB[:, 3 + g, 1, :], XB[:, 3 + g, 0, :])

            def post(st, name, f, yt):
                dve.wait_ge(rstd_ready, st + 1)
                for k in range(KT + 1):
                    if k < KT:
                        step(v.scalar_tensor_tensor(out=yt[:, k % 2, :], in0=Y[:, k, :], scalar=vec(name, k),
                                                    in1=RSTD[:, :], op0=MUL, op1=MUL))
                        v.tensor_tensor(RES[:, k, :], RES[:, k, :], yt[:, k % 2, :], ADD).then_inc(op_src, 1)
                    if k >= 1:
                        q = k - 1
                        dve.wait_ge(op_src, 32 + k)
                        operand_lo(f + q, RES[:, q, :], XA[:, q, 1, :], XA[:, q, 0, :], vec("pre1", q))
                        accumulate(5, q, SQ3[:, q % 2, :])

            for k in range(KT):
                tile_done(U6 + k)
                v.tensor_copy(Y[:, k, :], PS[:, (M6 + k) % 4, :]).then_inc(bank_free, 1)
                if k >= 1:
                    accumulate(4, k - 1, SQ3[:, (k - 1) % 2, :])
            accumulate(4, KT - 1, SQ3[:, (KT - 1) % 2, :])
            post(4, "post0", 40, YT)

            step(v.memset(GLU[:, :, 0:CK - 1], 0.0))
            tap_at = [0]

            todo = [(k, i) for k in range(KT) for i in range(CK - PE_TAPS[k] + 1)]

            def taps(n, tiles):
                for _ in range(n):
                    if tap_at[0] == len(todo) or todo[tap_at[0]][0] >= tiles:
                        return
                    k, i = todo[tap_at[0]]
                    tap_at[0] += 1
                    x = GLU[:, k, i:i + S]
                    w = DCW[:, i, k:k + 1]
                    if i == 0:
                        step(v.tensor_scalar(CV[:, k, :], x, w, vec("dw_b", k), MUL, ADD))
                    elif i < CK - PE_TAPS[k]:
                        step(v.scalar_tensor_tensor(out=CV[:, k, :], in0=x, scalar=w, in1=CV[:, k, :],
                                                    op0=MUL, op1=ADD))
                    else:
                        dve.wait_ge(cv_filled, k + 1)
                        v.tensor_tensor(CV[:, k, :], CV[:, k, :], PS[:, 4 + k % 3, :], ADD) \
                            .then_inc(cv_ready, 1)

            for u in range(U7, U8):
                n = u - U7
                tile_done(u)
                if n == 0:
                    dve.wait_ge(rstd_ready, 6)
                bank = PS[:, (M7 + n) % 4, :]
                dst = ABUF[:, n % 4, :] if n < 16 else GT3[:, n - 16, :]
                if n < 16 and n % 4 >= 2:
                    v.tensor_tensor(dst, bank, RSTD[:, :], MUL).then_inc(bank_free, 1)
                    dve.wait_ge(bank_free, M7 + n + 1)
                    k = 2 * (n // 4) + n % 4 - 2
                    dve.wait_ge(sig_done, k + 1)
                    v.tensor_tensor(GLU[:, k, CK - 1:], ABUF[:, n % 4 - 2, :], dst, MUL) \
                        .then_inc(glu_ready, 1)
                else:
                    v.tensor_tensor(dst, bank, RSTD[:, :], MUL).then_inc(bank_free, 1)
                tiles = min(2 * (n // 4) + max(n % 4 - 1, 0), KT)
                if n >= 2:
                    dve.wait_ge(glu_ready, tiles)
                taps(9, tiles)
            taps(CK * KT, KT)
            dve.wait_ge(cv_ready, KT)
            dve.wait_ge(cm_filled, 1)
            for k in range(KT):
                v.scalar_tensor_tensor(out=CV[:, k, :], in0=PS[:, 7, :], scalar=-1.0 / D, in1=CV[:, k, :],
                                       op0=MUL, op1=ADD).then_inc(cm_taken, 1)
            dve.wait_ge(rstd_ready, 7)
            dve.wait_ge(gate_done, 16 - 1)
            for k in range(KT + 2):
                if k < KT:
                    v.scalar_tensor_tensor(out=CV[:, k, :], in0=CV[:, k, :], scalar=vec("ln_g", k),
                                           in1=RSTD[:, :], op0=MUL, op1=MUL).then_inc(ln_in, 1)
                if 1 <= k <= KT:
                    dve.wait_ge(ln_done, k)
                    v.tensor_tensor(CV[:, k - 1, :], CV[:, k - 1, :], GT3[:, k - 1, :], MUL) \
                        .then_inc(op_src, 1)
                if k >= 2:
                    operand_lo(48 + k - 2, CV[:, k - 2, :], XB[:, k - 2, 1, :], XB[:, k - 2, 0, :])

            dve.wait_ge(wpost_in, 16)
            for g in range(2):
                for b in range(NB):
                    dve.wait_ge(ysq_done, 4 * g + b + 1)
                    v.tensor_tensor(YTOK[:, b, g * 512:(g + 1) * 512], PS[:, (M8 + b) % 4, :],
                                    WPOST[:, g * 512:(g + 1) * 512], MUL).then_inc(bank_free, 1)
            dve.wait_ge(ysq_done, 8)
            v.tensor_tensor(AS[:, 1, 0:4], AS[:, 0, 0:4], AS[:, 0, 4:8], ADD).then_inc(yss_ready, 1)
            dve.wait_ge(ysd_ready, 1)
            step(v.reciprocal(AS[:, 3, 0:4], AS[:, 2, 0:4]))
            dve.wait_ge(bank_free, M8 + 8)
            dve.wait_ge(rest_taken, KT)
            for b in range(NB):
                for g in range(2):
                    y = YTOK[:, b, g * 512:(g + 1) * 512]
                    v.scalar_tensor_tensor(out=y, in0=y, scalar=AS[:, 3, b:b + 1],
                                           in1=REST[:, b, g * 512:(g + 1) * 512],
                                           op0=MUL, op1=ADD).then_inc(ot_ready, 1)

        @block.tensor
        def _(pe):
            mm, tr = nc.tensor.matmul, nc.tensor.transpose

            def operand(f):
                pe.wait_ge(op_hi, f + 1)
                pe.wait_ge(op_lo, f + 1)

            def three(out, w_hi_, w_lo_, x_hi_, x_lo_, first, last):
                mm(out, w_hi_, x_hi_, start=first, stop=False)
                mm(out, w_hi_, x_lo_, start=False, stop=False)
                return mm(out, w_lo_, x_hi_, start=False, stop=last)

            def half_unit(n, out, X, k0, kn, first, last, fill=None, later=None):
                for s_ in (w_hi, w_lo):
                    pe.wait_ge(s_, n + 1 if later is None else later + (n + 1))
                for k in range(kn):
                    if fill is not None:
                        operand(8 * fill + k0 + k)
                    ins = three(out, WH[:, n % 4, k, :], WL[:, n % 4, k, :],
                                X[:, k0 + k, 0, :], X[:, k0 + k, 1, :],
                                first and k == 0, last and k == kn - 1)
                ins.then_inc(half_done, 1)

            def deltanet_ssq():
                pe.wait_ge(rsq_ready, 2)
                pe.wait_ge(tokk_ready, 4)
                pe.wait_ge(tokv_ready, 16)
                pe.wait_ge(o_ready, 4)
                for h in range(H):
                    ins = mm(PS[:, 4 + h, :], ONES[:, :], RR[:, h, :], start=True, stop=True)
                ins.then_inc(rssq_filled, 1)

            def unit(u, m, X, fill=None, later=None, mlater=None, midway=None):
                for q in QUADS:
                    if 0 <= u - q < 4:
                        if u == q:
                            for j in range(4):
                                pe.wait_ge(bank_free, m + j - 3)
                                half_unit(2 * q + j, PS[:, (m + j) % 4, :], X, 0, 4, True, False,
                                          fill if j == 0 else None)
                                if j == 1 and u == U2:
                                    deltanet_ssq()
                            if midway is not None:
                                stat(midway)
                        half_unit(2 * q + 4 + u - q, PS[:, m % 4, :], X, 4, 4, False, True,
                                  fill if u == q else None)
                        return
                if m >= 4:
                    pe.wait_ge(bank_free, m - 3 if mlater is None else mlater + (m - 3))
                out = PS[:, m % 4, :]
                half_unit(2 * u, out, X, 0, 4, True, False, fill, later)
                half_unit(2 * u + 1, out, X, 4, 4, False, True, fill, later)

            def wide_half(n, X, fill=None, last_of=None):
                q0 = max(q for q in WIDE if q <= n // 2)
                k = n - 2 * q0
                m = q0 if q0 < U2 else M8 + q0 - U8
                for s_ in (w_hi, w_lo):
                    pe.wait_ge(s_, n + 1)
                if fill is not None:
                    operand(8 * fill + k)
                w, wl = (r[:, n % 4, :, :].rearrange("p t c -> p (t c)") for r in (WH, WL))
                for b in range(NB):
                    if k == 0:
                        pe.wait_ge(bank_free, m + b - 3)
                    xh, xl = (X[:, k, q, b * P:(b + 1) * P] for q in range(2))
                    ins = three(PS[:, (m + b) % 4, :], xh, xl, w, wl, k == 0, k == KT - 1)
                    if k == KT - 1 and b < NB - 1 and last_of is not None:
                        ins.then_inc(last_of, 1)
                ins.then_inc(half_done, 1)

            def stat(st):
                pe.wait_ge(acc_done, 8 * (acc_round(st) + 1))
                mm(PS[:, 7, :], ONES[:, :], ACC[:, :], start=True, stop=True).then_inc(stat_filled, 1)

            def rstd_columns(n):
                pe.wait_ge(rstd_ready, n)
                for b in range(NB):
                    ins = mm(PS[:, 6, b:b + 1], RSTD[0:1, b * P:(b + 1) * P], ONES[0:1, 0:1],
                             start=True, stop=True)
                return ins

            pe.wait_ge(c_in, 16 * 18)
            pe.wait_ge(ones_ready, 5)
            c = 0
            for slot, n, bank in ((0, NVEC, 0), (1, 48, 0), (2, 66, 0), (5, 66, 0), (3, 124, 1), (4, 124, 1)):
                if slot == 3:
                    c = 0
                ins = tr(PS[:, bank, c:c + n], ROWS[0:n, slot, :], IDENT[0:n, 0:n])
                c += n
            ins.then_inc(par_filled, 1)
            pe.wait_ge(x_in, 16 * NB)
            for k in range(KT):
                if k >= 4:
                    pe.wait_ge(op_src, k - 3)
                for b in range(NB):
                    ins = tr(PS[:, 4 + k % 4, b * P:(b + 1) * P], XTOK[:, b, k * P:(k + 1) * P], IDENT[:, :])
                ins.then_inc(xt_filled, 1)
            pe.wait_ge(par_ready, 4)

            def ret_head(h):
                if h >= 1:
                    pe.wait_ge(ro_ready, h)
                if h == 0 or h == 2:
                    pe.wait_ge(rot_ready, 3 if h == 0 else 7)
                if h == 1 or h == 3:
                    pe.wait_ge(rot_ready, 4 if h == 1 else 8)

                def score(jb):
                    if 4 * h + jb >= 2:
                        pe.wait_ge(rs_ready, 4 * h + jb - 1)
                    mm(PS[:, 4 + jb % 2, 0:S - jb * P], RK[:, h % 2, jb * P:(jb + 1) * P],
                       RQ[:, h % 2, jb * P:], start=True, stop=True).then_inc(rs_filled, 1)

                def value(jb):
                    pe.wait_ge(rs_ready, 4 * h + jb + 1)
                    ins = mm(PS[:, 6, jb * P:], RV[:, h, jb, :], RS[:, jb % 2, 0:S - jb * P],
                             start=(jb == 0), stop=(jb == NB - 1))
                    if jb == NB - 1:
                        ins.then_inc(ro_filled, 1)

                score(0)
                for jb in range(1, NB):
                    score(jb)
                    value(jb - 1)
                value(NB - 1)

            def level(l):
                s = 2 << l
                def half(ap, two):
                    return ap.rearrange("p (b two s) -> p b two s", two=2, s=s)[:, :, two, :]
                for c in range(NB):
                    if l == 0 and c == 0:
                        pe.wait_ge(t2_ready, 1)
                        pe.wait_ge(tt_ready, 1)
                    if l > 0:
                        pe.wait_ge(upd_done, 4 * (l - 1) + c + 1)
                    for h in range(H):
                        a_ = 4 * c + h
                        ins = mm(PS[:, 4 + c, h * 64:(h + 1) * 64], M[:, a_, :], half(TT[:, a_, :], 1),
                                 start=True, stop=True)
                    ins.then_inc(xp_filled, 1)
                for c in range(NB):
                    pe.wait_ge(xs_ready, 4 * l + c + 1)
                    pe.wait_ge(xz_ready, 4 * l + c + 1)
                    for h in range(H):
                        a_ = 4 * c + h
                        ins = mm(PS[:, 4 + c, 256 + h * 64:256 + (h + 1) * 64], T[:, a_, :],
                                 half(XZ[:, c, h, :], 1), start=True, stop=True)
                        if l < 5:
                            ins = mm(PS[:, 4 + c, h * 64:(h + 1) * 64], XZ[:, c, h, :],
                                     half(T[:, a_, :], 0), start=True, stop=True)
                    ins.then_inc(txp_filled, 1)

            def by_token(c):
                if c >= 1:
                    pe.wait_ge(tokk_ready, c)
                    pe.wait_ge(tokv_ready, 4 * c)
                for j, bank in ((0, 4), (1, 5)):
                    for h in range(H):
                        src = KQ[:, h, 0, c * P:(c + 1) * P] if j == 0 else V[:, h, c * P:(c + 1) * P]
                        ins = tr(PS[:, bank, h * P:(h + 1) * P], src, IDENT[:, :])
                    ins.then_inc(tok_filled, 1)

            def weights_t(c):
                pe.wait_ge(tokk_ready, c + 1)
                pe.wait_ge(o_ready, c)
                for h in range(H):
                    ins = mm(PS[:, 6, h * P:(h + 1) * P], KB[:, h, :], TT[:, 4 * c + h, :], start=True, stop=True)
                ins.then_inc(nw_filled, 1)

            def new_values(c):
                pe.wait_ge(tokv_ready, 4 * (c + 1))
                if c >= 1:
                    pe.wait_ge(nw_ready, c)
                    pe.wait_ge(s_ready, c)
                for h in range(H):
                    o = PS[:, 7, h * P:(h + 1) * P]
                    ins = mm(o, TT[:, 4 * c + h, :], VB[:, h, :], start=True, stop=(c == 0))
                    if c >= 1:
                        ins = mm(o, NW[:, h, :], ST8[:, h, :], start=False, stop=True)
                ins.then_inc(u_filled, 1)

            def out_and_state(c):
                pe.wait_ge(u_ready, c + 1)
                if c >= 1:
                    pe.wait_ge(qd_ready, c)
                    pe.wait_ge(nw_ready, c)
                else:
                    pe.wait_ge(ro_ready, 4)
                for h in range(H):
                    o = PS[:, 6, h * P:(h + 1) * P]
                    ins = mm(o, UU[:, h, :], QKT[:, 4 * c + h, :], start=True, stop=(c == 0))
                    if c >= 1:
                        ins = mm(o, ST8[:, h, :], QD[:, h, :], start=False, stop=True)
                ins.then_inc(so_filled, 1)
                if c < NB - 1:
                    if c == 0:
                        pe.wait_ge(tokk_ready, 1)
                    for h in range(H):
                        ins = mm(PS[:, 7, h * P:(h + 1) * P], KD[:, h, :], UU[:, h, :], start=True, stop=True)
                    ins.then_inc(so_filled, 1)

            def ret_ssq(r):
                pe.wait_ge(rsq_ready, 1)
                pe.wait_ge(tokk_ready, r + 1)
                pe.wait_ge(tokv_ready, 4 * (r + 1))
                for h in range(2):
                    ins = mm(PS[:, 4 + h, :], ONES[:, :], RR[:, 2 * r + h, :], start=True, stop=True)
                ins.then_inc(rssq_filled, 1)

            for u in range(U1, U2):
                if 12 <= u < 16:
                    wide_half(2 * u, XA)
                    wide_half(2 * u + 1, XA)
                else:
                    unit(u, u, XA, fill=0 if u == 0 else None)
                if u == 0:
                    stat(0)
                if u == 3:
                    pe.wait_ge(ab_split, 2)
                    pe.wait_ge(rstd_ready, 1)
                    for k in range(KT):
                        ins = three(PS[0:8, 7, :], ABH[:, k, :], ABL[:, k, :], XA[:, k, 0, :], XA[:, k, 1, :],
                                    k == 0, k == KT - 1)
                    ins.then_inc(ab_filled, 1)
                if u == 4:
                    pe.wait_ge(ab_rows, 1)
                    rstd_columns(1)
                    for c in range(NB):
                        ins = tr(PS[:, 7, 8 * c:8 * c + 8], AB[:, c * P:(c + 1) * P], IDENT[0:8, 0:8])
                    ins.then_inc(abt_filled, 1)
                if u == 12 or u == 13:
                    pe.wait_ge(sqk, u - 11)
                    pe.wait_ge(sp_in, 1)
                    pe.wait_ge(rcol_ready, 1)
                    if u == 13:
                        pe.wait_ge(r4_ready, 1)
                        pe.wait_ge(gu_ready, 1)
                        mm(PS[:, 4, 0:16], UPPER, GG, start=True, stop=True).then_inc(gc_filled, 1)
                    for h in (1, 2, 3, 0):
                        if h == 0 and u == 13:
                            pe.wait_ge(gc_ready, 1)
                        ins = mm(PS[:, 4 + h, :], ONES[:, :], SQ4[:, h, :], start=True, stop=True)
                    ins.then_inc(ssq_filled, 1)
                if u == 14:
                    pe.wait_ge(r4_ready, 2)
                    for c in range(NB):
                        ins = mm(PS[:, 4 + c, :], ONES[:, :],
                                 T[:, 4 * c:4 * c + 4, :].rearrange("p h i -> p (h i)"), start=True, stop=True)
                    ins.then_inc(gcb_filled, 1)
                if u == 15 or u == 16:
                    if u == 15:
                        pe.wait_ge(x1_ready, 1)
                        pe.wait_ge(kq_normed, 2)
                    else:
                        pe.wait_ge(m_ready, 1)
                    for c in range(NB):
                        for h in range(H):
                            ins = mm(PS[:, 4 + c, h * P:(h + 1) * P], KQ[:, h, 0, c * P:(c + 1) * P],
                                     KQ[:, h, u - 15, c * P:(c + 1) * P], start=True, stop=True)
                    ins.then_inc(g_filled if u == 15 else qk_filled, 1)
                if u == 17:
                    pe.wait_ge(qkt_ready, 1)
                    pe.wait_ge(t2_ready, 1)
                    for a_ in range(16):
                        ins = tr(PS[:, 4 + a_ // 4, (a_ % 4) * P:(a_ % 4 + 1) * P], T[:, a_, :], IDENT[:, :])
                    ins.then_inc(tt_filled, 1)
                if 18 <= u <= 23:
                    heads = sum(g < u for g in RET_GAP)
                    if heads:
                        pe.wait_ge(ro_ready, heads)
                        pe.wait_ge(rs_ready, 4 * heads)
                    level(u - 18)
                if u in RET_GAP:
                    pe.wait_ge(upd_done, 4 * min(u - 17, 6))
                    ret_head(RET_GAP.index(u))
                if u == 24:
                    pe.wait_ge(rs_ready, 16)
                    by_token(0)
                if u == 25:
                    ret_ssq(0)
                if u == 26:
                    new_values(0)
                    pe.wait_ge(rr_ready, 1)
                    by_token(1)
                    out_and_state(0)
                if u == 27:
                    weights_t(1)
                    ret_ssq(1)
                if u == 28:
                    new_values(1)
                    pe.wait_ge(rr_ready, 2)
                    by_token(2)
                    out_and_state(1)
                if u == 29:
                    weights_t(2)
                if u == 30:
                    new_values(2)
                    by_token(3)
                    out_and_state(2)
                if u == 31:
                    weights_t(3)
                    new_values(3)
                    out_and_state(3)
            for k in range(KT):
                unit(U2 + k, M2 + k, XA, fill=1 if k == 0 else None)
                if k == 0:
                    pe.wait_ge(x2_in, 16 * NB)
                    pe.wait_ge(rr_ready, 3)
                if k >= 4:
                    pe.wait_ge(xt_taken, k - 3)
                for b in range(NB):
                    ins = tr(PS[:, 4 + k % 4, b * P:(b + 1) * P], XTOK2[:, b, k * P:(k + 1) * P], IDENT[:, :])
                ins.then_inc(xt_filled, 1)
            pe.wait_ge(xt_taken, KT)
            stat(1)
            operand(23)
            with pe.Fori(0, 11) as i:
                for j in range(4):
                    unit(U3 + j, M3 + j, XB, later=i * 8, mlater=i * 4)
            pe.wait_ge(ff_hi, 16)
            pe.wait_ge(ff_lo, 16)
            with pe.Fori(0, 2) as i:
                for j in range(12):
                    g, t, o = j // 2 % 3, j % 2, j // 6
                    m = M4 + 2 * o + t
                    if g == 0:
                        pe.wait_ge(bank_free, i * 4 + (m - 3))
                    if g == 2:
                        pe.wait_ge(ff_hi, FT)
                        pe.wait_ge(ff_lo, FT)
                    kn = 4 if g < 2 else 3
                    for hf in range(2):
                        half_unit(2 * (U4 + j) + hf, PS[:, m % 4, :], ACTS, 8 * g + kn * hf, kn,
                                  g == 0 and hf == 0, g == 2 and hf == 1, later=i * 24)
            stat(2)

            def probs_t(j):
                pe.wait_ge(p_ready, j + 1)
                if j >= 1:
                    pe.wait_ge(ov_taken, j)
                else:
                    pe.wait_ge(vt_ready, 1)
                for t in range(4):
                    for w in range(1 if j < 2 else 0, 2):
                        ins = tr(PS[:, 6 + t // 2, (2 * (t % 2) + w) * P:(2 * (t % 2) + w + 1) * P],
                                 SB[:, j % 2, t, w * P:(w + 1) * P], IDENT[:, :])
                ins.then_inc(pt_filled, 1)

            def scores(j):
                b, kv = j // 2, j % 2
                r = slice(kv * HD2, (kv + 1) * HD2)
                if j >= 1:
                    pe.wait_ge(sc_ready, j)
                for t in range(4):
                    lo = 0 if b else P
                    ins = mm(PS[:, 4 + t // 2, (t % 2) * 256 + lo:(t % 2 + 1) * 256],
                             QS[r, t, b * P:(b + 1) * P], KS[r, (b - 1) * P + lo:(b + 1) * P],
                             start=True, stop=True)
                ins.then_inc(sc_filled, 1)

            def values(j):
                b, kv = j // 2, j % 2
                r = slice(kv * HD2, (kv + 1) * HD2)
                pe.wait_ge(pt_ready, j + 1)
                for w in range(0 if b else 1, 2):
                    ins = mm(PS[r, 6, :], VS[:, b - 1 + w, r], PTS[:, :, w, :],
                             start=(w == (0 if b else 1)), stop=(w == 1))
                ins.then_inc(ov_filled, 1)

            for u in range(U5, U6):
                n = u - U5
                unit(u, M5 + n, XA, fill=3 if n == 0 else None, midway=3)
                j = n - 6
                if j == 0:
                    pe.wait_ge(bank_free, M5 + 6)
                    pe.wait_ge(rstd_ready, 4)
                    for b in range(NB):
                        ins = tr(PS[:, 7, b * P:(b + 1) * P], SQ3[:, 0, b * P:(b + 1) * P], IDENT[:, :])
                    ins.then_inc(vt_filled, 1)
                if 1 <= j <= 8:
                    probs_t(j - 1)
                if 0 <= j < 8:
                    scores(j)
                if 1 <= j <= 8:
                    values(j - 1)
                if j == 9:
                    pe.wait_ge(ali_in, 64)
                    pe.wait_ge(pool_ready, 4)
                    pe.wait_ge(ov_taken, 8)
                    for g in range(4):
                        ins = mm(PS[:, 4 + g, :], PW[:, g, :], PL[:, g, :], start=True, stop=True)
                    ins.then_inc(py_filled, 1)
            for k in range(KT):
                unit(U6 + k, M6 + k, XB, fill=4 if k == 0 else None)
            pe.wait_ge(py_taken, 4)
            stat(4)

            def conv_part(k):
                pe.wait_ge(glu_ready, k + 1)
                pe.wait_ge(diag_ready, k + 1)
                if k >= 3:
                    pe.wait_ge(cv_ready, k - 2)
                else:
                    pe.wait_ge(py_taken, 4)
                n = PE_TAPS[k]
                for t in range(n):
                    i = CK - n + t
                    ins = mm(PS[:, 4 + k % 3, :], DG[:, sum(PE_TAPS[:k]) + t, :], GLU[:, k, i:i + S],
                             start=(t == 0), stop=(t == n - 1))
                ins.then_inc(cv_filled, 1)

            conv_after = {4 * (k // 2) + 4 + k % 2: k for k in range(KT - 2)}
            conv_after[20], conv_after[22] = KT - 2, KT - 1
            for n in range(24):
                unit(U7 + n, M7 + n, XA, fill=5 if n == 0 else None, midway=5)
                if n in conv_after:
                    conv_part(conv_after[n])
            pe.wait_ge(rstd_ready, 6)
            for k in range(KT):
                pe.wait_ge(cv_ready, k + 1)
                ins = mm(PS[:, 7, :], ONES[:, :], CV[:, k, :], start=(k == 0), stop=(k == KT - 1))
            ins.then_inc(cm_filled, 1)
            for k in range(KT):
                pe.wait_ge(sq_ready, 48 + k + 1)
                ins = mm(PS[:, 6, :], ONES[:, :], CT[:, k % 2, :], start=(k == 0), stop=(k == KT - 1))
                ins.then_inc(ln_added, 1)

            def x_by_token(k):
                if k >= 4:
                    pe.wait_ge(rest_taken, k - 3)
                for b in range(NB):
                    ins = tr(PS[:, REST_BANK[k % 4], b * P:(b + 1) * P], RES[:, k, b * P:(b + 1) * P],
                             IDENT[:, :])
                ins.then_inc(rest_filled, 1)

            pe.wait_ge(cm_taken, KT)
            for k in range(3):
                x_by_token(k)
            pe.wait_ge(rstd_ready, 7)
            x_by_token(3)
            for g in range(2):
                for k in range(KT):
                    wide_half(2 * (U8 + 4 * g) + k, XB, fill=6 if g == 0 else None, last_of=y_done)
                if g == 0:
                    for k in range(4, KT):
                        x_by_token(k)


def constants():
    f = np.float32
    i, j = np.arange(P)[:, None], np.arange(P)[None, :]
    masks = [(i <= j).astype(f), (j < i).astype(f), ((i % 2 == 1) & (j == i - 1)).astype(f)]
    for level in range(6):
        s = 2 << level
        second = np.array([c for c in range(P) if c // s % 2 == 1])[None, :]
        masks.append(((i // s % 2 == 0) & (i // (2 * s) == second // (2 * s))).astype(f))
    angle = f(1.0) / f(10000.0) ** np.linspace(0.0, 1.0, P // 2, dtype=f)
    phase = (np.arange(S, dtype=f)[None, :] * np.repeat(angle, 2)[:, None]).astype(f).astype(np.float64)
    sign = np.where(np.arange(P) % 2 == 0, -1.0, 1.0)[:, None]
    log_gamma = np.log(1.0 - 2.0 ** (-5.0 - np.arange(H)))
    off = np.arange(S)[None, :] - np.arange(P)[:, None]
    decay = np.where(off >= 0, np.exp(np.maximum(off, 0)[None] * log_gamma[:, None, None]), 0.0) * P ** -0.5
    dist = np.arange(P)[:, None] + P - np.arange(256)[None, :]
    slopes = 2.0 ** (-np.arange(1, QH + 1, dtype=np.float64))
    ok = (dist >= 0) & (dist < P)
    alibi = np.where(ok[:, None, :], -slopes[None, :, None] * dist[:, None, :], NEG)
    cnt = np.minimum(np.arange(16)[None, :] + 1, np.array([2, 4, 8, 16])[:, None])
    return {
        "ident": np.eye(P, dtype=f),
        "masks": np.concatenate(masks, 1),
        "cos_sin": np.stack([np.cos(phase), np.sin(phase) * sign], 1).astype(f),
        "ret_decay": decay.transpose(1, 0, 2).astype(f),
        "alibi": alibi.astype(f),
        "inv_cnt": np.broadcast_to((1.0 / cnt).astype(f)[None], (P, 4, 16)).copy(),
    }


_INS = ["x", "attn_norm_w", "w_in", "gdn_conv_w", "gdn_a_log", "gdn_dt_bias", "gdn_norm_w", "w_out",
        "mlp_norm_w", "w_up", "mlp_conv_w", "w_down", "final_norm_w", "pre_norm_2", "post_norm_2",
        "a_w_in_2", "a_sinks_2", "b_pool_w_2", "b_pool_scale_2", "ab_w_out_2", "c_w_in_2", "c_dw_w_2",
        "c_dw_b_2", "c_ln_g_2", "c_ln_b_2", "c_w_out_2"]


def kernel(**inputs):
    import concourse.bacc as bacc
    from concourse.bass_utils import run_bass_kernel_spmd as run

    nc = bacc.Bacc("TRN2", target_bir_lowering=False, num_devices=1)
    arrays, a, const = {}, {}, {}
    for name in _INS:
        x = np.ascontiguousarray(inputs[name])
        arrays["in_" + name] = x
        a[name] = nc.dram_tensor("in_" + name, x.shape, F32, kind="ExternalInput").ap()
    for name, x in constants().items():
        arrays["const_" + name] = x
        const[name] = nc.dram_tensor("const_" + name, x.shape, F32, kind="ExternalInput").ap()
    out = nc.dram_tensor("result", (1, S, D), F32, kind="ExternalOutput").ap()
    build(nc, a, const, out)
    r = run(nc, [arrays], core_ids=[0])
    return r.results[0]["result"]
```

```python
import math
from contextlib import ExitStack

import numpy as np

import concourse.bass as bass
from concourse import mybir

P = 128
S = 512
D = 1024
KT = D // P
NB = S // P
H = 4
GW = H * P
IN_COLS = 8 * GW + 2 * H
DFF = 2816
FT = DFF // P
EPS = 1e-6
EXP_SET = 0
LN_EXP_SET = 6
SQRT_SET = 3
SILU_SET = 18
EVEN_IN = 2304
QH = 8
HD2 = 64
CK = 31
NEG = -1e30

F32 = mybir.dt.float32
F32R = mybir.dt.float32r
ACT = mybir.ActivationFunctionType
ALU = mybir.AluOpType
AX = mybir.AxisListType
MUL, ADD, SUB = ALU.mult, ALU.add, ALU.subtract

VECS = [("attn_norm_w", 8), ("mlp_norm_w", 8), ("final_norm_w", 8), ("pre0", 8), ("pre1", 8),
        ("post0", 8), ("post1", 8), ("pool_scale", 4), ("dw_b", 8), ("ln_g", 8), ("ln_b", 8),
        ("gdn_norm_w", 1)]
VEC_AT, _n = {}, 0
for _name, _rows in VECS:
    VEC_AT[_name] = _n
    _n += _rows
NVEC = _n

U1, U2, U3, U4, U5, U6, U7, U8 = 0, 32, 40, 84, 108, 126, 134, 158
UNITS = 166
M1, M2, M3, M4, M5, M6, M7, M8 = 0, 32, 40, 84, 92, 110, 118, 142
PAIRS = UNITS // 2
FILL = {1: 0, 2: 1, 3: 2, 5: 3, 6: 4, 7: 5, 8: 6}
PE_TAPS = [4, 5, 5, 6, 6, 6, 7, 7]
REST_BANK = [4, 5, 7, 6]
RET_GAP = [19, 20, 23, 24]


QUADS = (U1, U2, U5, U6, U7)
SPLIT_AT = [3, 5, 7]
SUM_AT = [U7 + n for n in (13, 15, 18, 21, 22, 23)]
POOL_SQUARES = 5
SHIFTED_BY_DVE = 3
WIDE = (12, U8, U8 + 4)


def unit_half(n):
    for q in QUADS:
        if 0 <= n - 2 * q < 8:
            return q + (n - 2 * q) % 4, (n - 2 * q) // 4
    return n // 2, n % 2


def halves_when_done(u):
    for q in QUADS:
        if 0 <= u - q < 4:
            return 2 * q + 5 + u - q
    for q in WIDE:
        if 0 <= u - q < 4:
            return 2 * q + 8
    return 2 * u + 2


def wide(u):
    return any(0 <= u - q < 4 for q in WIDE)


def split_when_free(p):
    return 4 * p - 2 if 2 * (p - 2) in QUADS else 4 * (p - 1)


def loads_before(p):
    n = 0
    for q in range(p % 2, p + 1, 2):
        n += 3 if U6 <= 2 * q < U7 else 2
    return n


def build(nc, a, const, out, x_t):
    ctx = ExitStack()
    with ctx:
        base = (nc.sbuf_base + 31) // 32 * 32

        def at(name, shape, dt, off):
            return nc.alloc_sbuf_tensor_at(name, shape, dt, offset=base + off)

        def sem(name):
            return ctx.enter_context(nc.semaphore(name))

        RAW = at("raw", [P, 2, KT, 256], F32, 0)
        WH = at("w_hi", [P, 4, 4, P], F32R, 16384)
        WL = at("w_lo", [P, 4, 4, P], F32R, 24576)
        XA = at("x_a", [P, KT, 2, S], F32R, 32768)
        AR = 65536
        G = 204800
        IDENT = at("ident", [P, P], F32, G)
        ONES = at("ones", [P, P], F32, G + 512)
        RSTD = at("rstd", [P, S], F32, G + 1024)
        ACC = at("acc", [P, S], F32, G + 3072)
        VEC = at("vec", [P, NVEC], F32, G + 5120)
        GCW = at("gdn_conv", [P, 4, 12], F32, G + 5120 + 352)
        MCW = at("mlp_conv", [P, 3, 44], F32, G + 5664)
        DCW = at("dw_conv", [P, CK, KT], F32, G + 6208)
        RCOL = at("rstd_col", [P, NB], F32, G + 7200)
        CB = at("const_bias", [P, 4], F32, G + 7232)

        KQ = at("kq", [P, H, 2, S], F32, AR)
        ROWS = at("rows", [P, 6, P], F32, AR)
        V = at("v", [P, H, S], F32, AR + 16384)
        RV = at("ret_v", [P, H, NB, P], F32, AR + 24576)
        XTOK = at("x_tok", [P, NB, D], F32, AR + 32768)
        XT = at("x_t", [P, KT, S], F32, AR + 16384)
        GT = at("gates", [P, 8, S], F32, AR + 32768)
        M = at("m", [P, NB * H, P], F32, AR + 32768)
        T = at("t", [P, NB * H, P], F32, AR + 40960)
        TT = at("tt", [P, NB * H, P], F32, AR + 49152)
        QKT = at("qkt", [P, NB * H, P], F32, AR + 57344)
        R4 = at("r4", [P, H, S], F32, AR + 57344)
        EB = at("eb", [P, NB * H, P], F32, AR + 65536)
        SQ4 = at("sq4", [P, H, S], F32, AR + 65536)
        XZ = at("xz", [P, NB, H, P], F32, AR + 73728)
        LB = at("lb", [P, NB * H, P], F32, AR + 73728)
        RR = at("rr", [P, H, S], F32, AR + 73728)
        VB = at("vb", [P, H, P], F32, AR + 81920)
        KB = at("kb", [P, H, P], F32, AR + 83968)
        KD = at("kd", [P, H, P], F32, AR + 86016)
        NW = at("nw", [P, H, P], F32, AR + 88064)
        UU = at("uu", [P, H, P], F32, AR + 90112)
        QD = at("qd", [P, H, P], F32, AR + 92160)
        ST8 = at("state", [P, H, P], F32, AR + 94208)
        CS = at("cos_sin", [P, 2, S], F32, AR + 96256)
        DR = at("ret_decay", [P, H, S], F32, AR + 100352)
        RQ = at("rq", [P, 2, S], F32, AR + 108544)
        RK = at("rk", [P, 2, S], F32, AR + 112640)
        RS = at("ret_s", [P, 2, S], F32, AR + 116736)
        PAD = at("pad", [P, 2, S + 4], F32, AR + 120832)
        SC = at("scratch", [P, 4, S], F32, AR + 124960)
        MASK = at("masks", [P, 3 * P + 6 * 64], F32, AR + 133152)
        AB = at("ab", [8, S], F32, AR + 136224)
        ABR = at("ab_raw", [P, KT, 8], F32, AR + 138272)
        SM = at("small", [P, 12, 16], F32, G + 7264)
        ABH = at("ab_hi", [P, KT, 8], F32R, AR + 116736)
        ABL = at("ab_lo", [P, KT, 8], F32R, AR + 116736 + 256)
        ABT = SM[:, 0:2, :].rearrange("p a b -> p (a b)").rearrange("p (c e) -> p c e", e=8)
        UPPER = MASK[:, 0:P]
        LOWER = MASK[:, P:2 * P]
        PAIRM = MASK[:, 2 * P:3 * P]
        GG = SM[:, 2, :]
        BETA = SM[:, 3, :]
        GC = SM[:, 4, :]
        EGC = SM[:, 5, :]
        BEN = SM[:, 6, :]
        KDC = SM[:, 7, :]
        SPR = SM[:, 8, :]
        SPM = SM[:, 9, :]
        SPB = SM[:, 10, :]
        ALD = SM[:, 11, 0:8]

        RES = at("res", [P, KT, S], F32, AR)
        XB = at("x_b", [P, KT, 2, S], F32R, AR + 16384)
        ACTS = at("mlp_act", [P, FT, 2, S], F32R, AR + 49152)
        XT2 = at("x_t2", [P, KT, S], F32, AR + 96256)
        SQ2 = at("sq2", [P, 2, S], F32, AR + 69632)
        PADF = at("pad_f", [P, 4, S + 4], F32, 32768)
        CF = at("conv_f", [P, 4, S], F32, 32768 + 8256)
        PRODF = at("prod_f", [P, 2, S], F32, 32768 + 16448)
        SQ4B = at("sq4b", [P, 2, S], F32, 32768 + 20544)

        A3 = AR + 49152
        QS = at("q_s", [P, 4, S], F32, A3)
        KS = at("k_s", [P, S], F32, A3 + 8192)
        VS = at("v_s", [P, NB, P], F32, A3 + 10240)
        GA = at("ga", [P, 4, S], F32, A3 + 12288)
        GB = at("gb", [P, 4, S], F32, A3 + 20480)
        PL = at("pooled", [P, 4, S], F32, A3 + 28672)
        ALI = at("alibi", [P, QH, 256], F32, A3 + 36864)
        SB = at("scores", [P, 2, 4, 256], F32, A3 + 45056)
        PTS = at("probs_t", [P, 4, 2, P], F32, A3 + 53248)
        MIXF = at("mix_f", [P, 8, S], F32, A3 + 57344)
        PW = at("pool_w", [P, 4, P], F32, A3 + 73728)
        UPD = at("u_pad", [P, 3, S + 16], F32, A3 + 75776)
        ITAB = at("inv_cnt", [P, 4, 16], F32, A3 + 82112)
        AS = at("att_small", [P, 8, 8], F32, A3 + 82368)
        SINK = at("sink", [P, QH], F32, A3 + 82624)
        SQ3 = at("sq3", [P, 2, S], F32, A3 + 82656)
        Y = at("y", [P, KT, S], F32, A3 + 57344)
        YT = at("y_t", [P, 2, S], F32, A3 + 75776)
        GPW = S + CK - 1
        GLU = at("glu", [P, KT, GPW], F32, A3)
        CV = at("conv", [P, KT, S], F32, A3 + 17344)
        GT3 = at("gate3", [P, KT, S], F32, A3 + 57344)
        DG = at("tap_diag", [P, sum(PE_TAPS), P], F32, AR + 16384)
        ABUF = at("a_buf", [P, 4, S], F32, A3 + 41920)
        CT = at("c_t", [P, 2, S], F32, A3 + 50112)
        REST = at("x_by_token", [P, NB, D], F32, A3)
        YTOK = at("y_by_token", [P, NB, D], F32, A3 + 57344)
        WPOST = at("post_w", [P, D], F32, A3 + 75776)

        PS = ctx.enter_context(nc.psum_tensor("ps", [P, 8, S], F32))
        MX = PS[:, 4:8, :]

        MEAN = ABUF[:, 0, :]
        OFF = ABUF[:, 3, :]
        raw_in = [sem("raw_in0"), sem("raw_in1")]
        w_hi, w_lo = sem("w_hi_ready"), sem("w_lo_ready")
        half_done = sem("half_done")
        bank_free = sem("bank_free")
        op_src, op_hi, op_lo = sem("op_src"), sem("op_hi"), sem("op_lo")
        sq_ready, acc_done = sem("sq_ready"), sem("acc_done")
        stat_filled, rstd_ready = sem("stat_filled"), sem("rstd_ready")
        dchain, achain, gchain = sem("dve_step"), sem("act_step"), sem("pool_step")
        x_in, c_in, out_done = sem("x_in"), sem("const_in"), sem("out_done")
        c2_in, x2_in, ali_in = sem("const2_in"), sem("x2_in"), sem("alibi_in")
        x_kept, ident_in = sem("x_kept"), sem("ident_in")
        xt_filled = sem("xt_filled")
        par_filled, par_ready = sem("par_filled"), sem("par_ready")
        ones_ready = sem("ones_ready")
        conv_ready, silu_done = sem("gdn_conv_ready"), sem("gdn_silu_done")
        ab_split, ab_filled, ab_rows = sem("ab_split"), sem("ab_filled"), sem("ab_rows")
        abt_filled, abt_ready, rcol_ready = sem("abt_filled"), sem("abt_ready"), sem("rcol_ready")
        sp_in, sp_done, gb_ready = sem("softplus_in"), sem("softplus_exp"), sem("g_beta_ready")
        sqk, ssq_filled, r4_ready = sem("kq_squares"), sem("kq_ssq_filled"), sem("kq_norm_ready")
        kq_normed, gu_ready = sem("kq_normed"), sem("gu_ready")
        gc_filled, gc_ready, lb_ready = sem("gc_filled"), sem("gc_ready"), sem("lb_ready")
        gcb_filled, eb_ready, x1_ready = sem("gcb_filled"), sem("eb_ready"), sem("x1_ready")
        dmm_ready, dexp, dt_ready = sem("dmm_ready"), sem("decay_exp"), sem("dt_ready")
        g_filled, m_ready, qk_filled = sem("g_filled"), sem("m_ready"), sem("qk_filled")
        qkt_ready, t2_ready = sem("qkt_ready"), sem("t2_ready")
        tt_filled, tt_ready = sem("tt_filled"), sem("tt_ready")
        xp_filled, xs_ready, xz_ready = sem("xp_filled"), sem("xs_ready"), sem("xz_ready")
        txp_filled, upd_done = sem("txp_filled"), sem("upd_done")
        rot_ready = sem("ret_rotated")
        rs_filled, rs_ready = sem("ret_s_filled"), sem("ret_s_ready")
        ro_filled, ro_ready = sem("ret_o_filled"), sem("ret_o_ready")
        rsq_ready, rssq_filled, rr_ready = sem("ret_sq"), sem("ret_ssq_filled"), sem("ret_rstd")
        tok_filled, tokv_ready, tokk_ready = sem("tok_filled"), sem("tok_v_ready"), sem("tok_k_ready")
        nw_filled, nw_ready = sem("nw_filled"), sem("nw_ready")
        u_filled, u_ready = sem("u_filled"), sem("u_ready")
        qd_ready = sem("qd_ready")
        so_filled, o_ready, s_ready = sem("so_filled"), sem("gdn_o_ready"), sem("state_ready")
        gate_done = sem("gate_silu")
        ff_conv, ff_silu = sem("ff_conv"), sem("ff_silu")
        sc_filled, sc_ready, p_exp, p_ready = (sem("scores_filled"), sem("scores_max"),
                                               sem("probs_exp"), sem("probs_ready"))
        pt_filled, pt_ready = sem("pt_filled"), sem("pt_ready")
        ov_filled, ov_taken = sem("att_o_filled"), sem("att_o_taken")
        pool_ready, py_filled, py_taken = sem("pooled_ready"), sem("pool_y_filled"), sem("pool_y_taken")
        ff_prod, ff_hi, ff_lo = sem("ff_product"), sem("ff_hi"), sem("ff_lo")
        sig_done = sem("sigmoid_done")
        diag_ready, glu_ready = sem("tap_diag_ready"), sem("glu_ready")
        cv_filled, cv_ready = sem("conv_part_filled"), sem("conv_ready")
        mean_ready, off_ready, var_ready = sem("mean_ready"), sem("mean_off_ready"), sem("var_ready")
        centered, centered_last, shifted = sem("ln_centered"), sem("ln_centered_last"), sem("ln_shifted")
        cv_added = sem("conv_added")
        ln_added, scaled = sem("ln_square_added"), sem("layer7_scaled")
        ln_in, ln_done = sem("ln_in"), sem("ln_silu")
        cm_filled = sem("mean_filled")
        vt_filled, vt_ready = sem("att_v_filled"), sem("att_v_ready")
        wpost_in, y_done, ysq_done = sem("post_w_in"), sem("y_block_done"), sem("y_squared")
        yss_ready, ysd_ready = sem("y_sum_ready"), sem("y_deviation_ready")
        yinv_ready, yhalf_scaled = sem("y_1_over_rms"), sem("y_half_scaled")
        out0_ready = sem("out_half0_ready")
        rest_filled, rest_taken, ot_ready = sem("x_t_filled"), sem("x_t_taken"), sem("out_ready")

        block = ctx.enter_context(nc.Block())

        def f32(ap):
            return ap.bitcast(F32)

        def vec(name, k=0):
            c = VEC_AT[name] + k
            return VEC[:, c:c + 1]

        @block.sync
        def _(sp):
            def rows(w, r0, n, c0):
                return w[r0:r0 + n * P, bass.ds(c0, 256)].rearrange("(k p) c -> p k c", p=P)

            def free_slot(p):
                sp.wait_ge(w_lo, split_when_free(p))

            def wide_pair(p, w, r0, c0):
                for k in (0, 2):
                    sp.dma_start(RAW[:, p % 2, 2 * k:2 * k + 4, :].rearrange("p (k t) c -> p k (t c)", t=2),
                                 w[r0 + k * P:r0 + (k + 2) * P, c0:c0 + 512]
                                 .rearrange("(k p) c -> p k c", p=P)).then_inc(raw_in[p % 2], 16)

            def pair(p, slot, w, c0, r0=0, n=8):
                m = n // 2
                for k0, kn in ((0, m), (m, n - m)):
                    sp.dma_start(RAW[:, slot, k0:k0 + kn, :], rows(w, r0 + k0 * P, kn, c0)) \
                        .then_inc(raw_in[slot], 16)

            for b in range(NB):
                sp.dma_start(XTOK[:, b, :], a["x"][0, b * P:(b + 1) * P, :]).then_inc(x_in, 16)
            sp.dma_start(IDENT[:, :], const["ident"]).then_inc(ident_in, 16)
            r = 0
            srcs = {"pre0": a["pre_norm_2"][0], "pre1": a["pre_norm_2"][1],
                    "post0": a["post_norm_2"][0], "post1": a["post_norm_2"][1],
                    "attn_norm_w": a["attn_norm_w"][0], "mlp_norm_w": a["mlp_norm_w"][0],
                    "final_norm_w": a["final_norm_w"], "pool_scale": a["b_pool_scale_2"][0],
                    "dw_b": a["c_dw_b_2"][0], "ln_g": a["c_ln_g_2"][0], "ln_b": a["c_ln_b_2"][0],
                    "gdn_norm_w": a["gdn_norm_w"][0]}
            for name, n in VECS:
                sp.dma_start(ROWS[r:r + n, 0, :], srcs[name].rearrange("(k p) -> k p", p=P)) \
                    .then_inc(c_in, 16)
                r += n
            w_in = a["w_in"][0]
            sp.dma_start(ROWS[0:48, 1, :], a["gdn_conv_w"][0].rearrange("i (t p) -> (i t) p", p=P)) \
                .then_inc(c_in, 16)
            mc = a["mlp_conv_w"][0].rearrange("i (t p) -> (i t) p", p=P)
            dc = a["c_dw_w_2"][0, :, 0, :].rearrange("i (t p) -> (i t) p", p=P)
            sp.dma_start(ROWS[0:66, 2, :], mc[0:66, :]).then_inc(c_in, 16)
            sp.dma_start(ROWS[0:66, 5, :], mc[66:132, :]).then_inc(c_in, 16)
            sp.dma_start(ROWS[0:124, 3, :], dc[0:124, :]).then_inc(c_in, 16)
            sp.dma_start(ROWS[0:124, 4, :], dc[124:248, :]).then_inc(c_in, 16)
            pair(0, 0, w_in, 512)
            pair(1, 1, w_in, 768)
            sp.dma_start(ABR[:, :, :], w_in[:, 4 * GW:4 * GW + 8].rearrange("(k p) c -> p k c", p=P)) \
                .then_inc(c2_in, 16)
            sp.dma_start(ALD[:, 0:4], a["gdn_a_log"][0].rearrange("(a n) -> a n", a=1)
                         .broadcast_to([P, 4])).then_inc(c2_in, 16)
            sp.dma_start(ALD[:, 4:8], a["gdn_dt_bias"][0].rearrange("(a n) -> a n", a=1)
                         .broadcast_to([P, 4])).then_inc(c2_in, 16)
            sp.dma_start(MASK[:, :], const["masks"]).then_inc(c2_in, 16)
            sp.dma_start(CS[:, :, :], const["cos_sin"]).then_inc(c2_in, 16)
            sp.dma_start(DR[:, :, :], const["ret_decay"]).then_inc(c2_in, 16)
            sp.wait_ge(op_src, KT)
            sp.dma_start(x_t, XT[:, :, :]).then_inc(x_kept, 16)
            R = 4 * GW + 8
            starts = [512, 768, 0, 256, 1024, 1280, R + 1024, R + 1280, R, R + 512, R + 256, R + 768,
                      R + 1536, R + 1792, 1536, 1792]
            for p in range(2, 16):
                free_slot(p)
                if wide(2 * p):
                    wide_pair(p, w_in, (p - 6) * 512, starts[6])
                else:
                    pair(p, p % 2, w_in, starts[p])
                if p == 13:
                    sp.wait_ge(ro_ready, 4)
                    sp.wait_ge(x_kept, 16)
                    sp.dma_start(XT2[:, :, :], x_t).then_inc(x2_in, 16)
            w_out = a["w_out"][0]
            for p in range(16, 20):
                free_slot(p)
                c0 = (p - 16) * 256
                for k0, r0 in ((0, GW), (4, 0)):
                    sp.dma_start(RAW[:, p % 2, k0:k0 + 4, :], rows(w_out, r0, 4, c0)) \
                        .then_inc(raw_in[p % 2], 16)
            w_up = a["w_up"][0]
            with sp.Fori(0, 11) as i:
                for s in range(2):
                    sp.wait_ge(w_lo, i * 8 + 4 * (U3 // 2 + s - 1))
                    pair(0, s, w_up, i * 256 + s * DFF)
            w_down = a["w_down"][0]
            with sp.Fori(0, 2) as i:
                for j in range(6):
                    sp.wait_ge(w_lo, i * 24 + 4 * (U4 // 2 + j - 1))
                    g = j % 3
                    pair(0, j % 2, w_down, i * 512 + 256 * (j // 3), r0=g * D, n=8 if g < 2 else 6)
            w5 = a["a_w_in_2"][0]
            for p in range(U5 // 2, U6 // 2):
                free_slot(p)
                j = p - U5 // 2
                if j in (0, 1, 3, 4):
                    c0 = (0 if j < 2 else 768) + 128 * ((j + 1) % 2 if j > 2 else j)
                    for kv in range(2):
                        sp.dma_start(RAW[:, p % 2, :, kv * P:(kv + 1) * P],
                                     w5[:, c0 + kv * 256:c0 + kv * 256 + P]
                                     .rearrange("(k p) c -> p k c", p=P)).then_inc(raw_in[p % 2], 16)
                else:
                    pair(p, p % 2, w5, {2: 512, 5: 1280, 6: 1536, 7: 1792, 8: 2048}[j])
                if j == 0:
                    sp.wait_ge(half_done, 2 * U5)
                    sp.dma_start(ALI[:, :, :], const["alibi"]).then_inc(ali_in, 16)
                    sp.dma_start(PW[:, :, :], a["b_pool_w_2"][0].rearrange("g c d -> c g d")) \
                        .then_inc(ali_in, 16)
                    sp.dma_start(ITAB[:, :, :], const["inv_cnt"]).then_inc(ali_in, 16)
                    sp.dma_start(SINK[:, :], a["a_sinks_2"][0].rearrange("(a n) -> a n", a=1)
                                 .broadcast_to([P, QH])).then_inc(ali_in, 16)
            w6 = a["ab_w_out_2"][0]
            for p in range(U6 // 2, U7 // 2):
                free_slot(p)
                c0 = (p - U6 // 2) * 256
                for kv in range(2):
                    sp.dma_start(RAW[kv * 64:(kv + 1) * 64, p % 2, 0:4, :],
                                 w6[kv * 256:(kv + 1) * 256, c0:c0 + 256]
                                 .rearrange("(t d) c -> d t c", d=HD2)).then_inc(raw_in[p % 2], 16)
                sp.dma_start(RAW[:, p % 2, 4:8, :], rows(w6, 512, 4, c0)).then_inc(raw_in[p % 2], 16)
            w7 = a["c_w_in_2"][0]
            for p in range(U7 // 2, U7 // 2 + 8):
                free_slot(p)
                j = p - U7 // 2
                for ab in range(2):
                    sp.dma_start(RAW[:, p % 2, :, ab * P:(ab + 1) * P],
                                 w7[:, ab * D + j * P:ab * D + (j + 1) * P]
                                 .rearrange("(k p) c -> p k c", p=P)).then_inc(raw_in[p % 2], 16)
                if j == 2:
                    sp.wait_ge(op_src, 40)
                    sp.dma_start(WPOST[:, :], a["post_norm_2"][1:2, :].broadcast_to([P, D])) \
                        .then_inc(wpost_in, 16)
            for p in range(U7 // 2 + 8, U8 // 2):
                free_slot(p)
                pair(p, p % 2, w7, 2 * D + (p - U7 // 2 - 8) * 256)
            w8 = a["c_w_out_2"][0]
            for p in range(U8 // 2, PAIRS):
                free_slot(p)
                j = p - U8 // 2
                wide_pair(p, w8, (j % 2) * 512, (j // 2) * 512)
            for b in range(NB):
                for g in (1, 0):
                    if g == 1 or b == NB - 1:
                        sp.wait_ge(ot_ready, b + 2 - g)
                    else:
                        sp.wait_ge(out0_ready, b + 1)
                    sp.dma_start(out[0, b * P:(b + 1) * P, g * 512:(g + 1) * 512],
                                 YTOK[:, b, g * 512:(g + 1) * 512]).then_inc(out_done, 16)
            sp.wait_ge(out_done, 32 * NB)

        def half_k(n):
            u = unit_half(n)[0]
            return 3 if U4 <= u < U5 and ((u - U4) // 2) % 3 == 2 else 4

        def by_heads(n):
            u = unit_half(n)[0]
            return U5 <= u < U5 + 4 or U5 + 6 <= u < U5 + 10

        def raw_half(n):
            kn = half_k(n)
            u, hf = unit_half(n)
            if wide(u):
                return RAW[:, (u // 2) % 2, 2 * (n % 4):2 * (n % 4) + 2, :].rearrange("p k (t c) -> p (k t) c", t=2)
            r = RAW[:, (u // 2) % 2, kn * hf:kn * hf + kn, :]
            t = u % 2
            if by_heads(n):
                return r.rearrange("p k (v t d) -> p k v t d", v=2, t=2)[:, :, :, t, :]
            return r[:, :, t * P:(t + 1) * P]

        def ring_half(w, n):
            w = w[:, n % 4, 0:half_k(n), :]
            return w.rearrange("p k (v d) -> p k v d", v=2) if by_heads(n) else w

        @block.gpsimd
        def _(gp):
            def split_lo(n, later=0):
                gp.wait_ge(w_hi, later + n + 1)
                nc.gpsimd.tensor_tensor(ring_half(WL, n), raw_half(n), f32(ring_half(WH, n)), SUB) \
                    .then_inc(w_lo, 1)

            def unit(u):
                split_lo(2 * u)
                split_lo(2 * u + 1)

            def zero(level, c):
                x = XZ[:, c, :, :].rearrange("p h (b two s) -> p h b two s", two=2, s=2 << level)
                nc.gpsimd.memset(x[:, :, :, 0, :], 0.0).then_inc(xz_ready, 1)

            nc.gpsimd.memset(ONES[:, :], 1.0).then_inc(ones_ready, 1)
            nc.gpsimd.memset(CB[:, 0:1], EPS).then_inc(ones_ready, 1)
            nc.gpsimd.memset(CB[:, 1:2], math.log(P ** -0.5)).then_inc(ones_ready, 1)
            nc.gpsimd.memset(CB[:, 2:3], 1.0).then_inc(ones_ready, 1)
            nc.gpsimd.memset(PAD[:, :, 0:3], 0.0).then_inc(ones_ready, 1)
            def add_squares(st, k0, k1, squares):
                if k0 == 0 and st > 0:
                    gp.wait_ge(rstd_ready, st)
                for k in range(k0, k1):
                    gp.wait_ge(sq_ready, 8 * st + k + 1)
                    if k == 0:
                        nc.gpsimd.tensor_copy(ACC[:, :], squares[:, 0, :]).then_inc(acc_done, 1)
                    else:
                        gp.wait_ge(acc_done, 8 * st + k)
                        nc.gpsimd.tensor_tensor(ACC[:, :], ACC[:, :], squares[:, k % 2, :], ADD) \
                            .then_inc(acc_done, 1)

            add_squares(0, 0, 2, SC[:, 2:4, :])
            split_lo(0)
            add_squares(0, 2, 4, SC[:, 2:4, :])
            split_lo(1)
            add_squares(0, 4, POOL_SQUARES, SC[:, 2:4, :])
            for u in range(1, 14):
                unit(u)
            gp.wait_ge(gb_ready, 1)
            gp.wait_ge(c2_in, 96)
            nc.gpsimd.tensor_tensor(LB[:, :, :], LOWER.unsqueeze(1).broadcast_to([P, 16, P]),
                                    BETA.unsqueeze(2).broadcast_to([P, 16, P]), MUL).then_inc(lb_ready, 1)
            unit(14)
            unit(15)
            unit(16)
            gp.wait_ge(dexp, 1)
            nc.gpsimd.tensor_tensor(T[:, :, :], T[:, :, :], UPPER.unsqueeze(1).broadcast_to([P, 16, P]),
                                    MUL).then_inc(dt_ready, 1)
            gp.wait_ge(m_ready, 1)
            for c in range(NB):
                zero(0, c)
            unit(17)
            unit(18)
            for level in range(5):
                unit(19 + level)
                for c in range(NB):
                    gp.wait_ge(txp_filled, 4 * level + c + 1)
                    zero(level + 1, c)
            for u in range(24, U3):
                unit(u)
            with gp.Fori(0, 11) as i:
                for j in range(8):
                    split_lo(2 * U3 + j, i * 8)
            def scale(n):
                if n == 0:
                    gp.wait_ge(rstd_ready, 6)
                gp.wait_ge(bank_free, M7 + n + 1)
                t = ABUF[:, n % 4, :] if n < 16 else GT3[:, n - 16, :]
                nc.gpsimd.tensor_tensor(t, t, RSTD[:, :], MUL).then_inc(scaled, 1)

            for u in range(U4, UNITS):
                for q, st in ((U5, 3), (U7, 5)):
                    if u == q + 1:
                        add_squares(st, 0, SPLIT_AT[0], SQ3)
                split_lo(2 * u)
                for q, st in ((U5, 3), (U7, 5)):
                    if u == q + 1:
                        add_squares(st, SPLIT_AT[0], POOL_SQUARES, SQ3)
                if u == U8 + 1:
                    gp.wait_ge(mean_ready, 1)
                    for k in range(KT - 1):
                        nc.gpsimd.tensor_tensor(CV[:, k, :], CV[:, k, :], MEAN, SUB).then_inc(centered, 1)
                n = u - 2 - U7
                if 1 <= n < 24:
                    scale(n)
                split_lo(2 * u + 1)
                if n == 0:
                    scale(n)
                if u in SUM_AT:
                    k = 1 + SUM_AT.index(u)
                    gp.wait_ge(cv_ready, k + 1)
                    if k >= 2:
                        gp.wait_ge(cv_added, k - 1)
                    nc.gpsimd.tensor_tensor(ACC[:, :], CV[:, 0, :] if k == 1 else ACC[:, :], CV[:, k, :], ADD) \
                        .then_inc(cv_added, 1)
                if u == U8 + 1:
                    gp.wait_ge(off_ready, 1)
                    gp.wait_ge(centered, KT - 1)
                    gp.wait_ge(centered_last, 1)
                    gp.wait_ge(ln_added, KT)
                    for k in range(SHIFTED_BY_DVE, KT):
                        nc.gpsimd.tensor_tensor(CV[:, k, :], CV[:, k, :], OFF, SUB).then_inc(shifted, 1)
                k = u - U7 - 2
                if 0 <= k < KT:
                    if k == 0:
                        gp.wait_ge(half_done, 2 * U7)
                        gp.wait_ge(par_ready, 4)
                    n0, n1 = sum(PE_TAPS[:k]), sum(PE_TAPS[:k + 1])
                    nc.gpsimd.tensor_tensor(DG[:, n0:n1, :],
                                            IDENT[:, :].unsqueeze(1).broadcast_to([P, n1 - n0, P]),
                                            DCW[:, CK - (n1 - n0):CK, k].unsqueeze(2)
                                            .broadcast_to([P, n1 - n0, P]), MUL).then_inc(diag_ready, 1)

            gp.wait_ge(rest_taken, KT)
            for b in range(NB - 1):
                gp.wait_ge(yhalf_scaled, b + 1)
                nc.gpsimd.tensor_tensor(YTOK[:, b, 0:512], YTOK[:, b, 0:512], REST[:, b, 0:512], ADD) \
                    .then_inc(out0_ready, 1)

        @block.scalar
        def _(act):
            steps = [0]

            def table(n):
                nc.scalar.add_instruction(mybir.InstLoadActFuncSet(
                    name=nc.get_next_instruction_name(), act_func_set_id=n,
                    engine=mybir.EngineType.Activation, ins=[], outs=[]))

            def step(ins):
                steps[0] += 1
                ins.then_inc(achain, 1)
                act.wait_ge(achain, steps[0])

            def split_hi(n, i=None):
                p = unit_half(n)[0] // 2
                if n >= UNITS * 2:
                    return
                if i is None:
                    act.wait_ge(raw_in[p % 2], 16 * loads_before(p))
                    if n >= 4:
                        act.wait_ge(half_done, n - 3)
                else:
                    act.wait_ge(raw_in[p % 2], i * 32 + 16 * loads_before(p))
                    act.wait_ge(half_done, i * 8 + n - 3)
                nc.scalar.activation(ring_half(WH, n), raw_half(n), ACT.Copy).then_inc(w_hi, 1)

            def splits(u):
                if u not in QUADS and u - 1 not in QUADS:
                    split_hi(2 * u + 3)
                if u not in QUADS and u + 1 not in QUADS:
                    split_hi(2 * u + 4)

            def operand_hi(src, dst, scale):
                nc.scalar.activation(dst, src, ACT.Copy, scale=scale).then_inc(op_hi, 1)

            def square(st, k, src, dst):
                if k >= 2:
                    act.wait_ge(acc_done, 8 * st + k - 1)
                nc.scalar.activation(dst, src, ACT.Square).then_inc(sq_ready, 1)

            def stat(st):
                table(LN_EXP_SET)
                act.wait_ge(stat_filled, st + 1)
                step(nc.scalar.activation(RSTD[:, :], PS[:, 7, :], ACT.Ln, bias=CB[:, 0:1], scale=1.0 / D))
                nc.scalar.activation(RSTD[:, :], RSTD[:, :], ACT.Exp, scale=-0.5).then_inc(rstd_ready, 1)

            table(EXP_SET)
            act.wait_ge(par_ready, 1)
            act.wait_ge(ones_ready, 5)
            for k in range(KT):
                act.wait_ge(op_src, k + 1)
                operand_hi(XT[:, k, :], XA[:, k, 0, :], vec("attn_norm_w", k))
                square(0, k, XT[:, k, :], SC[:, 2 + k % 2, :])
                if k % 2 == 1:
                    split_hi(k // 2)
            split_hi(4)
            split_hi(5)

            def tile_silu(u):
                act.wait_ge(conv_ready, u + 1)
                d = KQ[:, u % 4, u // 4, :] if u < 8 else V[:, u - 8, :]
                nc.scalar.activation(d, d, ACT.Silu).then_inc(silu_done, 1)

            def values(c):
                act.wait_ge(tok_filled, 2 * c + 2)
                for h in range(H):
                    nc.scalar.activation(VB[:, h, :], PS[:, 5, h * P:(h + 1) * P], ACT.Copy,
                                         scale=BETA[:, 4 * c + h:4 * c + h + 1]).then_inc(tokv_ready, 1)

            def new_values(c):
                act.wait_ge(u_filled, c + 1)
                nc.scalar.activation(UU[:, :, :], PS[:, 7, :].rearrange("p (h v) -> p h v", h=H), ACT.Copy) \
                    .then_inc(u_ready, 1)

            def outputs(c):
                act.wait_ge(so_filled, 2 * c + 1)
                nc.scalar.activation(KQ[:, :, 1, c * P:(c + 1) * P],
                                     PS[:, 6, :].rearrange("p (h i) -> p h i", h=H), ACT.Copy) \
                    .then_inc(o_ready, 1)

            def weights_t(c):
                act.wait_ge(nw_filled, c)
                nc.scalar.activation(NW[:, :, :], PS[:, 6, :].rearrange("p (h c) -> p h c", h=H), ACT.Copy) \
                    .then_inc(nw_ready, 1)

            def ret_out(h):
                act.wait_ge(ro_filled, h + 1)
                nc.scalar.activation(RV[:, h, :, :].rearrange("p b i -> p (b i)"), PS[:, 6, :], ACT.Copy) \
                    .then_inc(ro_ready, 1)

            def ret_norm(r):
                table(LN_EXP_SET)
                act.wait_ge(rssq_filled, r + 1)
                rr = RR[:, 2 * r:2 * r + 2, :]
                step(nc.scalar.activation(rr, MX[:, 0:2, :], ACT.Ln, bias=CB[:, 0:1], scale=1.0 / P))
                nc.scalar.activation(rr, rr, ACT.Exp, scale=-0.5).then_inc(rr_ready, 1)

            def ret_operand(h):
                act.wait_ge(op_src, 8 + h + 1)
                operand_hi(RV[:, h, :, :].rearrange("p b i -> p (b i)"), XA[:, h, 0, :], 1.0)

            for u in range(U1, U2):
                if u == 15:
                    split_hi(34)
                else:
                    splits(u)
                if u == 0:
                    stat(0)
                if 1 <= u <= 12:
                    tile_silu(u - 1)
                if u == 12:
                    act.wait_ge(silu_done, 8)
                    nc.scalar.activation(SQ4[:, :, :], KQ[:, :, 0, :], ACT.Square).then_inc(sqk, 1)
                    table(LN_EXP_SET)
                    act.wait_ge(sp_in, 1)
                    step(nc.scalar.activation(SPM, SPM, ACT.Exp))
                    step(nc.scalar.activation(SPM, SPM, ACT.Ln, bias=CB[:, 2:3]))
                    step(nc.scalar.activation(ALD[:, 0:4], ALD[:, 0:4], ACT.Exp))
                    nc.scalar.activation(SPB, SPB, ACT.Exp, scale=-1.0).then_inc(sp_done, 1)
                    act.wait_ge(ssq_filled, 1)
                    step(nc.scalar.activation(R4[:, :, :], MX, ACT.Ln, bias=CB[:, 0:1]))
                    nc.scalar.activation(R4[:, :, :], R4[:, :, :], ACT.Exp, scale=-0.5).then_inc(r4_ready, 1)
                    nc.scalar.activation(SQ4[:, :, :], KQ[:, :, 1, :], ACT.Square).then_inc(sqk, 1)
                if u == 13:
                    act.wait_ge(ssq_filled, 2)
                    act.wait_ge(kq_normed, 1)
                    step(nc.scalar.activation(R4[:, :, :], MX, ACT.Ln, bias=CB[:, 0:1]))
                    nc.scalar.activation(R4[:, :, :], R4[:, :, :], ACT.Exp, scale=-0.5, bias=CB[:, 1:2]) \
                        .then_inc(r4_ready, 1)
                if u == 14:
                    act.wait_ge(gc_ready, 1)
                    nc.scalar.activation(EGC, GC, ACT.Exp).then_inc(eb_ready, 1)
                    act.wait_ge(gcb_filled, 1)
                    nc.scalar.activation(EB[:, :, :].rearrange("p a i -> p (a i)"),
                                         MX.rearrange("p b s -> p (b s)"), ACT.Exp).then_inc(eb_ready, 1)
                    split_hi(33)
                    act.wait_ge(dmm_ready, 1)
                    nc.scalar.activation(T[:, :, :], T[:, :, :], ACT.Exp).then_inc(dexp, 1)
                    act.wait_ge(dmm_ready, 2)
                    nc.scalar.activation(M[:, :, :], M[:, :, :], ACT.Exp, scale=-1.0).then_inc(dexp, 1)
                if u == 17:
                    act.wait_ge(tt_filled, 1)
                    nc.scalar.activation(TT[:, :, :].rearrange("p a i -> p (a i)"),
                                         MX.rearrange("p b s -> p (b s)"), ACT.Copy).then_inc(tt_ready, 1)
                if u in RET_GAP:
                    ret_out(RET_GAP.index(u))
                if u == 24:
                    values(0)
                if u == 25:
                    act.wait_ge(ro_ready, 4)
                    nc.scalar.activation(RR[:, :, :], RV[:, :, :, :].rearrange("p h b i -> p h (b i)"),
                                         ACT.Square).then_inc(rsq_ready, 1)
                    ret_norm(0)
                if u == 26:
                    new_values(0)
                    values(1)
                    outputs(0)
                if u == 27:
                    weights_t(1)
                    ret_norm(1)
                if u == 28:
                    new_values(1)
                    values(2)
                    outputs(1)
                if u == 29:
                    act.wait_ge(bank_free, M1 + 28)
                    nc.scalar.activation(GT[:, 0:4, :], GT[:, 0:4, :], ACT.Silu).then_inc(gate_done, 1)
                    weights_t(2)
                if u == 30:
                    new_values(2)
                    values(3)
                    outputs(2)
                if u == 31:
                    weights_t(3)
                    act.wait_ge(half_done, 2 * U2)
                    ret_operand(0)
                    new_values(3)
                    ret_operand(1)
                    outputs(3)
                    ret_operand(2)
                    ret_operand(3)
                    act.wait_ge(o_ready, 4)
                    act.wait_ge(op_src, 12)
                    nc.scalar.activation(RR[:, :, :], KQ[:, :, 1, :], ACT.Square).then_inc(rsq_ready, 1)
                    act.wait_ge(bank_free, M1 + 32)
                    nc.scalar.activation(GT[:, 4:8, :], GT[:, 4:8, :], ACT.Silu).then_inc(gate_done, 1)
            split_hi(2 * U2 + 2)
            split_hi(2 * U2 + 3)
            table(LN_EXP_SET)
            act.wait_ge(rssq_filled, 3)
            step(nc.scalar.activation(RR[:, :, :], MX, ACT.Ln, bias=CB[:, 0:1], scale=1.0 / P))
            nc.scalar.activation(RR[:, :, :], RR[:, :, :], ACT.Exp, scale=-0.5).then_inc(rr_ready, 1)
            split_hi(2 * U2 + 4)
            split_hi(2 * U2 + 5)
            for h in range(H):
                act.wait_ge(op_src, 12 + h + 1)
                operand_hi(KQ[:, h, 1, :], XA[:, 4 + h, 0, :], 1.0)

            def from_residual(k):
                act.wait_ge(bank_free, M2 + k + 1)
                operand_hi(RES[:, k, :], XB[:, k, 0, :], vec("mlp_norm_w", k))
                square(1, k, RES[:, k, :], SQ2[:, k % 2, :])

            for u in range(U2, U3):
                k = u - U2
                splits(u)
                if k >= 1:
                    from_residual(k - 1)
            from_residual(KT - 1)
            stat(1)
            table(SILU_SET)
            with act.Fori(0, 11) as i:
                for j in range(4):
                    split_hi(2 * (U3 + j) + 3, i)
                    split_hi(2 * (U3 + j) + 4, i)
                    if j < 2:
                        act.wait_ge(ff_conv, i * 2 + j + 1)
                        nc.scalar.activation(CF[:, j, :], CF[:, j, :], ACT.Silu).then_inc(ff_silu, 1)
                    else:
                        act.wait_ge(ff_prod, i * 2 + j - 1)
                        nc.scalar.activation(ACTS[:, bass.ds(i * 2 + (j - 2), 1), 0, :]
                                             .rearrange("p a s -> p (a s)"), PRODF[:, j - 2, :], ACT.Copy) \
                            .then_inc(ff_hi, 1)

            for u in range(U4, U5 + 1):
                if u > U4 and (u - U4) % 6 == 0:
                    for k in (2 * ((u - U4) // 6) - 2, 2 * ((u - U4) // 6) - 1):
                        act.wait_ge(bank_free, M4 + k + 1)
                        square(2, k, RES[:, k, :], SQ4B[:, k % 2, :])
                if u < U5:
                    splits(u)
            stat(2)
            for k in range(KT):
                if k in SPLIT_AT:
                    split_hi(2 * U5 + 2 + SPLIT_AT.index(k))
                act.wait_ge(op_src, 16 + k + 1)
                operand_hi(RES[:, k, :], XA[:, k, 0, :], vec("pre0", k))
                square(3, k, RES[:, k, :], SQ3[:, k % 2, :])
            split_hi(2 * U5 + 5)

            def probs(j):
                act.wait_ge(sc_ready, j + 1)
                lo = P if j < 2 else 0
                for t in range(4):
                    nc.scalar.activation(SB[:, j % 2, t, lo:256], SB[:, j % 2, t, lo:256], ACT.Exp,
                                         bias=AS[:, 1, t:t + 1], accum_out=AS[:, 2, t:t + 1]) \
                        .then_inc(p_exp, 1)
                nc.scalar.activation(AS[:, 3, 0:4], AS[:, 3, 0:4], ACT.Exp).then_inc(p_exp, 1)

            for u in range(U5, U6):
                splits(u)
                if u == U5:
                    stat(3)
                j = u - (U5 + 6)
                if j == 0:
                    act.wait_ge(vt_filled, 1)
                    nc.scalar.activation(VS[:, :, :], PS[:, 7, :].rearrange("p (b d) -> p b d", b=NB),
                                         ACT.Copy).then_inc(vt_ready, 1)
                if 1 <= j <= 8:
                    act.wait_ge(pt_filled, j)
                    lo = 1 if j - 1 < 2 else 0
                    nc.scalar.activation(PTS[:, :, lo:2, :],
                                         PS[:, 6:8, :].rearrange("p b (t w i) -> p (b t) w i", t=2, w=2)
                                         [:, :, lo:2, :], ACT.Copy).then_inc(pt_ready, 1)
                if 0 <= j < 8:
                    probs(j)
                if 1 <= j <= 8:
                    b, kv = (j - 1) // 2, (j - 1) % 2
                    act.wait_ge(ov_filled, j)
                    nc.scalar.activation(MIXF[kv * HD2:(kv + 1) * HD2, 0:4, b * P:(b + 1) * P],
                                         PS[kv * HD2:(kv + 1) * HD2, 6, :]
                                         .rearrange("p (t i) -> p t i", t=4), ACT.Copy).then_inc(ov_taken, 1)
                if j == 9:
                    act.wait_ge(py_filled, 1)
                    for g in range(4):
                        nc.scalar.activation(PL[:, g, :], MX[:, g, :], ACT.Copy,
                                             scale=vec("pool_scale", g)).then_inc(py_taken, 1)
                    act.wait_ge(bank_free, M5 + 10)
                    nc.scalar.activation(GA[:, :, :], GA[:, :, :], ACT.Silu).then_inc(gate_done, 1)
                if j == 10:
                    for t in range(4):
                        act.wait_ge(op_src, 24 + t + 1)
                        operand_hi(MIXF[:, t, :], XB[:, t, 0, :], 1.0)
                if j >= 9:
                    g = j - 9
                    act.wait_ge(bank_free, M5 + 14 + g + 1)
                    nc.scalar.activation(GB[:, g, :], GB[:, g, :], ACT.Silu).then_inc(gate_done, 1)
            split_hi(2 * U6 + 2)
            split_hi(2 * U6 + 3)
            act.wait_ge(bank_free, M5 + 18)
            nc.scalar.activation(GB[:, 3, :], GB[:, 3, :], ACT.Silu).then_inc(gate_done, 1)
            for g in range(4):
                act.wait_ge(op_src, 28 + g + 1)
                operand_hi(MIXF[:, 4 + g, :], XB[:, 4 + g, 0, :], 1.0)
            split_hi(2 * U6 + 4)
            split_hi(2 * U6 + 5)

            for u in range(U6, U7):
                splits(u)
                k = u - U6
                if k >= 1:
                    act.wait_ge(bank_free, M6 + k)
                    square(4, k - 1, Y[:, k - 1, :], SQ3[:, (k - 1) % 2, :])
            act.wait_ge(bank_free, M6 + KT)
            square(4, KT - 1, Y[:, KT - 1, :], SQ3[:, 1, :])
            stat(4)
            for k in range(KT):
                if k in SPLIT_AT:
                    split_hi(2 * U7 + 2 + SPLIT_AT.index(k))
                act.wait_ge(op_src, 32 + k + 1)
                operand_hi(RES[:, k, :], XA[:, k, 0, :], vec("pre1", k))
                square(5, k, RES[:, k, :], SQ3[:, k % 2, :])
            split_hi(2 * U7 + 5)
            stat(5)
            def activate(n):
                if n < 16 and n % 2 == 0:
                    return
                act.wait_ge(scaled, n + 1)
                if n < 16:
                    t = ABUF[:, n % 4, :]
                    nc.scalar.activation(t, t, ACT.Sigmoid).then_inc(sig_done, 1)
                else:
                    nc.scalar.activation(GT3[:, n - 16, :], GT3[:, n - 16, :], ACT.Silu).then_inc(gate_done, 1)

            for u in range(U7, U8):
                splits(u)
                n = u - U7
                if n == 23:
                    act.wait_ge(glu_ready, KT)
                    act.wait_ge(cm_filled, 1)
                    nc.scalar.activation(MEAN, PS[:, 7, :], ACT.Copy, scale=1.0 / (P * (KT - 1))) \
                        .then_inc(mean_ready, 1)
                if n >= 1:
                    activate(n - 1)
                if 4 <= n < 16:
                    act.wait_ge(glu_ready, n // 2 - 1)
                act.wait_ge(half_done, halves_when_done(u))
                nc.scalar.activation(ABUF[:, n % 4, :] if n < 16 else GT3[:, n - 16, :],
                                     PS[:, (M7 + n) % 4, :], ACT.Copy).then_inc(bank_free, 1)
            split_hi(2 * U8 + 3)
            for k in range(KT):
                if k < KT - 1:
                    act.wait_ge(centered, k + 1)
                else:
                    act.wait_ge(centered_last, 1)
                if k >= 2:
                    act.wait_ge(ln_added, k - 1)
                nc.scalar.activation(ABUF[:, 1 + k % 2, :], CV[:, k, :], ACT.Square).then_inc(sq_ready, 1)
            table(LN_EXP_SET)
            act.wait_ge(scaled, 24)
            act.wait_ge(var_ready, 1)
            step(nc.scalar.activation(RSTD[:, :], ACC[:, :], ACT.Ln, bias=CB[:, 0:1]))
            nc.scalar.activation(RSTD[:, :], RSTD[:, :], ACT.Exp, scale=-0.5).then_inc(rstd_ready, 1)
            for k in range(KT + 1):
                if k < KT:
                    act.wait_ge(ln_in, k + 1)
                    nc.scalar.activation(CV[:, k, :], CV[:, k, :], ACT.Silu, bias=vec("ln_b", k)) \
                        .then_inc(ln_done, 1)
                if k >= 1:
                    act.wait_ge(op_src, 40 + k)
                    operand_hi(CV[:, k - 1, :], XB[:, k - 1, 0, :], 1.0)
                if k == 2:
                    activate(23)
                if k >= 3:
                    split_hi(2 * U8 + k + 1)

            def x_by_token(k):
                act.wait_ge(rest_filled, k + 1)
                nc.scalar.activation(REST[:, :, k * P:(k + 1) * P],
                                     PS[:, REST_BANK[k % 4], :].rearrange("p (b f) -> p b f", b=NB),
                                     ACT.Copy).then_inc(rest_taken, 1)

            def square_by_token(g, b):
                if b < NB - 1:
                    act.wait_ge(y_done, 3 * g + b + 1)
                else:
                    act.wait_ge(half_done, 2 * U8 + 8 * (g + 1))
                if 4 * g + b >= 2:
                    act.wait_ge(ysq_done, 4 * g + b - 1)
                nc.scalar.activation(CT[:, b % 2, :], PS[:, (M8 + b) % 4, :], ACT.Square,
                                     accum_out=AS[:, 0, 4 * g + b:4 * g + b + 1]).then_inc(ysq_done, 1)

            def deviation(b):
                act.wait_ge(yss_ready, b + 1)
                nc.scalar.activation(AS[:, 2, b:b + 1], AS[:, 1, b:b + 1], ACT.Sqrt, bias=CB[:, 0:1],
                                     scale=1.0 / D).then_inc(ysd_ready, 1)

            def scale_first_half(b):
                act.wait_ge(yinv_ready, b + 1)
                nc.scalar.activation(YTOK[:, b, 0:512], YTOK[:, b, 0:512], ACT.Copy,
                                     scale=AS[:, 3, b:b + 1]).then_inc(yhalf_scaled, 1)

            for k in range(4):
                x_by_token(k)
                if k % 2 == 1:
                    split_hi(2 * U8 + 10 + k // 2)
            for b in range(NB):
                square_by_token(0, b)
            for k in range(4):
                split_hi(2 * U8 + 12 + k)
                x_by_token(4 + k)
            table(SQRT_SET)
            for b in range(NB + 1):
                if b < NB:
                    square_by_token(1, b)
                if 1 <= b <= NB:
                    deviation(b - 1)
                if 2 <= b <= NB:
                    scale_first_half(b - 2)

        @block.vector
        def _(dve):
            v = nc.vector
            steps = [0]
            late = [None]

            def step(ins):
                steps[0] += 1
                ins.then_inc(dchain, 1)
                dve.wait_ge(dchain, steps[0] if late[0] is None else late[0] + steps[0])

            def tile_done(u):
                dve.wait_ge(half_done, halves_when_done(u))

            def operand_lo(f, src, dst_lo, dst_hi, scale=1.0):
                dve.wait_ge(op_hi, f + 1)
                v.scalar_tensor_tensor(out=dst_lo, in0=src, scalar=scale, in1=f32(dst_hi), op0=MUL, op1=SUB) \
                    .then_inc(op_lo, 1)

            def accumulate(st, k, sq):
                n = 8 * st + k
                dve.wait_ge(sq_ready, n + 1)
                if k == 0:
                    v.tensor_copy(ACC[:, :], sq).then_inc(acc_done, 1)
                else:
                    dve.wait_ge(acc_done, n)
                    v.tensor_tensor(ACC[:, :], ACC[:, :], sq, ADD).then_inc(acc_done, 1)

            MX16 = MX.rearrange("p b (h i) -> p (b h) i", h=H)

            def lastdim(ap):
                return ap.unsqueeze(2).broadcast_to([P, 16, P])

            def x_tile(k):
                dve.wait_ge(xt_filled, k + 1)
                v.tensor_copy(XT[:, k, :], PS[:, 4 + k % 4, :]).then_inc(op_src, 1)

            for k in range(4):
                x_tile(k)
            dve.wait_ge(par_filled, 1)
            v.tensor_copy(VEC[:, :], PS[:, 0, 0:NVEC]).then_inc(par_ready, 1)
            v.tensor_copy(GCW[:, :, :].rearrange("p a b -> p (a b)"), PS[:, 0, NVEC:NVEC + 48]) \
                .then_inc(par_ready, 1)
            v.tensor_copy(MCW[:, :, :].rearrange("p a b -> p (a b)"), PS[:, 0, NVEC + 48:NVEC + 180]) \
                .then_inc(par_ready, 1)
            v.tensor_copy(DCW[:, :, :].rearrange("p a b -> p (a b)"), PS[:, 1, 0:248]).then_inc(par_ready, 1)
            dve.wait_ge(par_ready, 4)
            for k in range(KT):
                if k < 4:
                    x_tile(k + 4)
                dve.wait_ge(op_src, k + 1)
                operand_lo(k, XT[:, k, :], XA[:, k, 1, :], XA[:, k, 0, :], vec("attn_norm_w", k))
                if k >= POOL_SQUARES:
                    accumulate(0, k, SC[:, 2 + k % 2, :])

            def conv_tile(u):
                t = {0: 4, 1: 0, 2: 8}[u // 4] + u % 4
                d = KQ[:, u % 4, u // 4, :] if u < 8 else V[:, u - 8, :]
                x = PAD[:, u % 2, :]
                v.tensor_tensor(x[:, 3:3 + S], PS[:, u % 4, :], RSTD[:, :], MUL).then_inc(bank_free, 1)
                dve.wait_ge(bank_free, u + 1)
                step(v.tensor_scalar(d, x[:, 3:3 + S], GCW[:, 3, t:t + 1], None, MUL))
                for i in (2, 1):
                    step(v.scalar_tensor_tensor(out=d, in0=x[:, i:i + S], scalar=GCW[:, i, t:t + 1],
                                                in1=d, op0=MUL, op1=ADD))
                v.scalar_tensor_tensor(out=d, in0=x[:, 0:S], scalar=GCW[:, 0, t:t + 1], in1=d,
                                       op0=MUL, op1=ADD).then_inc(conv_ready, 1)

            SWAP = [i ^ 1 for i in range(32)]

            def rotate_tile(u):
                h = u % 2 + 2 * ((u - 16) // 4)
                d = (RQ if (u - 16) % 4 < 2 else RK)[:, h % 2, :]
                if h >= 2:
                    dve.wait_ge(rs_filled, 4 * (h - 1))
                step(v.tensor_tensor(d, PS[:, u % 4, :], CS[:, 0, :], MUL))
                v.stream_shuffle(SC[:, u % 2, :], PS[:, u % 4, :], SWAP).then_inc(bank_free, 1)
                dve.wait_ge(bank_free, u + 1)
                step(v.tensor_tensor(SC[:, u % 2, :], SC[:, u % 2, :], CS[:, 1, :], MUL))
                v.tensor_tensor(d, d, SC[:, u % 2, :], ADD).then_inc(rot_ready, 1)

            def level(l):
                s = 2 << l
                def half(ap, two):
                    return ap.rearrange("p h (b two s) -> p h b two s", two=2, s=s)[:, :, :, two, :]
                def part(bank, off):
                    return PS[:, bank, off:off + 256].rearrange("p (h b s) -> p h b s", h=H, s=s)
                mask = MASK[:, 3 * P + 64 * l:3 * P + 64 * (l + 1)].rearrange("p (b s) -> p b s", s=s) \
                    .unsqueeze(1).broadcast_to([P, H, 64 // s, s])
                for c in range(NB):
                    dve.wait_ge(xp_filled, 4 * l + c + 1)
                    v.tensor_tensor(half(XZ[:, c, :, :], 1), part(4 + c, 0), mask, MUL).then_inc(xs_ready, 1)
                for c in range(NB):
                    dve.wait_ge(txp_filled, 4 * l + c + 1)
                    u_ = half(TT[:, 4 * c:4 * c + 4, :], 1)
                    ins = v.tensor_tensor(u_, u_, part(4 + c, 256), SUB)
                    if l < 5:
                        t_ = half(T[:, 4 * c:4 * c + 4, :], 0)
                        ins = v.tensor_tensor(t_, t_, part(4 + c, 0), SUB)
                    ins.then_inc(upd_done, 1)

            def ret_scores(h):
                for jb in range(NB):
                    n = S - jb * P
                    dve.wait_ge(rs_filled, 4 * h + jb + 1)
                    v.tensor_tensor(RS[:, jb % 2, 0:n], PS[:, 4 + jb % 2, 0:n], DR[:, h, 0:n], MUL) \
                        .then_inc(rs_ready, 1)

            def keys(c):
                kt = PS[:, 4, :].rearrange("p (h d) -> p h d", h=H)
                dve.wait_ge(tok_filled, 2 * c + 1)
                if c > 0:
                    step(v.tensor_tensor(KB[:, :, :], kt, BEN[:, 4 * c:4 * c + 4].unsqueeze(2)
                                         .broadcast_to([P, H, P]), MUL))
                    state(c - 1)
                v.tensor_tensor(KD[:, :, :], kt, KDC[:, 4 * c:4 * c + 4].unsqueeze(2)
                                .broadcast_to([P, H, P]), MUL).then_inc(tokk_ready, 1)
                if c > 0:
                    v.tensor_tensor(QD[:, :, :], KQ[:, :, 1, c * P:(c + 1) * P],
                                    EB[:, 4 * c:4 * c + 4, :], MUL).then_inc(qd_ready, 1)

            def state(c):
                dve.wait_ge(so_filled, 2 * c + 2)
                for h in range(H):
                    ps = PS[:, 7, h * P:(h + 1) * P]
                    if c == 0:
                        ins = v.tensor_copy(ST8[:, h, :], ps)
                    else:
                        ins = v.scalar_tensor_tensor(out=ST8[:, h, :], in0=ST8[:, h, :],
                                                     scalar=EB[:, 4 * c + h, P - 1:P], in1=ps,
                                                     op0=MUL, op1=ADD)
                ins.then_inc(s_ready, 1)

            for u in range(U1, U2):
                if u == 8:
                    dve.wait_ge(x_kept, 16)
                if u == 3:
                    tile_done(u)
                    dve.wait_ge(ab_filled, 1)
                    v.tensor_tensor(AB[:, :], PS[0:8, 7, :], RSTD[0:8, :], MUL).then_inc(ab_rows, 1)
                if u == 4:
                    dve.wait_ge(abt_filled, 1)
                    step(v.tensor_copy(ABT, PS[:, 7, 0:32].rearrange("p (c e) -> p c e", e=8)))
                    v.tensor_copy(RCOL[:, :], PS[:, 6, 0:NB]).then_inc(rcol_ready, 1)
                    spm, spr, spb = (x.rearrange("p (c h) -> p c h", h=H) for x in (SPM, SPR, SPB))
                    step(v.tensor_tensor(spr, ABT[:, :, 0:4],
                                         ALD[:, 4:8].unsqueeze(1).broadcast_to([P, NB, H]), ADD))
                    step(v.scalar_tensor_tensor(out=SPM, in0=SPR, scalar=-1.0, in1=SPR, op0=MUL, op1=ALU.min))
                    step(v.tensor_scalar(SPR, SPR, 0.0, None, ALU.max))
                    v.tensor_copy(spb, ABT[:, :, 4:8]).then_inc(sp_in, 1)
                if u == 12:
                    dve.wait_ge(sp_done, 1)
                    gg = GG.rearrange("p (c h) -> p c h", h=H)
                    spr = SPR.rearrange("p (c h) -> p c h", h=H)
                    step(v.tensor_tensor(SPR, SPR, SPM, ADD))
                    step(v.scalar_tensor_tensor(out=gg, in0=spr, scalar=-1.0,
                                                in1=ALD[:, 0:4].unsqueeze(1).broadcast_to([P, NB, H]),
                                                op0=MUL, op1=MUL))
                    step(v.tensor_scalar(SPB, SPB, 1.0, None, ADD))
                    v.reciprocal(BETA, SPB).then_inc(gb_ready, 1)
                    v.tensor_tensor(T[:, :, :], UPPER.unsqueeze(1).broadcast_to([P, 16, P]), lastdim(GG), MUL) \
                        .then_inc(gu_ready, 1)
                    dve.wait_ge(r4_ready, 1)
                    v.tensor_tensor(KQ[:, :, 0, :], KQ[:, :, 0, :], R4[:, :, :], MUL).then_inc(kq_normed, 1)
                if u == 13:
                    dve.wait_ge(gc_filled, 1)
                    v.tensor_copy(GC, PS[:, 4, 0:16]).then_inc(gc_ready, 1)
                    dve.wait_ge(r4_ready, 2)
                    v.tensor_tensor(KQ[:, :, 1, :], KQ[:, :, 1, :], R4[:, :, :], MUL).then_inc(kq_normed, 1)
                if u == 14:
                    dve.wait_ge(eb_ready, 1)
                    step(v.scalar_tensor_tensor(out=BEN, in0=BETA, scalar=-1.0, in1=EGC, op0=MUL, op1=MUL))
                    dve.wait_ge(eb_ready, 2)
                    v.tensor_tensor(TT[:, :, :], MX16, lastdim(GC), SUB).then_inc(x1_ready, 1)
                    dve.wait_ge(x1_ready, 1)
                    v.tensor_scalar(T[:, :, :], TT[:, :, :], 0.0, None, ALU.min).then_inc(dmm_ready, 1)
                    v.tensor_scalar(M[:, :, :], TT[:, :, :], 0.0, None, ALU.max).then_inc(dmm_ready, 1)
                if u == 16:
                    dve.wait_ge(dt_ready, 1)
                    v.tensor_copy(KDC.unsqueeze(2), T[:, :, P - 1:P])
                    dve.wait_ge(qk_filled, 1)
                    v.tensor_tensor(QKT[:, :, :], MX16, T[:, :, :], MUL).then_inc(qkt_ready, 1)
                    dve.wait_ge(qkt_ready, 1)
                    dve.wait_ge(m_ready, 1)
                    step(v.tensor_tensor(T[:, :, :], M[:, :, :], PAIRM.unsqueeze(1).broadcast_to([P, 16, P]), MUL))
                    v.scalar_tensor_tensor(out=T[:, :, :], in0=T[:, :, :], scalar=-1.0,
                                           in1=IDENT[:, :].unsqueeze(1).broadcast_to([P, 16, P]),
                                           op0=MUL, op1=ADD).then_inc(t2_ready, 1)
                if 18 <= u <= 23:
                    level(u - 18)
                if u in RET_GAP:
                    ret_scores(RET_GAP.index(u))
                if u in (24, 26, 28, 30):
                    keys((u - 24) // 2)

                if not 12 <= u < 15:
                    tile_done(u)
                if u == 0:
                    dve.wait_ge(rstd_ready, 1)
                if u < 12:
                    conv_tile(u)
                elif u < 15:
                    pass
                elif u == 15:
                    dve.wait_ge(rcol_ready, 1)
                    for b in range(NB):
                        v.tensor_scalar(RV[:, :, b, :], PS[:, b, :].rearrange("p (h d) -> p h d", h=H),
                                        RCOL[:, b:b + 1], None, MUL).then_inc(bank_free, 1)
                    dve.wait_ge(lb_ready, 1)
                    dve.wait_ge(dexp, 2)
                    step(v.tensor_tensor(M[:, :, :], M[:, :, :], LB[:, :, :], MUL))
                    dve.wait_ge(g_filled, 1)
                    v.tensor_tensor(M[:, :, :], MX16, M[:, :, :], MUL).then_inc(m_ready, 1)
                elif u < 24:
                    rotate_tile(u)
                else:
                    v.tensor_tensor(GT[:, u - 24, :], PS[:, u % 4, :], RSTD[:, :], MUL).then_inc(bank_free, 1)
                if u == 1:
                    dve.wait_ge(c2_in, 96)
                    v.tensor_copy(ABH[:, :, :], ABR[:, :, :]).then_inc(ab_split, 1)
                    dve.wait_ge(ab_split, 1)
                    v.tensor_tensor(ABL[:, :, :], ABR[:, :, :], f32(ABH[:, :, :]), SUB).then_inc(ab_split, 1)
                    v.tensor_tensor(CS[:, 0, :], CS[:, 0, :], RSTD[:, :], MUL)
                    step(v.tensor_tensor(CS[:, 1, :], CS[:, 1, :], RSTD[:, :], MUL))
                if u == 30:
                    dve.wait_ge(rr_ready, 2)
                    for h in range(H):
                        o = RV[:, h, :, :].rearrange("p b i -> p (b i)")
                        step(v.tensor_tensor(o, o, RR[:, h, :], MUL))
                        if h == 0:
                            dve.wait_ge(gate_done, 1)
                        v.tensor_tensor(o, o, GT[:, h, :], MUL).then_inc(op_src, 1)
            for h in range(H):
                operand_lo(8 + h, RV[:, h, :, :].rearrange("p b i -> p (b i)"), XA[:, h, 1, :], XA[:, h, 0, :])
            dve.wait_ge(rr_ready, 3)
            for h in range(H + 1):
                if h < H:
                    o = KQ[:, h, 1, :]
                    step(v.scalar_tensor_tensor(out=o, in0=o, scalar=vec("gdn_norm_w"), in1=RR[:, h, :],
                                                op0=MUL, op1=MUL))
                    if h == 0:
                        dve.wait_ge(gate_done, 2)
                    v.tensor_tensor(o, o, GT[:, 4 + h, :], MUL).then_inc(op_src, 1)
                if h >= 1:
                    operand_lo(12 + h - 1, KQ[:, h - 1, 1, :], XA[:, 3 + h, 1, :], XA[:, 3 + h, 0, :])

            def after_residual(k):
                operand_lo(16 + k, RES[:, k, :], XB[:, k, 1, :], XB[:, k, 0, :], vec("mlp_norm_w", k))
                accumulate(1, k, SQ2[:, k % 2, :])

            for k in range(KT):
                tile_done(U2 + k)
                dve.wait_ge(x2_in, 16)
                v.tensor_tensor(RES[:, k, :], PS[:, (M2 + k) % 4, :], XT2[:, k, :], ADD) \
                    .then_inc(bank_free, 1)
                if k >= 1:
                    after_residual(k - 1)
            dve.wait_ge(bank_free, M2 + KT)
            after_residual(KT - 1)

            dve.wait_ge(half_done, 2 * U3)
            step(v.memset(PADF[:, :, 0:3], 0.0))
            dve.wait_ge(rstd_ready, 2)
            base_steps = steps[0]
            PER = 10
            with dve.Fori(0, 11) as i:
                late[0] = i * PER
                for j in range(4):
                    dve.wait_ge(half_done, i * 8 + 2 * (U3 + j + 1))
                    x = PADF[:, j, :]
                    d = CF[:, j, :]
                    t = i * 2 + (j % 2 + FT * (j // 2))
                    w = [MCW[:, q, bass.ds(t, 1)] for q in range(3)]
                    v.tensor_tensor(x[:, 3:3 + S], PS[:, j, :], RSTD[:, :], MUL).then_inc(bank_free, 1)
                    dve.wait_ge(bank_free, i * 4 + (M3 + j + 1))
                    step(v.tensor_scalar(d, x[:, 3:3 + S], w[2], None, MUL))
                    step(v.scalar_tensor_tensor(out=d, in0=x[:, 2:2 + S], scalar=w[1], in1=d,
                                                op0=MUL, op1=ADD))
                    ins = v.scalar_tensor_tensor(out=d, in0=x[:, 1:1 + S], scalar=w[0], in1=d,
                                                 op0=MUL, op1=ADD)
                    if j < 2:
                        ins.then_inc(ff_conv, 1)
                    else:
                        step(ins)
                        dve.wait_ge(ff_silu, i * 2 + (j - 1))
                        v.tensor_tensor(PRODF[:, j - 2, :], CF[:, j - 2, :], d, MUL).then_inc(ff_prod, 1)
                for j in range(2):
                    dve.wait_ge(ff_hi, i * 2 + (j + 1))
                    act_hi, act_lo = (ACTS[:, bass.ds(i * 2 + j, 1), q, :].rearrange("p a s -> p (a s)")
                                      for q in range(2))
                    v.tensor_tensor(act_lo, PRODF[:, j, :], f32(act_hi), SUB).then_inc(ff_lo, 1)
            assert steps[0] - base_steps == PER
            late[0] = None
            steps[0] = base_steps + 11 * PER

            for k in range(KT):
                tile_done(U4 + 6 * (k // 2) + 4 + k % 2)
                v.tensor_tensor(RES[:, k, :], PS[:, (M4 + k) % 4, :], RES[:, k, :], ADD).then_inc(bank_free, 1)
                if k >= 1:
                    accumulate(2, k - 1, SQ4B[:, (k - 1) % 2, :])
            accumulate(2, KT - 1, SQ4B[:, (KT - 1) % 2, :])
            dve.wait_ge(rstd_ready, 3)
            for k in range(KT + 1):
                if k < KT:
                    v.scalar_tensor_tensor(out=RES[:, k, :], in0=RES[:, k, :], scalar=vec("final_norm_w", k),
                                           in1=RSTD[:, :], op0=MUL, op1=MUL).then_inc(op_src, 1)
                if k >= 1:
                    dve.wait_ge(op_src, 16 + k)
                    operand_lo(24 + k - 1, RES[:, k - 1, :], XA[:, k - 1, 1, :], XA[:, k - 1, 0, :],
                               vec("pre0", k - 1))
                    if k - 1 >= POOL_SQUARES:
                        accumulate(3, k - 1, SQ3[:, (k - 1) % 2, :])

            step(v.memset(UPD[:, :, 0:16], 0.0))

            def scores(j):
                b, kv = j // 2, j % 2
                lo = P if b == 0 else 0
                sb = SB[:, j % 2, :, lo:256]
                dve.wait_ge(sc_filled, j + 1)
                step(v.scalar_tensor_tensor(out=sb, in0=PS[:, 4:6, :].rearrange("p a (t k) -> p (a t) k", t=2)
                                            [:, :, lo:256], scalar=HD2 ** -0.5,
                                            in1=ALI[:, 4 * kv:4 * kv + 4, lo:256], op0=MUL, op1=ADD))
                step(v.tensor_reduce(AS[:, 0, 0:4], sb, AX.X, ALU.max))
                sink = SINK[:, 4 * kv:4 * kv + 4]
                step(v.tensor_tensor(AS[:, 0, 0:4], AS[:, 0, 0:4], sink, ALU.max))
                step(v.tensor_tensor(AS[:, 3, 0:4], sink, AS[:, 0, 0:4], SUB))
                v.tensor_scalar(AS[:, 1, 0:4], AS[:, 0, 0:4], -1.0, None, MUL).then_inc(sc_ready, 1)
                dve.wait_ge(p_exp, 5 * (j + 1))
                step(v.tensor_tensor(AS[:, 4, 0:4], AS[:, 2, 0:4], AS[:, 3, 0:4], ADD))
                step(v.reciprocal(AS[:, 4, 0:4], AS[:, 4, 0:4]))
                v.tensor_tensor(sb, sb, AS[:, 4, 0:4].unsqueeze(2).broadcast_to([P, 4, 256 - lo]), MUL) \
                    .then_inc(p_ready, 1)

            def pool(g):
                src = UPD[:, 0, :]
                for i in range(g + 1):
                    dst = UPD[:, 1 + i % 2, :]
                    sh = 1 << i
                    step(v.tensor_tensor(dst[:, 16:], src[:, 16:], src[:, 16 - sh:16 + S - sh], ADD))
                    src = dst
                step(v.scalar_tensor_tensor(out=PL[:, g, :], in0=src[:, 16:], scalar=0.5 ** (g + 1),
                                            in1=UPD[:, 0, 16:], op0=MUL, op1=SUB))
                step(v.tensor_tensor(src[:, 16:32], src[:, 16:32], ITAB[:, g, :], MUL))
                v.tensor_tensor(PL[:, g, 0:16], src[:, 16:32], UPD[:, 0, 16:32], SUB).then_inc(pool_ready, 1)

            dve.wait_ge(ali_in, 64)
            for u in range(U5, U6):
                n = u - U5
                j = n - 6
                if 0 <= j < 8:
                    scores(j)
                tile_done(u)
                if n == 0:
                    dve.wait_ge(rstd_ready, 4)
                bank = PS[:, (M5 + n) % 4, :]
                dst = (QS[:, n, :] if n < 4 else KS[:, :] if n == 4 else SQ3[:, 0, :] if n == 5 else
                       GA[:, n - 6, :] if n < 10 else UPD[:, 0, 16:] if n < 14 else GB[:, n - 14, :])
                v.tensor_tensor(dst, bank, RSTD[:, :], MUL).then_inc(bank_free, 1)
                if 10 <= n < 14:
                    dve.wait_ge(bank_free, M5 + n + 1)
                    pool(n - 10)
                if n == 16:
                    dve.wait_ge(ov_taken, 8)
                    dve.wait_ge(gate_done, 3)
                    for t in range(4):
                        v.tensor_tensor(MIXF[:, t, :], MIXF[:, t, :], GA[:, t, :], MUL).then_inc(op_src, 1)
                    for t in range(4):
                        operand_lo(32 + t, MIXF[:, t, :], XB[:, t, 1, :], XB[:, t, 0, :])
            dve.wait_ge(py_taken, 4)
            for g in range(5):
                if g < 4:
                    dve.wait_ge(gate_done, 4 + g)
                    v.tensor_tensor(MIXF[:, 4 + g, :], PL[:, g, :], GB[:, g, :], MUL).then_inc(op_src, 1)
                if g >= 1:
                    operand_lo(36 + g - 1, MIXF[:, 3 + g, :], XB[:, 3 + g, 1, :], XB[:, 3 + g, 0, :])

            def post(st, name, f, yt):
                dve.wait_ge(rstd_ready, st + 1)
                first = steps[0]
                for k in range(KT + 2):
                    if k < KT:
                        v.scalar_tensor_tensor(out=yt[:, k % 2, :], in0=Y[:, k, :], scalar=vec(name, k),
                                               in1=RSTD[:, :], op0=MUL, op1=MUL).then_inc(dchain, 1)
                        steps[0] += 1
                    if 1 <= k <= KT:
                        dve.wait_ge(dchain, first + k)
                        v.tensor_tensor(RES[:, k - 1, :], RES[:, k - 1, :], yt[:, (k - 1) % 2, :], ADD) \
                            .then_inc(op_src, 1)
                    if k >= 1 and k < KT:
                        dve.wait_ge(op_src, 32 + k)
                    if k >= 2:
                        q = k - 2
                        dve.wait_ge(op_src, 32 + q + 1)
                        operand_lo(f + q, RES[:, q, :], XA[:, q, 1, :], XA[:, q, 0, :], vec("pre1", q))
                        if q >= POOL_SQUARES:
                            accumulate(5, q, SQ3[:, q % 2, :])

            for k in range(KT):
                tile_done(U6 + k)
                v.tensor_copy(Y[:, k, :], PS[:, (M6 + k) % 4, :]).then_inc(bank_free, 1)
                if k >= 1:
                    accumulate(4, k - 1, SQ3[:, (k - 1) % 2, :])
            accumulate(4, KT - 1, SQ3[:, (KT - 1) % 2, :])
            post(4, "post0", 40, YT)

            step(v.memset(GLU[:, :, 0:CK - 1], 0.0))
            tap_at = [0]

            todo = [(k, i) for k in range(KT) for i in range(CK - PE_TAPS[k] + 2)]
            last_of_chain = [0, 0]

            def taps(n, tiles):
                for _ in range(n):
                    if tap_at[0] == len(todo) or todo[tap_at[0]][0] >= tiles:
                        return
                    k, i = todo[tap_at[0]]
                    tap_at[0] += 1
                    own = CK - PE_TAPS[k]
                    chain = 1 if i == own else i % 2
                    d = (CV[:, k, :], CT[:, k % 2, :])[chain]
                    if i <= own + 1 and (i > 1 or k > 0):
                        dve.wait_ge(dchain, last_of_chain[chain] if i <= own else max(last_of_chain))
                    if i == own + 1:
                        v.tensor_tensor(CV[:, k, :], CV[:, k, :], CT[:, k % 2, :], ADD).then_inc(cv_ready, 1)
                        continue
                    if i == own:
                        dve.wait_ge(cv_filled, k + 1)
                        ins = v.tensor_tensor(d, d, PS[:, 4 + k % 3, :], ADD)
                    elif i == 0:
                        ins = v.tensor_scalar(d, GLU[:, k, i:i + S], DCW[:, i, k:k + 1], vec("dw_b", k), MUL, ADD)
                    elif i == 1:
                        ins = v.tensor_scalar(d, GLU[:, k, i:i + S], DCW[:, i, k:k + 1], None, MUL)
                    else:
                        ins = v.scalar_tensor_tensor(out=d, in0=GLU[:, k, i:i + S], scalar=DCW[:, i, k:k + 1],
                                                     in1=d, op0=MUL, op1=ADD)
                    steps[0] += 1
                    ins.then_inc(dchain, 1)
                    last_of_chain[chain] = steps[0]

            for k in range(KT):
                dve.wait_ge(scaled, 2 * k + 2)
                dve.wait_ge(sig_done, k + 1)
                v.tensor_tensor(GLU[:, k, CK - 1:], ABUF[:, 2 * k % 4, :], ABUF[:, (2 * k + 1) % 4, :], MUL) \
                    .then_inc(glu_ready, 1)
                dve.wait_ge(glu_ready, k + 1)
                taps(19, k + 1)
            taps(CK * KT, KT)
            dve.wait_ge(cv_ready, KT)
            dve.wait_ge(mean_ready, 1)
            v.tensor_tensor(CV[:, KT - 1, :], CV[:, KT - 1, :], MEAN, SUB).then_inc(centered_last, 1)
            dve.wait_ge(cm_filled, 2)
            v.tensor_scalar(OFF, PS[:, 7, :], 1.0 / D, None, MUL).then_inc(off_ready, 1)
            dve.wait_ge(off_ready, 1)
            step(v.tensor_tensor(ACC[:, :], OFF, OFF, MUL))
            dve.wait_ge(ln_added, KT)
            step(v.scalar_tensor_tensor(out=ACC[:, :], in0=PS[:, 6, :], scalar=1.0 / D, in1=ACC[:, :],
                                        op0=MUL, op1=SUB))
            v.tensor_scalar(ACC[:, :], ACC[:, :], 0.0, None, ALU.max).then_inc(var_ready, 1)
            dve.wait_ge(centered, KT - 1)
            for k in range(SHIFTED_BY_DVE):
                step(v.tensor_tensor(CV[:, k, :], CV[:, k, :], OFF, SUB))
            dve.wait_ge(rstd_ready, 7)
            dve.wait_ge(gate_done, 7 + KT - 1)
            for k in range(KT + 2):
                if k < KT:
                    if k >= SHIFTED_BY_DVE:
                        dve.wait_ge(shifted, k + 1 - SHIFTED_BY_DVE)
                    v.scalar_tensor_tensor(out=CV[:, k, :], in0=CV[:, k, :], scalar=vec("ln_g", k),
                                           in1=RSTD[:, :], op0=MUL, op1=MUL).then_inc(ln_in, 1)
                if 1 <= k <= KT:
                    if k == KT:
                        dve.wait_ge(gate_done, 7 + KT)
                    dve.wait_ge(ln_done, k)
                    v.tensor_tensor(CV[:, k - 1, :], CV[:, k - 1, :], GT3[:, k - 1, :], MUL) \
                        .then_inc(op_src, 1)
                if k >= 2:
                    operand_lo(48 + k - 2, CV[:, k - 2, :], XB[:, k - 2, 1, :], XB[:, k - 2, 0, :])

            dve.wait_ge(wpost_in, 16)
            def weighted(g, b):
                dve.wait_ge(ysq_done, 4 * g + b + 1)
                v.tensor_tensor(YTOK[:, b, g * 512:(g + 1) * 512], PS[:, (M8 + b) % 4, :],
                                WPOST[:, g * 512:(g + 1) * 512], MUL).then_inc(bank_free, 1)

            for b in range(NB):
                weighted(0, b)
            dve.wait_ge(rest_taken, KT)
            for b in range(NB + 1):
                if b < NB:
                    weighted(1, b)
                    v.tensor_tensor(AS[:, 1, b:b + 1], AS[:, 0, b:b + 1], AS[:, 0, 4 + b:5 + b], ADD) \
                        .then_inc(yss_ready, 1)
                if b >= 1:
                    c = b - 1
                    dve.wait_ge(ysd_ready, c + 1)
                    v.reciprocal(AS[:, 3, c:c + 1], AS[:, 2, c:c + 1]).then_inc(yinv_ready, 1)
                    dve.wait_ge(yinv_ready, c + 1)
                    dve.wait_ge(bank_free, M8 + 4 + c + 1)
                    y = YTOK[:, c, 512:D]
                    v.scalar_tensor_tensor(out=y, in0=y, scalar=AS[:, 3, c:c + 1], in1=REST[:, c, 512:D],
                                           op0=MUL, op1=ADD).then_inc(ot_ready, 1)
            y = YTOK[:, NB - 1, 0:512]
            v.scalar_tensor_tensor(out=y, in0=y, scalar=AS[:, 3, NB - 1:NB], in1=REST[:, NB - 1, 0:512],
                                   op0=MUL, op1=ADD).then_inc(ot_ready, 1)

        @block.tensor
        def _(pe):
            mm, tr = nc.tensor.matmul, nc.tensor.transpose

            def operand(f):
                pe.wait_ge(op_hi, f + 1)
                pe.wait_ge(op_lo, f + 1)

            def three(out, w_hi_, w_lo_, x_hi_, x_lo_, first, last):
                mm(out, w_hi_, x_hi_, start=first, stop=False)
                mm(out, w_hi_, x_lo_, start=False, stop=False)
                return mm(out, w_lo_, x_hi_, start=False, stop=last)

            def half_unit(n, out, X, k0, kn, first, last, fill=None, later=None):
                for s_ in (w_hi, w_lo):
                    pe.wait_ge(s_, n + 1 if later is None else later + (n + 1))
                for k in range(kn):
                    if fill is not None:
                        operand(8 * fill + k0 + k)
                    ins = three(out, WH[:, n % 4, k, :], WL[:, n % 4, k, :],
                                X[:, k0 + k, 0, :], X[:, k0 + k, 1, :],
                                first and k == 0, last and k == kn - 1)
                ins.then_inc(half_done, 1)

            def deltanet_ssq():
                pe.wait_ge(rsq_ready, 2)
                pe.wait_ge(tokk_ready, 4)
                pe.wait_ge(tokv_ready, 16)
                pe.wait_ge(o_ready, 4)
                for h in range(H):
                    ins = mm(PS[:, 4 + h, :], ONES[:, :], RR[:, h, :], start=True, stop=True)
                ins.then_inc(rssq_filled, 1)

            def unit(u, m, X, fill=None, later=None, mlater=None, midway=None):
                for q in QUADS:
                    if 0 <= u - q < 4:
                        if u == q:
                            for j in range(4):
                                if m >= 4:
                                    pe.wait_ge(bank_free, m + j - 3)
                                half_unit(2 * q + j, PS[:, (m + j) % 4, :], X, 0, 4, True, False,
                                          fill if j == 0 else None)
                                if j == 1 and u == U2:
                                    deltanet_ssq()
                            if midway is not None:
                                stat(midway)
                        half_unit(2 * q + 4 + u - q, PS[:, m % 4, :], X, 4, 4, False, True,
                                  fill if u == q else None)
                        return
                if m >= 4:
                    pe.wait_ge(bank_free, m - 3 if mlater is None else mlater + (m - 3))
                out = PS[:, m % 4, :]
                half_unit(2 * u, out, X, 0, 4, True, False, fill, later)
                half_unit(2 * u + 1, out, X, 4, 4, False, True, fill, later)

            def wide_half(n, X, fill=None, last_of=None):
                q0 = max(q for q in WIDE if q <= n // 2)
                k = n - 2 * q0
                m = q0 if q0 < U2 else M8 + q0 - U8
                for s_ in (w_hi, w_lo):
                    pe.wait_ge(s_, n + 1)
                if fill is not None:
                    operand(8 * fill + k)
                w, wl = (r[:, n % 4, :, :].rearrange("p t c -> p (t c)") for r in (WH, WL))
                for b in range(NB):
                    if k == 0:
                        pe.wait_ge(bank_free, m + b - 3)
                    xh, xl = (X[:, k, q, b * P:(b + 1) * P] for q in range(2))
                    ins = three(PS[:, (m + b) % 4, :], xh, xl, w, wl, k == 0, k == KT - 1)
                    if k == KT - 1 and b < NB - 1 and last_of is not None:
                        ins.then_inc(last_of, 1)
                ins.then_inc(half_done, 1)

            def stat(st):
                pe.wait_ge(acc_done, 8 * (st + 1))
                mm(PS[:, 7, :], ONES[:, :], ACC[:, :], start=True, stop=True).then_inc(stat_filled, 1)

            def rstd_columns(n):
                pe.wait_ge(rstd_ready, n)
                for b in range(NB):
                    ins = mm(PS[:, 6, b:b + 1], RSTD[0:1, b * P:(b + 1) * P], ONES[0:1, 0:1],
                             start=True, stop=True)
                return ins

            def x_tile(k):
                if k >= 4:
                    pe.wait_ge(op_src, k - 3)
                for b in range(NB):
                    ins = tr(PS[:, 4 + k % 4, b * P:(b + 1) * P], XTOK[:, b, k * P:(k + 1) * P], IDENT[:, :])
                ins.then_inc(xt_filled, 1)

            pe.wait_ge(x_in, 16 * NB)
            pe.wait_ge(ident_in, 16)
            for k in range(4):
                x_tile(k)
            pe.wait_ge(c_in, 16 * 17)
            pe.wait_ge(ones_ready, 5)
            c = 0
            for slot, n, bank in ((0, NVEC, 0), (1, 48, 0), (2, 66, 0), (5, 66, 0), (3, 124, 1), (4, 124, 1)):
                if slot == 3:
                    c = 0
                ins = tr(PS[:, bank, c:c + n], ROWS[0:n, slot, :], IDENT[0:n, 0:n])
                c += n
            ins.then_inc(par_filled, 1)
            for k in range(4, KT):
                x_tile(k)
            pe.wait_ge(par_ready, 4)

            def ret_head(h):
                if h >= 1:
                    pe.wait_ge(ro_ready, h)
                if h == 0 or h == 2:
                    pe.wait_ge(rot_ready, 3 if h == 0 else 7)
                if h == 1 or h == 3:
                    pe.wait_ge(rot_ready, 4 if h == 1 else 8)

                def score(jb):
                    if 4 * h + jb >= 2:
                        pe.wait_ge(rs_ready, 4 * h + jb - 1)
                    mm(PS[:, 4 + jb % 2, 0:S - jb * P], RK[:, h % 2, jb * P:(jb + 1) * P],
                       RQ[:, h % 2, jb * P:], start=True, stop=True).then_inc(rs_filled, 1)

                def value(jb):
                    pe.wait_ge(rs_ready, 4 * h + jb + 1)
                    ins = mm(PS[:, 6, jb * P:], RV[:, h, jb, :], RS[:, jb % 2, 0:S - jb * P],
                             start=(jb == 0), stop=(jb == NB - 1))
                    if jb == NB - 1:
                        ins.then_inc(ro_filled, 1)

                score(0)
                for jb in range(1, NB):
                    score(jb)
                    value(jb - 1)
                value(NB - 1)

            def level(l):
                s = 2 << l
                def half(ap, two):
                    return ap.rearrange("p (b two s) -> p b two s", two=2, s=s)[:, :, two, :]
                for c in range(NB):
                    if l == 0 and c == 0:
                        pe.wait_ge(t2_ready, 1)
                        pe.wait_ge(tt_ready, 1)
                    if l > 0:
                        pe.wait_ge(upd_done, 4 * (l - 1) + c + 1)
                    for h in range(H):
                        a_ = 4 * c + h
                        ins = mm(PS[:, 4 + c, h * 64:(h + 1) * 64], M[:, a_, :], half(TT[:, a_, :], 1),
                                 start=True, stop=True)
                    ins.then_inc(xp_filled, 1)
                for c in range(NB):
                    pe.wait_ge(xs_ready, 4 * l + c + 1)
                    pe.wait_ge(xz_ready, 4 * l + c + 1)
                    for h in range(H):
                        a_ = 4 * c + h
                        ins = mm(PS[:, 4 + c, 256 + h * 64:256 + (h + 1) * 64], T[:, a_, :],
                                 half(XZ[:, c, h, :], 1), start=True, stop=True)
                        if l < 5:
                            ins = mm(PS[:, 4 + c, h * 64:(h + 1) * 64], XZ[:, c, h, :],
                                     half(T[:, a_, :], 0), start=True, stop=True)
                    ins.then_inc(txp_filled, 1)

            def by_token(c):
                if c >= 1:
                    pe.wait_ge(tokk_ready, c)
                    pe.wait_ge(tokv_ready, 4 * c)
                for j, bank in ((0, 4), (1, 5)):
                    for h in range(H):
                        src = KQ[:, h, 0, c * P:(c + 1) * P] if j == 0 else V[:, h, c * P:(c + 1) * P]
                        ins = tr(PS[:, bank, h * P:(h + 1) * P], src, IDENT[:, :])
                    ins.then_inc(tok_filled, 1)

            def weights_t(c):
                pe.wait_ge(tokk_ready, c + 1)
                pe.wait_ge(o_ready, c)
                for h in range(H):
                    ins = mm(PS[:, 6, h * P:(h + 1) * P], KB[:, h, :], TT[:, 4 * c + h, :], start=True, stop=True)
                ins.then_inc(nw_filled, 1)

            def new_values(c):
                pe.wait_ge(tokv_ready, 4 * (c + 1))
                if c >= 1:
                    pe.wait_ge(nw_ready, c)
                    pe.wait_ge(s_ready, c)
                for h in range(H):
                    o = PS[:, 7, h * P:(h + 1) * P]
                    ins = mm(o, TT[:, 4 * c + h, :], VB[:, h, :], start=True, stop=(c == 0))
                    if c >= 1:
                        ins = mm(o, NW[:, h, :], ST8[:, h, :], start=False, stop=True)
                ins.then_inc(u_filled, 1)

            def out_and_state(c):
                pe.wait_ge(u_ready, c + 1)
                if c >= 1:
                    pe.wait_ge(qd_ready, c)
                    pe.wait_ge(nw_ready, c)
                else:
                    pe.wait_ge(ro_ready, 4)
                for h in range(H):
                    o = PS[:, 6, h * P:(h + 1) * P]
                    ins = mm(o, UU[:, h, :], QKT[:, 4 * c + h, :], start=True, stop=(c == 0))
                    if c >= 1:
                        ins = mm(o, ST8[:, h, :], QD[:, h, :], start=False, stop=True)
                ins.then_inc(so_filled, 1)
                if c < NB - 1:
                    if c == 0:
                        pe.wait_ge(tokk_ready, 1)
                    for h in range(H):
                        ins = mm(PS[:, 7, h * P:(h + 1) * P], KD[:, h, :], UU[:, h, :], start=True, stop=True)
                    ins.then_inc(so_filled, 1)

            def ret_ssq(r):
                pe.wait_ge(rsq_ready, 1)
                pe.wait_ge(tokk_ready, r + 1)
                pe.wait_ge(tokv_ready, 4 * (r + 1))
                for h in range(2):
                    ins = mm(PS[:, 4 + h, :], ONES[:, :], RR[:, 2 * r + h, :], start=True, stop=True)
                ins.then_inc(rssq_filled, 1)

            for u in range(U1, U2):
                if 12 <= u < 16:
                    wide_half(2 * u, XA)
                    wide_half(2 * u + 1, XA)
                else:
                    unit(u, u, XA, fill=0 if u == 0 else None, midway=0)
                if u == 3:
                    pe.wait_ge(ab_split, 2)
                    pe.wait_ge(rstd_ready, 1)
                    for k in range(KT):
                        ins = three(PS[0:8, 7, :], ABH[:, k, :], ABL[:, k, :], XA[:, k, 0, :], XA[:, k, 1, :],
                                    k == 0, k == KT - 1)
                    ins.then_inc(ab_filled, 1)
                if u == 4:
                    pe.wait_ge(ab_rows, 1)
                    rstd_columns(1)
                    for c in range(NB):
                        ins = tr(PS[:, 7, 8 * c:8 * c + 8], AB[:, c * P:(c + 1) * P], IDENT[0:8, 0:8])
                    ins.then_inc(abt_filled, 1)
                if u == 12 or u == 13:
                    pe.wait_ge(sqk, u - 11)
                    pe.wait_ge(sp_in, 1)
                    pe.wait_ge(rcol_ready, 1)
                    if u == 13:
                        pe.wait_ge(r4_ready, 1)
                        pe.wait_ge(gu_ready, 1)
                        mm(PS[:, 4, 0:16], UPPER, GG, start=True, stop=True).then_inc(gc_filled, 1)
                    for h in (1, 2, 3, 0):
                        if h == 0 and u == 13:
                            pe.wait_ge(gc_ready, 1)
                        ins = mm(PS[:, 4 + h, :], ONES[:, :], SQ4[:, h, :], start=True, stop=True)
                    ins.then_inc(ssq_filled, 1)
                if u == 14:
                    pe.wait_ge(r4_ready, 2)
                    for c in range(NB):
                        ins = mm(PS[:, 4 + c, :], ONES[:, :],
                                 T[:, 4 * c:4 * c + 4, :].rearrange("p h i -> p (h i)"), start=True, stop=True)
                    ins.then_inc(gcb_filled, 1)
                if u == 15 or u == 16:
                    if u == 15:
                        pe.wait_ge(x1_ready, 1)
                        pe.wait_ge(kq_normed, 2)
                    else:
                        pe.wait_ge(m_ready, 1)
                    for c in range(NB):
                        for h in range(H):
                            ins = mm(PS[:, 4 + c, h * P:(h + 1) * P], KQ[:, h, 0, c * P:(c + 1) * P],
                                     KQ[:, h, u - 15, c * P:(c + 1) * P], start=True, stop=True)
                    ins.then_inc(g_filled if u == 15 else qk_filled, 1)
                if u == 17:
                    pe.wait_ge(qkt_ready, 1)
                    pe.wait_ge(t2_ready, 1)
                    for a_ in range(16):
                        ins = tr(PS[:, 4 + a_ // 4, (a_ % 4) * P:(a_ % 4 + 1) * P], T[:, a_, :], IDENT[:, :])
                    ins.then_inc(tt_filled, 1)
                if 18 <= u <= 23:
                    heads = sum(g < u for g in RET_GAP)
                    if heads:
                        pe.wait_ge(ro_ready, heads)
                        pe.wait_ge(rs_ready, 4 * heads)
                    level(u - 18)
                if u in RET_GAP:
                    pe.wait_ge(upd_done, 4 * min(u - 17, 6))
                    ret_head(RET_GAP.index(u))
                if u == 24:
                    pe.wait_ge(rs_ready, 16)
                    by_token(0)
                if u == 25:
                    ret_ssq(0)
                if u == 26:
                    new_values(0)
                    pe.wait_ge(rr_ready, 1)
                    by_token(1)
                    out_and_state(0)
                if u == 27:
                    weights_t(1)
                    ret_ssq(1)
                if u == 28:
                    new_values(1)
                    pe.wait_ge(rr_ready, 2)
                    by_token(2)
                    out_and_state(1)
                if u == 29:
                    weights_t(2)
                if u == 30:
                    new_values(2)
                    by_token(3)
                    out_and_state(2)
                if u == 31:
                    weights_t(3)
                    new_values(3)
                    out_and_state(3)
            for k in range(KT):
                unit(U2 + k, M2 + k, XA, fill=1 if k == 0 else None)
            pe.wait_ge(rr_ready, 3)
            stat(1)
            operand(23)
            with pe.Fori(0, 11) as i:
                for j in range(4):
                    unit(U3 + j, M3 + j, XB, later=i * 8, mlater=i * 4)
            pe.wait_ge(ff_hi, 16)
            pe.wait_ge(ff_lo, 16)
            with pe.Fori(0, 2) as i:
                for j in range(12):
                    g, t, o = j // 2 % 3, j % 2, j // 6
                    m = M4 + 2 * o + t
                    if g == 0:
                        pe.wait_ge(bank_free, i * 4 + (m - 3))
                    if g == 2:
                        pe.wait_ge(ff_hi, FT)
                        pe.wait_ge(ff_lo, FT)
                    kn = 4 if g < 2 else 3
                    for hf in range(2):
                        half_unit(2 * (U4 + j) + hf, PS[:, m % 4, :], ACTS, 8 * g + kn * hf, kn,
                                  g == 0 and hf == 0, g == 2 and hf == 1, later=i * 24)
            stat(2)

            def probs_t(j):
                pe.wait_ge(p_ready, j + 1)
                if j >= 1:
                    pe.wait_ge(ov_taken, j)
                else:
                    pe.wait_ge(vt_ready, 1)
                for t in range(4):
                    for w in range(1 if j < 2 else 0, 2):
                        ins = tr(PS[:, 6 + t // 2, (2 * (t % 2) + w) * P:(2 * (t % 2) + w + 1) * P],
                                 SB[:, j % 2, t, w * P:(w + 1) * P], IDENT[:, :])
                ins.then_inc(pt_filled, 1)

            def scores(j):
                b, kv = j // 2, j % 2
                r = slice(kv * HD2, (kv + 1) * HD2)
                if j >= 1:
                    pe.wait_ge(sc_ready, j)
                for t in range(4):
                    lo = 0 if b else P
                    ins = mm(PS[:, 4 + t // 2, (t % 2) * 256 + lo:(t % 2 + 1) * 256],
                             QS[r, t, b * P:(b + 1) * P], KS[r, (b - 1) * P + lo:(b + 1) * P],
                             start=True, stop=True)
                ins.then_inc(sc_filled, 1)

            def values(j):
                b, kv = j // 2, j % 2
                r = slice(kv * HD2, (kv + 1) * HD2)
                pe.wait_ge(pt_ready, j + 1)
                for w in range(0 if b else 1, 2):
                    ins = mm(PS[r, 6, :], VS[:, b - 1 + w, r], PTS[:, :, w, :],
                             start=(w == (0 if b else 1)), stop=(w == 1))
                ins.then_inc(ov_filled, 1)

            for u in range(U5, U6):
                n = u - U5
                unit(u, M5 + n, XA, fill=3 if n == 0 else None, midway=3)
                j = n - 6
                if j == 0:
                    pe.wait_ge(bank_free, M5 + 6)
                    pe.wait_ge(rstd_ready, 4)
                    for b in range(NB):
                        ins = tr(PS[:, 7, b * P:(b + 1) * P], SQ3[:, 0, b * P:(b + 1) * P], IDENT[:, :])
                    ins.then_inc(vt_filled, 1)
                if 1 <= j <= 8:
                    probs_t(j - 1)
                if 0 <= j < 8:
                    scores(j)
                if 1 <= j <= 8:
                    values(j - 1)
                if j == 9:
                    pe.wait_ge(ali_in, 64)
                    pe.wait_ge(pool_ready, 4)
                    pe.wait_ge(ov_taken, 8)
                    for g in range(4):
                        ins = mm(PS[:, 4 + g, :], PW[:, g, :], PL[:, g, :], start=True, stop=True)
                    ins.then_inc(py_filled, 1)
            for k in range(KT):
                unit(U6 + k, M6 + k, XB, fill=4 if k == 0 else None)
            pe.wait_ge(py_taken, 4)
            stat(4)

            def conv_part(k):
                pe.wait_ge(glu_ready, k + 1)
                pe.wait_ge(diag_ready, k + 1)
                if k >= 3:
                    pe.wait_ge(cv_ready, k - 2)
                else:
                    pe.wait_ge(py_taken, 4)
                n = PE_TAPS[k]
                for t in range(n):
                    i = CK - n + t
                    ins = mm(PS[:, 4 + k % 3, :], DG[:, sum(PE_TAPS[:k]) + t, :], GLU[:, k, i:i + S],
                             start=(t == 0), stop=(t == n - 1))
                ins.then_inc(cv_filled, 1)

            def channel_sum(last):
                if last:
                    pe.wait_ge(centered_last, 1)
                    pe.wait_ge(mean_ready, 1)
                else:
                    pe.wait_ge(cv_added, KT - 2)
                    pe.wait_ge(rstd_ready, 6)
                mm(PS[:, 7, :], ONES[:, :], CV[:, KT - 1, :] if last else ACC[:, :], start=True, stop=True) \
                    .then_inc(cm_filled, 1)

            conv_after = {2 * k + 4: k for k in range(KT)}
            for n in range(24):
                unit(U7 + n, M7 + n, XA, fill=5 if n == 0 else None, midway=5)
                if n in conv_after:
                    conv_part(conv_after[n])
                if n == 22:
                    channel_sum(False)
            for k in range(KT):
                if k == KT - 2:
                    channel_sum(True)
                if k == 0:
                    pe.wait_ge(cv_ready, 6)
                pe.wait_ge(sq_ready, 48 + k + 1)
                mm(PS[:, 6, :], ONES[:, :], ABUF[:, 1 + k % 2, :], start=(k == 0), stop=(k == KT - 1)) \
                    .then_inc(ln_added, 1)

            def x_by_token(k):
                if k >= 4:
                    pe.wait_ge(rest_taken, k - 3)
                for b in range(NB):
                    ins = tr(PS[:, REST_BANK[k % 4], b * P:(b + 1) * P], RES[:, k, b * P:(b + 1) * P],
                             IDENT[:, :])
                ins.then_inc(rest_filled, 1)

            pe.wait_ge(off_ready, 1)
            for k in range(3):
                x_by_token(k)
            pe.wait_ge(var_ready, 1)
            x_by_token(3)
            for g in range(2):
                for k in range(KT):
                    wide_half(2 * (U8 + 4 * g) + k, XB, fill=6 if g == 0 else None, last_of=y_done)
                if g == 0:
                    for k in range(4, KT):
                        x_by_token(k)


def constants():
    f = np.float32
    i, j = np.arange(P)[:, None], np.arange(P)[None, :]
    masks = [(i <= j).astype(f), (j < i).astype(f), ((i % 2 == 1) & (j == i - 1)).astype(f)]
    for level in range(6):
        s = 2 << level
        second = np.array([c for c in range(P) if c // s % 2 == 1])[None, :]
        masks.append(((i // s % 2 == 0) & (i // (2 * s) == second // (2 * s))).astype(f))
    angle = f(1.0) / f(10000.0) ** np.linspace(0.0, 1.0, P // 2, dtype=f)
    phase = (np.arange(S, dtype=f)[None, :] * np.repeat(angle, 2)[:, None]).astype(f).astype(np.float64)
    sign = np.where(np.arange(P) % 2 == 0, -1.0, 1.0)[:, None]
    log_gamma = np.log(1.0 - 2.0 ** (-5.0 - np.arange(H)))
    off = np.arange(S)[None, :] - np.arange(P)[:, None]
    decay = np.where(off >= 0, np.exp(np.maximum(off, 0)[None] * log_gamma[:, None, None]), 0.0) * P ** -0.5
    dist = np.arange(P)[:, None] + P - np.arange(256)[None, :]
    slopes = 2.0 ** (-np.arange(1, QH + 1, dtype=np.float64))
    ok = (dist >= 0) & (dist < P)
    alibi = np.where(ok[:, None, :], -slopes[None, :, None] * dist[:, None, :], NEG)
    cnt = np.minimum(np.arange(16)[None, :] + 1, np.array([2, 4, 8, 16])[:, None])
    return {
        "ident": np.eye(P, dtype=f),
        "masks": np.concatenate(masks, 1),
        "cos_sin": np.stack([np.cos(phase), np.sin(phase) * sign], 1).astype(f),
        "ret_decay": decay.transpose(1, 0, 2).astype(f),
        "alibi": alibi.astype(f),
        "inv_cnt": np.broadcast_to((1.0 / cnt).astype(f)[None], (P, 4, 16)).copy(),
    }


_INS = ["x", "attn_norm_w", "w_in", "gdn_conv_w", "gdn_a_log", "gdn_dt_bias", "gdn_norm_w", "w_out",
        "mlp_norm_w", "w_up", "mlp_conv_w", "w_down", "final_norm_w", "pre_norm_2", "post_norm_2",
        "a_w_in_2", "a_sinks_2", "b_pool_w_2", "b_pool_scale_2", "ab_w_out_2", "c_w_in_2", "c_dw_w_2",
        "c_dw_b_2", "c_ln_g_2", "c_ln_b_2", "c_w_out_2"]


def kernel(**inputs):
    import concourse.bacc as bacc
    from concourse.bass_utils import run_bass_kernel_spmd as run

    nc = bacc.Bacc("TRN2", target_bir_lowering=False, num_devices=1)
    arrays, a, const = {}, {}, {}
    for name in _INS:
        x = np.ascontiguousarray(inputs[name])
        arrays["in_" + name] = x
        a[name] = nc.dram_tensor("in_" + name, x.shape, F32, kind="ExternalInput").ap()
    for name, x in constants().items():
        arrays["const_" + name] = x
        const[name] = nc.dram_tensor("const_" + name, x.shape, F32, kind="ExternalInput").ap()
    out = nc.dram_tensor("result", (1, S, D), F32, kind="ExternalOutput").ap()
    x_t = nc.dram_tensor("x_by_feature", (P, KT, S), F32, kind="Internal").ap()
    build(nc, a, const, out, x_t)
    r = run(nc, [arrays], core_ids=[0])
    return r.results[0]["result"]
```
